# Optimizing a Trainium2 kernel written in Bass

```python
import math
import jax, jax.numpy as jnp
from jax import lax
import numpy as np

D_MODEL = 1024
BATCH = 1
SEQ = 256
DEPTH = 2

GRID_W = 64
CTX_LEN = 256
HEAD_DIM = 64
N_Q_HEADS = 8
N_KV_HEADS = 2
Q_PER_KV = N_Q_HEADS // N_KV_HEADS
D_ATTN = N_Q_HEADS * HEAD_DIM
D_KV = N_KV_HEADS * HEAD_DIM
WINDOW = 128
BLOCK = 128
ROPE_THETA = 10000.0
D_SSM = D_MODEL // 2
SSM_GROUP = 16
N_SSM_GROUPS = D_SSM // SSM_GROUP
SSM_STATE = 64
D_IN = D_ATTN + 2 * D_KV + D_SSM + 2 * D_MODEL
D_FF = 2816
N_EXPERTS = 8
TOP_K = 2
D_FF_EXPERT = 3584
N_DENSE = (DEPTH + 1) // 2
N_MOE = DEPTH // 2
RMS_EPS = 1e-6
NEG_INF = -1e30

kernel_name = 'hybrid_dit_window_gqa_s5_moe'

def _rmsnorm(x, g):
    xf = x.astype(jnp.float32)
    y = xf * lax.rsqrt(jnp.mean(xf * xf, axis=-1, keepdims=True) + RMS_EPS)
    return (y * g.astype(jnp.float32)).astype(x.dtype)

def _modulate(h, shift, scale):
    return h * (1.0 + scale) + shift

def _split_proj(p):
    sizes = (D_ATTN, D_KV, D_KV, D_SSM, D_MODEL, D_MODEL)
    idx = [sum(sizes[:i + 1]) for i in range(len(sizes) - 1)]
    return jnp.split(p, idx, axis=-1)

def _heads(t, n):
    return t.reshape(t.shape[:2] + (n, HEAD_DIM))

def _axial_rope(L):
    rows = L // GRID_W
    row = jnp.broadcast_to(jnp.arange(rows, dtype=jnp.float32)[:, None], (rows, GRID_W)).reshape(L)
    col = jnp.broadcast_to(jnp.arange(GRID_W, dtype=jnp.float32)[None, :], (rows, GRID_W)).reshape(L)
    n_freq = HEAD_DIM // 4
    inv_freq = ROPE_THETA ** (-jnp.arange(n_freq, dtype=jnp.float32) / n_freq)
    ang = jnp.concatenate([row[:, None] * inv_freq, col[:, None] * inv_freq], axis=-1)
    return jnp.cos(ang), jnp.sin(ang)

def _rope(x, cos, sin):
    half = HEAD_DIM // 2
    x1, x2 = x[..., :half], x[..., half:]
    cs = cos[:, None, :].astype(x.dtype)
    sn = sin[:, None, :].astype(x.dtype)
    return jnp.concatenate([x1 * cs - x2 * sn, x2 * cs + x1 * sn], axis=-1)

def _latent_window_attention(q, k, v, kc, vc, sink):
    Bn, L = q.shape[:2]
    C = kc.shape[1]
    nb = L // BLOCK
    scale = HEAD_DIM ** -0.5
    qb = q.reshape(Bn, nb, BLOCK, N_KV_HEADS, Q_PER_KV, HEAD_DIM)
    pad = ((0, 0), (BLOCK, BLOCK), (0, 0), (0, 0))
    kp = jnp.pad(k, pad).reshape(Bn, nb + 2, BLOCK, N_KV_HEADS, HEAD_DIM)
    vp = jnp.pad(v, pad).reshape(Bn, nb + 2, BLOCK, N_KV_HEADS, HEAD_DIM)
    kb = jnp.concatenate([kp[:, :-2], kp[:, 1:-1], kp[:, 2:]], axis=2)
    vb = jnp.concatenate([vp[:, :-2], vp[:, 1:-1], vp[:, 2:]], axis=2)
    qpos = jnp.arange(nb)[:, None, None] * BLOCK + jnp.arange(BLOCK)[None, :, None]
    kpos = jnp.arange(nb)[:, None, None] * BLOCK - BLOCK + jnp.arange(3 * BLOCK)[None, None, :]
    valid = (jnp.abs(qpos - kpos) <= WINDOW) & (kpos >= 0) & (kpos < L)
    s_loc = jnp.einsum('bnqhgd,bnkhd->bnhgqk', qb, kb, preferred_element_type=jnp.float32) * scale
    s_loc = jnp.where(valid[:, None, None], s_loc, NEG_INF)
    s_ctx = jnp.einsum('bnqhgd,bchd->bnhgqc', qb, kc, preferred_element_type=jnp.float32) * scale
    s_sink = jnp.broadcast_to(sink.astype(jnp.float32).reshape(N_KV_HEADS, Q_PER_KV, 1, 1),
                              s_loc.shape[:-1] + (1,))
    p = jax.nn.softmax(jnp.concatenate([s_loc, s_ctx, s_sink], axis=-1), axis=-1)
    p_loc = p[..., :3 * BLOCK].astype(v.dtype)
    p_ctx = p[..., 3 * BLOCK:3 * BLOCK + C].astype(v.dtype)
    o = (jnp.einsum('bnhgqk,bnkhd->bnqhgd', p_loc, vb)
         + jnp.einsum('bnhgqc,bchd->bnqhgd', p_ctx, vc))
    return o.reshape(Bn, L, D_ATTN)

def _context_attention(q, k, v, sink):
    Bn, C = q.shape[:2]
    scale = HEAD_DIM ** -0.5
    qg = q.reshape(Bn, C, N_KV_HEADS, Q_PER_KV, HEAD_DIM)
    s = jnp.einsum('bqhgd,bkhd->bhgqk', qg, k, preferred_element_type=jnp.float32) * scale
    s_sink = jnp.broadcast_to(sink.astype(jnp.float32).reshape(N_KV_HEADS, Q_PER_KV, 1, 1),
                              s.shape[:-1] + (1,))
    p = jax.nn.softmax(jnp.concatenate([s, s_sink], axis=-1), axis=-1)[..., :C]
    o = jnp.einsum('bhgqk,bkhd->bqhgd', p.astype(v.dtype), v)
    return o.reshape(Bn, C, D_ATTN)

def _zoh(a_re, a_im, log_dt, b_re, b_im):
    a = lax.complex(a_re.astype(jnp.float32), a_im.astype(jnp.float32))
    dt = jnp.exp(log_dt.astype(jnp.float32))[..., None]
    a_bar = jnp.exp(a * dt)
    b = lax.complex(b_re.astype(jnp.float32), b_im.astype(jnp.float32))
    b_bar = ((a_bar - 1.0) / a)[..., None] * b
    return a_bar, b_bar

def _scan_combine(e1, e2):
    return (e1[0] * e2[0], e2[0] * e1[1] + e2[1])

def _diag_scan(u, a_bar, b_bar, s0, reverse):
    L = u.shape[1]
    bu = jnp.einsum('blgh,gph->blgp', u.astype(jnp.complex64), b_bar)
    a = jnp.broadcast_to(a_bar, (1, L) + a_bar.shape)
    a_cum, s = lax.associative_scan(_scan_combine, (a, bu), reverse=reverse, axis=1)
    if s0 is not None:
        s = s + a_cum * s0[:, None]
    return s

def _readout(s, c_mat):
    return jnp.einsum('blgp,ghp->blgh', s, c_mat).real

def _bidir_ssm(u_lat, u_ctx, a_bar, b_bar, c_mat, d_skip, need_ctx_out):
    Bn, L, _ = u_lat.shape
    C = u_ctx.shape[1]
    ul = u_lat.astype(jnp.float32).reshape(Bn, L, N_SSM_GROUPS, SSM_GROUP)
    uc = u_ctx.astype(jnp.float32).reshape(Bn, C, N_SSM_GROUPS, SSM_GROUP)
    d = d_skip.astype(jnp.float32)
    sc_f = _diag_scan(uc, a_bar[0], b_bar[0], None, False)
    sc_b = _diag_scan(uc, a_bar[1], b_bar[1], None, True)
    sl_f = _diag_scan(ul, a_bar[0], b_bar[0], sc_f[:, -1], False)
    sl_b = _diag_scan(ul, a_bar[1], b_bar[1], sc_b[:, 0], True)
    y_lat = ((_readout(sl_f, c_mat[0]) + _readout(sl_b, c_mat[1])).reshape(Bn, L, D_SSM)
             + d * u_lat.astype(jnp.float32))
    y_ctx = None
    if need_ctx_out:
        y_ctx = ((_readout(sc_f, c_mat[0]) + _readout(sc_b, c_mat[1])).reshape(Bn, C, D_SSM)
                 + d * u_ctx.astype(jnp.float32))
        y_ctx = y_ctx.astype(u_ctx.dtype)
    return y_lat.astype(u_lat.dtype), y_ctx

def _glu(y, w, b):
    g = jax.nn.gelu(y)
    return g * jax.nn.sigmoid(g @ w + b)

def _merge(o_attn, y_ssm, g_attn, g_ssm, w_pa, w_pb, w_o):
    m = jax.nn.sigmoid(g_attn) * (o_attn @ w_pa) + jax.nn.sigmoid(g_ssm) * (y_ssm @ w_pb)
    return m @ w_o

def _swiglu(h, wg, wu, wd):
    return (jax.nn.silu(h @ wg) * (h @ wu)) @ wd

def _moe_swiglu(h, w_router, b_router, wg, wu, wd):
    shp = h.shape
    hf = h.reshape(-1, shp[-1])
    logits = (hf @ w_router).astype(jnp.float32) + b_router.astype(jnp.float32)
    top_v, top_i = lax.top_k(logits, TOP_K)
    top_w = jax.nn.softmax(top_v, axis=-1)
    gates = jnp.sum(jax.nn.one_hot(top_i, N_EXPERTS, dtype=jnp.float32) * top_w[..., None], axis=-2)
    gates = gates.astype(h.dtype)
    y = jnp.zeros_like(hf)
    for e in range(N_EXPERTS):
        y = y + gates[:, e:e + 1] * _swiglu(hf, wg[e], wu[e], wd[e])
    return y.reshape(shp)

def setup_inputs(seed: int = 0) -> dict:
    key = jax.random.key(seed)
    ks = iter(jax.random.split(key, 40))
    f32 = jnp.float32

    def nrm(shape, s):
        return s * jax.random.normal(next(ks), shape, f32)

    D = D_MODEL
    G, P, H = N_SSM_GROUPS, SSM_STATE, SSM_GROUP
    n_idx = jnp.arange(P, dtype=f32)
    return {
        'x': nrm((BATCH, SEQ, D), 1.0),
        'c': nrm((BATCH, D), 1.0),
        'ctx': nrm((BATCH, CTX_LEN, D), 1.0),
        'c_ctx': nrm((D,), 1.0),
        'w_mod': nrm((DEPTH, D, 6 * D), 0.5 * D ** -0.5),
        'b_mod': nrm((DEPTH, 6 * D), 0.02),
        'norm_g': 1.0 + nrm((DEPTH, 4, D), 0.02),
        'w_in': nrm((DEPTH, D, D_IN), D ** -0.5),
        'attn_sink': nrm((DEPTH, N_Q_HEADS), 0.5),
        'ssm_a_re': -0.5 + nrm((DEPTH, 2, G, P), 0.01),
        'ssm_a_im': math.pi * n_idx + nrm((DEPTH, 2, G, P), 0.01),
        'ssm_log_dt': jax.random.uniform(next(ks), (DEPTH, 2, G), f32, math.log(1e-3), math.log(1e-1)),
        'ssm_b_re': nrm((DEPTH, 2, G, P, H), (2.0 * H) ** -0.5),
        'ssm_b_im': nrm((DEPTH, 2, G, P, H), (2.0 * H) ** -0.5),
        'ssm_c_re': nrm((DEPTH, 2, G, H, P), (2.0 * P) ** -0.5),
        'ssm_c_im': nrm((DEPTH, 2, G, H, P), (2.0 * P) ** -0.5),
        'ssm_d': nrm((DEPTH, D_SSM), 1.0),
        'w_glu': nrm((DEPTH, D_SSM, D_SSM), D_SSM ** -0.5),
        'b_glu': nrm((DEPTH, D_SSM), 0.02),
        'w_branch_attn': nrm((DEPTH, D_ATTN, D), D_ATTN ** -0.5),
        'w_branch_ssm': nrm((DEPTH, D_SSM, D), D_SSM ** -0.5),
        'w_out': nrm((DEPTH, D, D), D ** -0.5),
        'w_ffn_gate': nrm((N_DENSE, D, D_FF), D ** -0.5),
        'w_ffn_up': nrm((N_DENSE, D, D_FF), D ** -0.5),
        'w_ffn_down': nrm((N_DENSE, D_FF, D), D_FF ** -0.5),
        'w_router': nrm((N_MOE, D, N_EXPERTS), D ** -0.5),
        'b_router': nrm((N_MOE, N_EXPERTS), 0.01),
        'w_exp_gate': nrm((N_MOE, N_EXPERTS, D, D_FF_EXPERT), D ** -0.5),
        'w_exp_up': nrm((N_MOE, N_EXPERTS, D, D_FF_EXPERT), D ** -0.5),
        'w_exp_down': nrm((N_MOE, N_EXPERTS, D_FF_EXPERT, D), D_FF_EXPERT ** -0.5),
    }

def reference(x, c, ctx, c_ctx, w_mod, b_mod, norm_g, w_in, attn_sink, ssm_a_re, ssm_a_im,
              ssm_log_dt, ssm_b_re, ssm_b_im, ssm_c_re, ssm_c_im, ssm_d, w_glu, b_glu,
              w_branch_attn, w_branch_ssm, w_out, w_ffn_gate, w_ffn_up, w_ffn_down,
              w_router, b_router, w_exp_gate, w_exp_up, w_exp_down):
    L = x.shape[1]
    cos, sin = _axial_rope(L)
    xc = ctx
    cond_lat = jax.nn.silu(c)
    cond_ctx = jax.nn.silu(c_ctx)
    for l in range(DEPTH):
        last = l == DEPTH - 1
        mod_l = jnp.split((cond_lat @ w_mod[l] + b_mod[l])[:, None, :], 6, axis=-1)
        mod_c = jnp.split(cond_ctx @ w_mod[l] + b_mod[l], 6, axis=-1)

        h_l = _modulate(_rmsnorm(x, norm_g[l, 0]), mod_l[0], mod_l[1])
        h_c = _modulate(_rmsnorm(xc, norm_g[l, 0]), mod_c[0], mod_c[1])
        q_l, k_l, v_l, u_l, ga_l, gb_l = _split_proj(h_l @ w_in[l])
        q_c, k_c, v_c, u_c, ga_c, gb_c = _split_proj(h_c @ w_in[l])
        k_c = _heads(k_c, N_KV_HEADS)
        v_c = _heads(v_c, N_KV_HEADS)

        q_lh = _rope(_heads(q_l, N_Q_HEADS), cos, sin)
        k_lh = _rope(_heads(k_l, N_KV_HEADS), cos, sin)
        o_l = _latent_window_attention(q_lh, k_lh, _heads(v_l, N_KV_HEADS), k_c, v_c, attn_sink[l])

        a_bar, b_bar = _zoh(ssm_a_re[l], ssm_a_im[l], ssm_log_dt[l], ssm_b_re[l], ssm_b_im[l])
        c_mat = lax.complex(ssm_c_re[l].astype(jnp.float32), ssm_c_im[l].astype(jnp.float32))
        y_l, y_c = _bidir_ssm(u_l, u_c, a_bar, b_bar, c_mat, ssm_d[l], not last)
        s_l = _glu(y_l, w_glu[l], b_glu[l])

        m_l = _merge(o_l, s_l, ga_l, gb_l, w_branch_attn[l], w_branch_ssm[l], w_out[l])
        x = x + mod_l[2] * _rmsnorm(m_l, norm_g[l, 1])
        if not last:
            o_c = _context_attention(_heads(q_c, N_Q_HEADS), k_c, v_c, attn_sink[l])
            s_c = _glu(y_c, w_glu[l], b_glu[l])
            m_c = _merge(o_c, s_c, ga_c, gb_c, w_branch_attn[l], w_branch_ssm[l], w_out[l])
            xc = xc + mod_c[2] * _rmsnorm(m_c, norm_g[l, 1])

        j = l // 2
        if l % 2 == 0:
            ffn = lambda h: _swiglu(h, w_ffn_gate[j], w_ffn_up[j], w_ffn_down[j])
        else:
            ffn = lambda h: _moe_swiglu(h, w_router[j], b_router[j], w_exp_gate[j], w_exp_up[j], w_exp_down[j])
        h_l = _modulate(_rmsnorm(x, norm_g[l, 2]), mod_l[3], mod_l[4])
        x = x + mod_l[5] * _rmsnorm(ffn(h_l), norm_g[l, 3])
        if not last:
            h_c = _modulate(_rmsnorm(xc, norm_g[l, 2]), mod_c[3], mod_c[4])
            xc = xc + mod_c[5] * _rmsnorm(ffn(h_c), norm_g[l, 3])
    return x


_drawn_inputs = setup_inputs


def setup_inputs(seed=0):
    import zlib

    import numpy as np

    out = dict(_drawn_inputs(seed))
    spreads = {}
    factors = {'attn_sink': 8.0, 'ssm_a_re': 6.668, 'b_glu': 8.0, 'b_router': 4.232}
    for name, (base, spread) in spreads.items():
        noise = np.random.default_rng([zlib.crc32(name.encode()), seed]).standard_normal(out[name].shape)
        drawn = base * np.exp(spread * noise) if base else spread * noise
        out[name] = __import__('jax').numpy.asarray(drawn.astype(out[name].dtype))
    for name, factor in factors.items():
        out[name] = (out[name] * factor).astype(out[name].dtype)
    return out
```

```python
from contextlib import ExitStack

import numpy as np

import concourse.bass as bass
from concourse import mybir

F = mybir.dt.float32
R = mybir.dt.float32r
I32 = mybir.dt.int32
ACT = mybir.ActivationFunctionType
ALU = mybir.AluOpType
AX = mybir.AxisListType.X

P = 128
L = 2
D = 1024
KT = D // P
N = 512
TT = N // P
CTX = 256
HD = 64
NH = 8
NKV = 2
QPK = NH // NKV
DS = 512
G = 32
H = 16
T = 8
C = N // T
DFF = 2816
DFE = 3584
NE = 8
FC = 256
EPS = 1e-6
NEG = -(2.0 ** 103)
MM3 = ((0, 0), (0, 1), (1, 0))
TWO_PI = 6.283185307179586
PI_PARTS = (6.28125, 0.0019353071693331003, 1.0253131677018246e-11)
ROUND = 12582912.0
LN2 = (0.693359375, -2.1219444005469057e-4)
INV_LN2 = 1.4426950408889634


def toks(l):
    return [0, 1, 2, 3] if l == 0 else [2, 3]


class Banks:

    def __init__(self, full, free, w_used):
        self.full, self.free, self.w_used = full, free, w_used
        self.uses, self.fulls = [0] * 8, [0] * 8
        self.filled, self.emptied = {}, {}

    def begin(self, pe, key, bank, i=None, per=0):
        if self.uses[bank] > 0:
            pe.wait_ge(self.free[bank], self.uses[bank] if i is None else self.uses[bank] + i * per)
        self.uses[bank] += 1
        self.emptied[key] = (self.free[bank], self.uses[bank], per, bank)

    def end(self, ins, key):
        *_, per, bank = self.emptied[key]
        self.fulls[bank] += 1
        ins.then_inc(self.full[bank], 1)
        self.filled[key] = (self.full[bank], self.fulls[bank], per)

    def end_unit(self, ins, key, unit, per=0):
        ins.then_inc(self.w_used, 1)
        self.filled[key] = (self.w_used, unit + 1, per)

    def wait(self, eng, key, i=None):
        sem, count, per = self.filled[key]
        eng.wait_ge(sem, count if i is None else count + i * per)

    def release(self, ins, key):
        ins.then_inc(self.emptied[key][0], 1)

    def released(self, eng, key, i=None, turns_back=0):
        sem, count, per, _ = self.emptied[key]
        count -= turns_back * per
        eng.wait_ge(sem, count if i is None else count + i * per)


class Chain:

    def __init__(self, eng, sem):
        self.eng, self.sem, self.n, self.off = eng, sem, 0, None

    def __call__(self, ins):
        ins.then_inc(self.sem, 1)
        self.n += 1
        self.eng.wait_ge(self.sem, self.n if self.off is None else self.n + self.off)


def weight_units(a):
    units = []

    def rows(key, w, k0, nk, c0, nc):
        units.append((key, w[k0 * P:(k0 + nk) * P, c0:c0 + nc].rearrange("(a p) n -> p a n", p=P), nk, nc))

    for l in range(L):
        for nb in range(12):
            for hf in range(2):
                rows(("mod", l, nb, hf), a["w_mod"][l], 4 * hf, 4, nb * 512, 512)
    for l in range(L):
        w = a["w_in"][l]
        rows(("kv", l), w, 0, 8, 512, 256)
        for hf in range(2):
            rows(("u", l, hf), w, 4 * hf, 4, 768, 512)
        for hf in range(2):
            rows(("q", l, hf), w, 4 * hf, 4, 0, 512)
        for i in range(8):
            rows(("gate", l, i), w, 0, 8, 1280 + 256 * i, 256)
        rows(("glu", l), a["w_glu"][l], 0, 4, 0, 512)
        for nb in range(2):
            rows(("pa", l, nb), a["w_branch_attn"][l], 0, 4, nb * 512, 512)
            rows(("pb", l, nb), a["w_branch_ssm"][l], 0, 4, nb * 512, 512)
        for nb in range(2):
            for hf in range(2):
                rows(("out", l, nb, hf), a["w_out"][l], 4 * hf, 4, nb * 512, 512)
        if l == 0:
            for kind, c in ffn_order(DFF // FC):
                w = a[{"g": "w_ffn_gate", "u": "w_ffn_up", "d": "w_ffn_down"}[kind]][0]
                if kind == "d":
                    rows(("d", c), w, 2 * c, 2, 0, D)
                else:
                    rows((kind, c), w, 0, 8, c * FC, FC)
    return units


def ffn_order(chunks):
    out = []
    for c in range(chunks + 1):
        if c < chunks:
            out += [("g", c), ("u", c)]
        if c > 0:
            out.append(("d", c - 1))
    return out


def build_program(nc, a, consts, out):
    units = weight_units(a)
    U = {u[0]: n for n, u in enumerate(units)}
    NU = len(units)
    ECH = DFE // FC
    EUNITS = 3 * ECH
    eorder = ffn_order(ECH)
    EU = {kc: n for n, kc in enumerate(eorder)}

    ctx = ExitStack()
    with ctx:
        cursor = [16512]

        def region(size):
            at = cursor[0]
            cursor[0] += size
            return at

        def sb(name, shape, dt, at):
            return nc.alloc_sbuf_tensor_at(name, shape, dt, offset=at)

        r_raw, r_split = region(3 * 8192), region(3 * 16384)
        r_x, r_ht, r_ot = region(16384), region(32768), region(16384)
        r_gb, r_qk, r_qs = region(8192), region(12288), region(10240)
        r_uy, r_small, r_ring = region(8192), region(15104), region(10240)
        r_const = region(0)

        raw = sb("raw", [P, 3, 2048], F, r_raw)
        split = sb("split", [P, 3, 2, 2048], R, r_split)
        X = sb("X", [P, TT, D], F, r_x)
        S = sb("ssm_state", [P, 2, G, C], F, r_x)
        STR = sb("ssm_out", [P, 2, 4, N], R, r_x)
        HT = sb("HT", [P, 2, KT, N], R, r_ht)
        BM = sb("b_mod_rows", [2, L, 6 * D], F, r_ht)
        Hm = sb("read_mats", [P, 2, 2, 4, P], F, r_ht)
        KB = sb("lag_blocks", [H, 2, 4, 15, H], F, r_ht + 8192)
        MI = sb("chunk_mats", [P, 2, 4, P], F, r_ht + 8192 + 7680)
        GTR = sb("glu_in", [P, 2, 4, N], R, r_ht)
        OT = sb("attn_out", [P, 2, 4, N], R, r_ot)
        YA = sb("YA", [P, TT, D], F, r_ot)
        GB = sb("gate_rows", [P, 2, D], F, r_gb)
        UC = sb("chunked_u", [P, G, C], F, r_gb)
        qT = sb("qT", [P, TT, 4, P], F, r_qk)
        kT = sb("kT", [P, N], F, r_qk + 8192)
        V = sb("V", [P, TT, P], F, r_qk + 10240)
        QS = sb("q_tok", [P, TT, 512], F, r_qs)
        KS = sb("k_tok", [P, TT, P], F, r_qs + 8192)
        PR = sb("probs", [P, 2, 512], F, r_qs)
        PT = sb("probsT", [P, 2, 4, P], F, r_qs + 4096)
        YK = sb("y_tok", [P, TT, 512], F, r_qs)
        NG = sb("norm_rows", [2, L, 2, D], F, r_qk)
        SGA = sb("sig_a", [P, 2, 512], F, r_qk)
        SGB = sb("sig_b", [P, 2, 512], F, r_qk + 4096)
        HC = sb("hidden", [P, 2, 2, 2, 512], R, r_qk)
        UU = sb("u_chunks", [P, T, 256], F, r_uy)
        YY = sb("y_chunks", [P, T, 256], F, r_uy)
        GF = sb("gelu", [P, 4, 512], F, r_uy)
        MT1 = sb("merge_a", [P, 4, 512], F, r_uy)
        MS = sb("mod_stage", [2, 2, 512], F, r_qk + 16384)
        UP = sb("u_grouped", [P, H, T, H], F, r_ot)
        HTF = sb("HT_f32", [P, KT, CTX], F, r_uy)
        SIL = sb("silu", [P, 2, 512], F, r_uy)
        HF = sb("hidden_f", [P, 2, 512], F, r_uy + 4096)
        PW = sb("powers", [P, 2, T + 1, G], F, r_small)
        BB = sb("b_bar", [P, 2, G, H], F, r_small + 2304)
        CC = sb("c_mat", [P, 2, G, H], F, r_small + 2304 + 4096)
        A8 = sb("a_chunk", [P, 2, 2, G], F, r_small + 2304 + 8192)
        PG = sb("powers_in_out", [P, 2, 2, T, G], F, r_small + 11008)
        BT = sb("b_bar_tmp", [P, 2, 512], F, r_small + 11008)
        GP = sb("in_mats_pre", [P, 2, 4, P], F, r_qs + 4096)
        GT = sb("in_mats_t", [P, 2, 4, P], F, r_qs)
        DR = sb("ssm_skip", [H, G, H], F, r_qs + 8192)
        ZS = sb("zoh", [P, 16, G], F, r_ring + 8192)
        TM = sb("tmp", [P, 512], F, r_ring + 8192)
        CW = sb("cond_cols", [P, 2, KT, P], R, r_ring)
        STG = sb("stage", [P, 2, 512], F, r_ring)
        JUNK = sb("junk", [P, 2, D], F, r_ring)
        TN = sb("norm_tmp", [P, 2, 512], F, r_ring + 4096)
        SGT = sb("glu_sig", [P, 2, 512], F, r_ring)
        SF = sb("ssm_out_f", [P, 2, 512], F, r_ring + 4096)
        CI = sb("c_rows", [P, 2, 4, 2, 64], F, r_uy)
        BI = sb("b_rows", [P, 2, G, H], F, r_uy + 4096)

        names = iter(range(10 ** 6))
        cur = [r_const]

        def small(name, shape, dt=F):
            size = 4 * int(np.prod(shape[1:]))
            t = sb(name, shape, dt, cur[0])
            cur[0] += (size + 31) // 32 * 32
            return t

        CT = small("consts", [P, 768 + 128])
        EYE = CT[:, 0:128]
        MASK = [CT[:, 128:384], CT[:, 384:640]]
        COS = CT[:, 640:704].rearrange("p (t d) -> p t d", t=2)
        SIN = CT[:, 704:768].rearrange("p (t d) -> p t d", t=2)
        IOTA8 = CT[:, 768:776]
        CR = small("col_rows", [100, P])
        CV = small("cond_rows", [16, P])
        CF = small("cond_f", [P, 16])
        COLS = small("cols", [P, 100])
        AF = small("norm_gain", [P, 2, 2, KT])
        SS = small("sumsq", [P, TT])
        RS = small("rstd", [P, TT])
        SK = small("sink", [P, NH])
        ST = small("softmax_stats", [P, 2, 8])
        DTR = small("ssm_dt", [P, G])
        ARI = small("ssm_a_rows", [G, 2, P])
        ZI = small("zoh_int", [P, G], I32)
        RT = small("recur_tmp", [P, 2, 2, G])
        WR = small("router", [P, KT, NE])
        LG = small("logits", [P, 2, NE])
        TV = small("top_v", [P, 2, 8])
        TI = small("top_i", [P, 2, 8], mybir.dt.uint32)
        TF = small("top_f", [P, 2, 8])
        GA = small("gates", [P, 2, NE])
        GC = small("gate_now", [P, 2])
        RW = small("gate_tmp", [P, 2, 8])
        BR = small("router_bias", [P, NE])
        LT = small("sink_exp", [P, 2, 8])
        assert cur[0] <= 229344, cur[0]

        banks_t = [ctx.enter_context(nc.psum_tensor(f"bank{i}", [P, 512], F)) for i in range(8)]

        modrow = nc.dram_tensor("mod_rows", [L, 2, 6 * D], F).ap()
        uscr = nc.dram_tensor("u_scratch", [L, N, DS], F).ap()
        yscr = nc.dram_tensor("y_scratch", [L, N, DS], F).ap()
        gscr = nc.dram_tensor("gate_scratch", [L, 16, P, N], F).ap()
        xscr = nc.dram_tensor("x_scratch", [2 * L - 1, N, D], F).ap()

        def sem(name):
            return ctx.enter_context(nc.semaphore(name))

        full = [sem(f"bank_full{i}") for i in range(8)]
        free = [sem(f"bank_free{i}") for i in range(8)]
        
        w_landed = [sem(f"w_landed{i}") for i in range(3)]
        w_round, w_split, w_used = sem("w_rounded"), sem("w_split"), sem("w_used")
        banks = Banks(full, free, w_used)
        dve_step, act_step, pool_step = sem("dve_step"), sem("act_step"), sem("pool_step")
        ld_const, ld_cond, ld_bm = sem("ld_const"), sem("ld_cond"), sem("ld_bm")
        cond_zero, cond_hi, cond_ready = sem("cond_zero"), sem("cond_hi"), sem("cond_ready")
        mod_row, mod_stored = sem("mod_row"), [sem(f"mod_stored{i}") for i in range(2)]
        ld_cols, ld_x, ld_gb, cols_ready = sem("ld_cols"), sem("ld_x"), sem("ld_gb"), sem("cols_ready")
        sq_done, ms_ready, rt_done = sem("sq_done"), sem("ms_ready"), sem("rt_done")
        xn_ready, ht_hi, ht_ready = sem("xn_ready"), sem("ht_hi"), sem("ht_ready")
        q_tok, k_tok, v_ready = sem("q_tok"), sem("k_tok"), sem("v_ready")
        u_stored, ld_u, u_grouped = [sem(f"u_stored{i}") for i in range(2)], sem("ld_u"), sem("u_grouped")
        g_stored = [sem(f"gate_stored{i}") for i in range(2)]
        ld_g = [sem(f"ld_gates{i}") for i in range(2)]
        row_max, sink_done, p_norm = sem("row_max"), sem("sink_done"), sem("probs_norm")
        o_hi = sem("o_hi")
        ld_ssm, ld_skip, ang_ready, sin_done = sem("ld_ssm"), sem("ld_skip"), sem("ang_ready"), sem("sin_done")
        prep_done, gp_ready, v_fwd = sem("prep_done"), sem("in_pre"), sem("v_fwd")
        rec_done = sem("recurrence")
        h_ready, kb_copied, mi_loaded = sem("read_mats"), sem("kb_copied"), [sem(f"mi_loaded{i}") for i in range(2)]
        y_stored, ld_y, g_hi, g_ready = sem("y_stored"), sem("ld_y"), sem("g_hi"), sem("g_ready")
        s_f, s_hi, s_ready = sem("s_f"), sem("s_hi"), sem("s_ready")
        m_f, m_hi, m_ready = sem("m_f"), sem("m_hi"), sem("m_ready")
        y_zero, x_new, x_stored = sem("y_zero"), sem("x_new"), sem("x_stored")
        hc_hi, hc_ready = sem("hidden_hi"), sem("hidden_ready")
        ld_wr, top_diff, top_exp, out_stored = sem("ld_router"), sem("top_diff"), sem("top_exp"), sem("out_stored")
        LD_SSM = 14 * 16
        xn_ready_at = {(0, 0): 4, (0, 1): 8, (1, 0): 12, (1, 1): 14}
        ht_ready_at = {(0, 0): 8, (0, 1): 16, (1, 0): 24, (1, 1): 32}
        att_items = lambda l: [(t, h) for t in toks(l) for h in range(NH)]
        att_base = [0, 4 * NH]
        norm_no = {(0, 0): 0, (0, "r0"): 1, (0, 1): 2, (0, "r1"): 3, (1, 0): 4, (1, "r0"): 5, (1, 1): 6, (1, "r1"): 7}
        x_new_at = {(0, 0): 4, (0, 1): 8, (1, 0): 10, (1, 1): 12}
        x_stores_before = {(0, 1): 1, (1, 0): 2, (1, 1): 3}
        ld_x_at = {(0, 0): 32, (0, 1): 64, (0, 2): 80, (1, 0): 80, (1, 1): 96, (1, 2): 112}
        ld_sink, ya_done = sem("ld_sink"), sem("ya_done")
        pool_n = [0]
        ffn_hc0 = [0, 2 * (DFF // FC)]

        block = ctx.enter_context(nc.Block())

        def unit_view(slot, part, nk, ncol):
            return split[:, slot, part, :].rearrange("p (a n) -> p a n", a=nk)

        @block.tensor
        def _(pe):
            def unit(key):
                n = U[key]
                pe.wait_ge(w_split, n + 1)
                nk = units[n][2]
                return [unit_view(n % 3, q, nk, units[n][3]) for q in range(2)]

            def mm3(outp, lhs, rhs, start, stop):
                for j, (x, w) in enumerate(MM3):
                    ins = nc.tensor.matmul(outp, lhs(x, w), rhs(x, w), start=start and j == 0, stop=stop and j == 2)
                return ins

            def bank(i):
                return banks_t[i]

            pe.wait_ge(ld_const, 16)
            pe.wait_ge(ld_cond, 32)
            banks.begin(pe, "cond", 6)
            banks.end(nc.tensor.transpose(bank(6)[:, 0:16], CV[:, :], EYE[0:16, 0:16]), "cond")
            pe.wait_ge(cond_ready, 1)
            for l in range(L):
                for nb in range(12):
                    key = ("mod", l, nb)
                    for hf in range(2):
                        w = unit(("mod", l, nb, hf))
                        if hf == 0:
                            banks.begin(pe, key, nb % 4)
                        for k in range(4):
                            ins = mm3(bank(nb % 4)[:, :], lambda x, q: CW[:, x, 4 * hf + k, :],
                                      lambda x, q: w[q][:, k, :], hf == 0 and k == 0, hf == 1 and k == 3)
                        if hf == 1:
                            banks.end_unit(ins, key, U[("mod", l, nb, hf)])
                        else:
                            ins.then_inc(w_used, 1)

            def columns(l):
                pe.wait_ge(ld_cols, 96 * (l + 1))
                banks.begin(pe, ("cols", l), 7)
                banks.end(nc.tensor.transpose(bank(7)[:, 0:100], CR[:, :], EYE[0:100, 0:100]), ("cols", l))

            def norm(l, n, tiles):
                pe.wait_ge(xn_ready, xn_ready_at[(l, n)])
                for k in range(KT):
                    key = ("norm", l, n, k)
                    b = 6 + k % 2
                    banks.begin(pe, key, b)
                    for t in tiles:
                        ins = nc.tensor.transpose(bank(b)[:, t * P:(t + 1) * P], X[:, t, k * P:(k + 1) * P], EYE)
                    banks.end(ins, key)

            def tok_major(name, l, tiles, keys, width, src):
                n = len(keys)
                for i, ukey in enumerate(keys):
                    w = unit(ukey)
                    nk = units[U[ukey]][2]
                    for t in tiles:
                        key = (name, l, t)
                        if i == 0:
                            banks.begin(pe, key, t)
                        for k in range(nk):
                            kk = i * nk + k
                            ins = mm3(bank(t)[:, 0:width], lambda x, q: src[:, x, kk, t * P:(t + 1) * P],
                                      lambda x, q: w[q][:, k, :], kk == 0, i == n - 1 and k == nk - 1)
                        if i == n - 1 and t == tiles[-1]:
                            banks.end_unit(ins, key, U[ukey])
                        elif i == n - 1:
                            banks.end(ins, key)
                        elif t == tiles[-1]:
                            ins.then_inc(w_used, 1)

            def inproj(l):
                pe.wait_ge(ht_ready, ht_ready_at[(l, 0)])
                tok_major("kv", l, range(4), [("kv", l)], 256, HT)
                tok_major("u", l, range(4), [("u", l, 0), ("u", l, 1)], 512, HT)
                tok_major("q", l, toks(l), [("q", l, 0), ("q", l, 1)], 512, HT)
                for t in range(2):
                    banks.released(pe, ("kv", l, t))
                pe.wait_ge(k_tok, 2 * (l + 1))
                banks.begin(pe, ("kT", l), 7)
                for t in range(4):
                    ins = nc.tensor.transpose(bank(7)[:, t * P:(t + 1) * P], KS[:, t, :], EYE)
                banks.end(ins, ("kT", l))
                for t in toks(l):
                    if t < 2:
                        banks.released(pe, ("q", l, t))
                    else:
                        pe.wait_ge(q_tok, 2 * l + t - 1)
                    b = 6 + t % 2
                    banks.begin(pe, ("qT", l, t), b)
                    for j in range(4):
                        ins = nc.tensor.transpose(bank(b)[:, j * P:(j + 1) * P], QS[:, t, j * P:(j + 1) * P], EYE)
                    banks.end(ins, ("qT", l, t))

            def gates(l):
                c0 = 0 if l == 0 else CTX
                for i in range(8):
                    w = unit(("gate", l, i))
                    for f in range(2):
                        key = ("gate", l, i, f)
                        banks.begin(pe, key, 4 + f)
                        for k in range(KT):
                            ins = mm3(bank(4 + f)[:, 0:N - c0], lambda x, q: w[q][:, k, f * P:(f + 1) * P],
                                      lambda x, q: HT[:, x, k, c0:N], k == 0, k == KT - 1)
                        if f == 0:
                            banks.end(ins, key)
                        else:
                            banks.end_unit(ins, key, U[("gate", l, i)])

            def attention(l):
                banks.released(pe, ("kT", l))
                items = att_items(l)

                def scores(i):
                    t, h = items[i]
                    g, j = h // QPK, h % QPK
                    key, b = ("sc", l, i), 4 + i % 2
                    if h == 0:
                        banks.released(pe, ("qT", l, t))
                    banks.begin(pe, key, b)
                    lat = t >= 2
                    w = N if lat else CTX
                    if lat:
                        nc.tensor.matmul(bank(b)[:, CTX:N], EYE, MASK[t - 2], start=True, stop=False,
                                         skip_group_check=True)
                        nc.tensor.matmul(bank(b)[:, CTX:N], qT[g * HD:(g + 1) * HD, t, j, :],
                                         kT[g * HD:(g + 1) * HD, CTX:N], start=False, stop=True, skip_group_check=True)
                        ins = nc.tensor.matmul(bank(b)[:, 0:CTX], qT[g * HD:(g + 1) * HD, t, j, :],
                                               kT[g * HD:(g + 1) * HD, 0:CTX], start=False, stop=True,
                                               skip_group_check=True)
                    else:
                        ins = nc.tensor.matmul(bank(b)[:, 0:w], qT[g * HD:(g + 1) * HD, t, j, :],
                                               kT[g * HD:(g + 1) * HD, 0:w], start=True, stop=True)
                    banks.end(ins, key)

                def turn(i):
                    t, h = items[i]
                    key, b = ("pt", l, i), 6 + i % 2
                    pe.wait_ge(p_norm, att_base[l] + i + 1)
                    banks.begin(pe, key, b)
                    for kb in range(4 if t >= 2 else 2):
                        ins = nc.tensor.transpose(bank(b)[:, kb * P:(kb + 1) * P], PR[:, i % 2, kb * P:(kb + 1) * P], EYE)
                    banks.end(ins, key)

                def pv(i):
                    t, h = items[i]
                    g = h // QPK
                    key, b = ("o", l, t), t % 2
                    banks.released(pe, ("pt", l, i))
                    if h == 0:
                        banks.begin(pe, key, b)
                    nkb = 4 if t >= 2 else 2
                    r = (h % 2) * HD
                    for kb in range(nkb):
                        ins = nc.tensor.matmul(bank(b)[r:r + HD, (h // 2) * P:(h // 2 + 1) * P],
                                               V[:, kb, g * HD:(g + 1) * HD], PT[:, i % 2, kb, :],
                                               start=kb == 0, stop=kb == nkb - 1)
                    if h == NH - 1:
                        banks.end(ins, key)

                n = len(items)
                for i in range(n + 3):
                    if i < n:
                        scores(i)
                    if 2 <= i < n + 2:
                        turn(i - 2)
                    if i >= 3:
                        pv(i - 3)

            def ssm_prep(l):
                pe.wait_ge(ld_ssm, LD_SSM * (l + 1))
                for r in range(2):
                    banks.begin(pe, ("arow", l, r), 6 + r)
                    banks.end(nc.tensor.transpose(bank(6 + r)[:, 0:G], ARI[:, r, :], EYE[0:G, 0:G]), ("arow", l, r))
                for r in range(2):
                    banks.begin(pe, ("crow", l, r), 4 + r)
                    for b in range(4):
                        ins = nc.tensor.transpose(bank(4 + r)[:, b * P:(b + 1) * P],
                                                  CI[:, r, b, :, :].rearrange("p a b -> p (a b)"), EYE)
                    banks.end(ins, ("crow", l, r))

            def ssm_in(l):
                pe.wait_ge(u_grouped, 2 * (l + 1))
                for q in range(4):
                    b = 6 + q % 2
                    s = q // 2
                    banks.begin(pe, ("uc", l, q), b)
                    for g in range(8):
                        gl = (8 * q + g) % 16
                        ins = nc.tensor.transpose(bank(b)[:, g * C:(g + 1) * C],
                                                  UP[s * C:(s + 1) * C, gl, :, :].rearrange("p t h -> p (t h)"),
                                                  EYE[s * C:(s + 1) * C, s * C:(s + 1) * C])
                    banks.end(ins, ("uc", l, q))
                for q in range(4):
                    banks.released(pe, ("uc", l, q))
                for q in range(8):
                    pe.wait_ge(gp_ready, 8 * l + q + 1)
                    for r in range(2):
                        banks.begin(pe, ("gt", l, q, r), 4 + r)
                        for g in range(4):
                            ins = nc.tensor.transpose(bank(4 + r)[:, g * P:(g + 1) * P], GP[:, r, g, :], EYE)
                        banks.end(ins, ("gt", l, q, r))
                    for r in range(2):
                        banks.released(pe, ("gt", l, q, r))
                    b = q % 2
                    banks.begin(pe, ("v", l, q), b)
                    for r in range(2):
                        for g in range(4):
                            ins = nc.tensor.matmul(bank(b)[:, (r * 4 + g) * C:(r * 4 + g + 1) * C], GT[:, r, g, :],
                                                   UC[:, 4 * q + g, :], start=True, stop=True)
                    banks.end(ins, ("v", l, q))

            def ssm_out(l):
                c0 = 0 if l == 0 else C // 2
                for q in range(9):
                    if q < 8:
                        pe.wait_ge(h_ready, 8 * l + q + 1)
                        x = q % 2
                        for side in range(2):
                            banks.begin(pe, ("kb", l, q, side), 2 + side)
                            h = slice(64 * side, 64 * side + 64)
                            lags = slice(0, 112) if side == 0 else slice(16, 128)
                            for g in range(4):
                                gi = 4 * q + g
                                for r in range(2):
                                    ins = nc.tensor.matmul(bank(2 + side)[0:H, g * 112:(g + 1) * 112], BB[h, r, gi, :],
                                                           Hm[h, x, r, g, lags], start=r == 0, stop=r == 1,
                                                           skip_group_check=True)
                            if side == 1:
                                banks.end(ins, ("kb", l, q, 1))
                        for g in range(4):
                            gi = 4 * q + g
                            for r in range(2):
                                ins = nc.tensor.matmul(bank(2)[0:H, 448 + g * H:448 + (g + 1) * H], BB[:, r, gi, :],
                                                       CC[:, r, gi, :], start=r == 0, stop=r == 1, skip_group_check=True)
                        banks.end(ins, ("kb", l, q, 0))
                    if q == 0:
                        pe.wait_ge(rec_done, l + 1)
                    if q >= 1:
                        p = q - 1
                        x = p % 2
                        s = p // 4
                        pe.wait_ge(mi_loaded[x], 16 * T * (4 * l + p // 2 + 1))
                        b = p % 2
                        banks.begin(pe, ("y", l, p), b)
                        rows = slice(s * 64, s * 64 + C - c0)
                        for g in range(4):
                            gi = 4 * p + g
                            o = bank(b)[rows, g * P:(g + 1) * P]
                            nc.tensor.matmul(o, UC[:, gi, c0:C], MI[:, x, g, :], start=True, stop=False)
                            nc.tensor.matmul(o, S[:, 0, gi, c0:C], Hm[:, x, 0, g, :], start=False, stop=False)
                            ins = nc.tensor.matmul(o, S[:, 1, gi, c0:C], Hm[:, x, 1, g, :], start=False, stop=True)
                        banks.end(ins, ("y", l, p))

            def glu(l):
                c0 = 0 if l == 0 else CTX
                pe.wait_ge(ld_y, 16 * (l + 1))
                for f in range(4):
                    b = 6 + f % 2
                    banks.begin(pe, ("yT", l, f), b)
                    for t in toks(l):
                        ins = nc.tensor.transpose(bank(b)[:, t * P:(t + 1) * P], YK[:, t, f * P:(f + 1) * P], EYE)
                    banks.end(ins, ("yT", l, f))
                pe.wait_ge(g_ready, 4 * (l + 1))
                w = unit(("glu", l))
                for f in range(4):
                    key = ("glu", l, f)
                    banks.begin(pe, key, f)
                    for k in range(4):
                        ins = mm3(bank(f)[:, c0:N], lambda x, q: w[q][:, k, f * P:(f + 1) * P],
                                  lambda x, q: GTR[:, x, k, c0:N], k == 0, k == 3)
                    if f < 3:
                        banks.end(ins, key)
                    else:
                        banks.end_unit(ins, key, U[("glu", l)])

            def merge(l):
                c0 = 0 if l == 0 else CTX
                for t in toks(l):
                    banks.released(pe, ("o", l, t))
                for nb in range(2):
                    for name, src in (("pa", OT), ("pb", STR)):
                        w = unit((name, l, nb))
                        if name == "pb" and nb == 0:
                            pe.wait_ge(s_ready, 4 * (l + 1))
                        for f in range(4):
                            key = (name, l, nb, f)
                            b = f if name == "pa" else 4 + f
                            banks.begin(pe, key, b)
                            for k in range(4):
                                ins = mm3(bank(b)[:, c0:N], lambda x, q: w[q][:, k, f * P:(f + 1) * P],
                                          lambda x, q: src[:, x, k, c0:N], k == 0, k == 3)
                            if f < 3:
                                banks.end(ins, key)
                            else:
                                banks.end_unit(ins, key, U[(name, l, nb)])
                pe.wait_ge(m_ready, 8 * (l + 1))
                for nb in range(2):
                    for hf in range(2):
                        w = unit(("out", l, nb, hf))
                        for t in toks(l):
                            key = ("out", l, nb, t)
                            if hf == 0:
                                banks.begin(pe, key, t)
                            for k in range(4):
                                ins = mm3(bank(t)[:, :], lambda x, q: HT[:, x, 4 * hf + k, t * P:(t + 1) * P],
                                          lambda x, q: w[q][:, k, :], hf == 0 and k == 0, hf == 1 and k == 3)
                            if hf == 1 and t == 3:
                                banks.end_unit(ins, key, U[("out", l, nb, hf)])
                            elif hf == 1:
                                banks.end(ins, key)
                            elif t == 3:
                                ins.then_inc(w_used, 1)

            def ffn(l, order, i=None):
                c0 = 0 if l == 0 else CTX
                base = U[("g", 0)] if l == 0 else NU
                per = ECH if l else 0

                def count(v, k):
                    return v if i is None else v + i * k

                for n, (kind, c) in enumerate(order):
                    pe.wait_ge(w_split, count(base + n + 1, len(order)))
                    slot = (base + n) % 3
                    if kind in "gu":
                        w = [unit_view(slot, q, 8, FC) for q in range(2)]
                        for f in range(2):
                            b = (4 if kind == "g" else 6) + f
                            key = (kind, l, c, f)
                            banks.begin(pe, key, b, i, per)
                            for k in range(KT):
                                ins = mm3(bank(b)[:, 0:N - c0], lambda x, q: w[q][:, k, f * P:(f + 1) * P],
                                          lambda x, q: HT[:, x, k, c0:N], k == 0, k == KT - 1)
                            if f == 0:
                                banks.end(ins, key)
                            else:
                                banks.end_unit(ins, key, base + n, EUNITS)
                    else:
                        w = [unit_view(slot, q, 2, D) for q in range(2)]
                        pe.wait_ge(hc_ready, count(ffn_hc0[l] + 2 * (c + 1), 2 * ECH))
                        for t in toks(l):
                            for nb in range(2):
                                key = ("d", l, c, t, nb)
                                b = (2 * t + nb) % 4
                                banks.begin(pe, key, b, i, per)
                                for f in range(2):
                                    ins = mm3(bank(b)[:, :], lambda x, q: HC[:, c % 2, x, f, t * P - c0:(t + 1) * P - c0],
                                              lambda x, q: w[q][:, f, nb * 512:(nb + 1) * 512], f == 0, f == 1)
                                if (t, nb) == (3, 1):
                                    banks.end_unit(ins, key, base + n, EUNITS)
                                else:
                                    banks.end(ins, key)

            def router():
                pe.wait_ge(ht_ready, ht_ready_at[(1, 1)])
                pe.wait_ge(ld_wr, 32)
                banks.begin(pe, "router", 0)
                for t in range(2):
                    for k in range(KT):
                        ins = nc.tensor.matmul(bank(0)[:, t * NE:(t + 1) * NE], HTF[:, k, t * P:(t + 1) * P],
                                               WR[:, k, :], start=k == 0, stop=k == KT - 1)
                banks.end(ins, "router")

            for l in range(L):
                ssm_prep(l)
                columns(l)
                norm(l, 0, range(4))
                inproj(l)
                ssm_in(l)
                gates(l)
                attention(l)
                ssm_out(l)
                glu(l)
                merge(l)
                norm(l, 1, toks(l))
                pe.wait_ge(ht_ready, ht_ready_at[(l, 1)])
                if l == 0:
                    ffn(0, ffn_order(DFF // FC))
                else:
                    router()
                    with pe.Fori(0, NE) as i:
                        ffn(1, eorder, i)

        @block.scalar
        def _(act):
            chain = Chain(act, act_step)
            rounded = [0]

            def round_to(n, i=None, base=0):
                last = NU if i is None else EUNITS
                while rounded[0] <= min(n, last - 1):
                    u = rounded[0]
                    full_u = u if i is None else NU + u
                    slot = full_u % 3
                    if i is None:
                        act.wait_ge(w_landed[slot], 16 * (u // 3 + 1))
                        if u >= 3:
                            act.wait_ge(w_used, u - 2)
                    else:
                        act.wait_ge(w_landed[slot], 16 * (full_u // 3 + 1) + i * (16 * EUNITS // 3))
                        act.wait_ge(w_used, full_u - 2 + i * EUNITS)
                    nc.scalar.activation(split[:, slot, 0, :], raw[:, slot, :], ACT.Copy).then_inc(w_round, 1)
                    rounded[0] += 1

            banks.wait(act, "cond")
            banks.release(nc.scalar.activation(CF[:, :], banks_t[6][:, 0:16], ACT.Silu), "cond")
            banks.released(act, "cond")
            act.wait_ge(cond_zero, 1)
            nc.scalar.activation(CW[:, 0, :, 0:2], CF[:, :].rearrange("p (s k) -> p k s", s=2), ACT.Copy)\
                .then_inc(cond_hi, 1)
            round_to(U[("mod", L - 1, 11, 1)] + 2)

            def norm(l, n, tiles):
                for t in tiles:
                    chain(nc.scalar.activation(JUNK[:, t % 2, :], X[:, t, :], ACT.Square, accum_out=SS[:, t:t + 1]))
                k = norm_no[(l, n)]
                nc.scalar.nop().then_inc(sq_done, 1)
                act.wait_ge(ms_ready, k + 1)
                a0, a1 = tiles[0], tiles[-1] + 1
                nc.scalar.activation(RS[:, a0:a1], RS[:, a0:a1], ACT.Sqrt).then_inc(rt_done, 1)

            def norm_hi(l, n, c0):
                for k in range(KT):
                    banks.released(act, ("norm", l, n, k))
                    if (l, n) == (1, 1):
                        src = HTF[:, k, :]
                    else:
                        src = TN[:, k % 2, c0:N]
                    nc.scalar.activation(HT[:, 0, k, c0:N], src, ACT.Copy).then_inc(ht_hi, 1)

            def square_sums(l, n, src, tiles):
                for t in tiles:
                    chain(nc.scalar.activation(JUNK[:, t % 2, :], src[:, t, :], ACT.Square, accum_out=SS[:, t:t + 1]))
                nc.scalar.nop().then_inc(sq_done, 1)
                act.wait_ge(ms_ready, norm_no[(l, n)] + 1)
                a0, a1 = tiles[0], tiles[-1] + 1
                nc.scalar.activation(RS[:, a0:a1], RS[:, a0:a1], ACT.Sqrt).then_inc(rt_done, 1)

            def store_x(l, n):
                tiles = toks(l)
                act.wait_ge(x_new, x_new_at[(l, n)])
                if (l, n) == (1, 1):
                    for t in (2, 3):
                        act.dma_start(out[0, (t - 2) * P:(t - 1) * P, :], X[:, t, :]).then_inc(out_stored, 16)
                    act.wait_ge(out_stored, 32)
                else:
                    act.dma_start(xscr[2 * l + n, tiles[0] * P:N, :].rearrange("(t p) d -> p t d", p=P),
                                  X[:, tiles[0]:TT, :]).then_inc(x_stored, 16)

            for l in range(L):
                c0 = 0 if l == 0 else CTX
                act.wait_ge(ang_ready, l + 1)
                nc.scalar.activation(ZS[:, 7, :], ZS[:, 6, :], ACT.Sin)
                nc.scalar.activation(ZS[:, 8, :], ZS[:, 6, :], ACT.Sin, scale=0.5).then_inc(sin_done, 1)
                act.wait_ge(ld_x, ld_x_at[(l, 0)])
                norm(l, 0, list(range(4)))
                norm_hi(l, 0, 0)
                round_to(U[("kv", l)] + 2)
                for t in range(4):
                    banks.wait(act, ("kv", l, t))
                    nc.scalar.activation(V[:, t, :], banks_t[t][:, P:2 * P], ACT.Copy).then_inc(v_ready, 1)
                round_to(U[("u", l, 1)] + 2)
                for t in range(4):
                    banks.wait(act, ("u", l, t))
                    if t >= 2:
                        act.wait_ge(u_stored[t % 2], 16 * (2 * l + 1))
                    elif l > 0:
                        act.wait_ge(g_stored[t], 128 * l)
                    banks.release(nc.scalar.activation(STG[:, t % 2, :], banks_t[t][:, :], ACT.Copy), ("u", l, t))
                    banks.released(act, ("u", l, t))
                    act.dma_start(uscr[l, t * P:(t + 1) * P, :], STG[:, t % 2, :]).then_inc(u_stored[t % 2], 16)
                round_to(U[("q", l, 1)] + 2)
                banks.wait(act, ("kT", l))
                banks.release(nc.scalar.activation(kT[:, :], banks_t[7][:, :], ACT.Copy), ("kT", l))
                for t in toks(l):
                    banks.wait(act, ("qT", l, t))
                    banks.release(nc.scalar.activation(qT[:, t, :, :].rearrange("p a b -> p (a b)"),
                                                       banks_t[6 + t % 2][:, :], ACT.Copy), ("qT", l, t))
                for q in range(4):
                    banks.wait(act, ("uc", l, q))
                    banks.release(nc.scalar.activation(UC[:, 8 * q:8 * q + 8, :].rearrange("p a b -> p (a b)"),
                                                       banks_t[6 + q % 2][:, :], ACT.Copy), ("uc", l, q))
                for q in range(8):
                    for r in range(2):
                        banks.wait(act, ("gt", l, q, r))
                        banks.release(nc.scalar.activation(GT[:, r, :, :].rearrange("p a b -> p (a b)"),
                                                           banks_t[4 + r][:, :], ACT.Copy), ("gt", l, q, r))
                    banks.wait(act, ("v", l, q))
                    nc.scalar.activation(S[0:64, :, 4 * q:4 * q + 4, 1:C],
                                         banks_t[q % 2][0:64, :].rearrange("p (r g c) -> p r g c", r=2, g=4)[:, :, :, 0:C - 1],
                                         ACT.Copy).then_inc(v_fwd, 1)
                for i in range(8):
                    round_to(U[("gate", l, i)] + 2)
                    for f in range(2):
                        banks.wait(act, ("gate", l, i, f))
                        if i == 0:
                            act.wait_ge(u_stored[f], 32 * (l + 1))
                        else:
                            act.wait_ge(g_stored[f], 16 * (8 * l + i))
                        banks.release(nc.scalar.activation(STG[:, f, c0:N], banks_t[4 + f][:, 0:N - c0], ACT.Sigmoid),
                                      ("gate", l, i, f))
                        banks.released(act, ("gate", l, i, f))
                        act.dma_start(gscr[l, 2 * i + f, :, c0:N], STG[:, f, c0:N]).then_inc(g_stored[f], 16)
                act.wait_ge(ld_sink, 16 * (l + 1))
                items = att_items(l)

                def exps(i):
                    t, h = items[i]
                    k = att_base[l] + i
                    w = N if t >= 2 else CTX
                    banks.wait(act, ("sc", l, i))
                    act.wait_ge(row_max, k + 1)
                    st = ST[:, i % 2, :]
                    if k >= 2:
                        act.wait_ge(p_norm, k - 1)
                    if i >= 2:
                        banks.wait(act, ("pt", l, i - 2))
                    nc.scalar.activation(LT[:, i % 2, 0:1], SK[:, h:h + 1], ACT.Exp, bias=st[:, 1:2]).then_inc(sink_done, 1)
                    banks.release(nc.scalar.activation(PR[:, i % 2, 0:w], banks_t[4 + i % 2][:, 0:w], ACT.Exp,
                                                       bias=st[:, 1:2], scale=HD ** -0.5, accum_out=st[:, 2:3]),
                                  ("sc", l, i))

                def turned(i):
                    t, h = items[i]
                    w = N if t >= 2 else CTX
                    banks.wait(act, ("pt", l, i))
                    banks.release(nc.scalar.activation(PT[:, i % 2, 0:w // P, :].rearrange("p a b -> p (a b)"),
                                                       banks_t[6 + i % 2][:, 0:w], ACT.Copy), ("pt", l, i))
                    if h == 1 and t > toks(l)[0]:
                        o_part(t - 1)

                def o_part(t):
                    banks.wait(act, ("o", l, t))
                    nc.scalar.activation(OT[:, 0, :, t * P:(t + 1) * P],
                                         banks_t[t % 2][:, :].rearrange("p (k n) -> p k n", k=4), ACT.Copy).then_inc(o_hi, 1)

                n = len(items)
                for i in range(n + 2):
                    if i < n:
                        exps(i)
                    if i >= 2:
                        turned(i - 2)
                o_part(3)
                for q in range(9):
                    if q < 8:
                        x = q % 2
                        if q >= 2:
                            act.wait_ge(mi_loaded[x], 16 * T * (4 * l + q // 2))
                        for side in (1, 0):
                            banks.wait(act, ("kb", l, q, side))
                            ins = nc.scalar.activation(
                                KB[:, x, :, 8 - 8 * side:15 - 8 * side, :],
                                banks_t[2 + side][0:H, 0:448].rearrange("p (g a h) -> p g a h", g=4, a=7), ACT.Copy)
                            if side == 1:
                                banks.release(ins, ("kb", l, q, 1))
                            else:
                                ins.then_inc(kb_copied, 1)
                    if q >= 1:
                        p = q - 1
                        s = p // 4
                        rows = slice(s * 64, s * 64 + (64 if l == 0 else 32))
                        gl = (4 * p) % 16
                        banks.wait(act, ("y", l, p))
                        banks.release(nc.scalar.activation(
                            YY[rows, :, gl * H:(gl + 4) * H].rearrange("p t (g h) -> p g t h", g=4),
                            banks_t[p % 2][rows, :].rearrange("p (g t h) -> p g t h", g=4, t=T), ACT.Copy), ("y", l, p))
                banks.released(act, ("y", l, 6))
                banks.released(act, ("y", l, 7))
                nch = 64 if l == 0 else 32
                for s in range(2):
                    act.dma_start(yscr[l, c0:N, s * 256:(s + 1) * 256].rearrange("(c t) h -> c t h", t=T),
                                  YY[s * 64:s * 64 + nch, :, :]).then_inc(y_stored, 16)
                act.wait_ge(y_stored, 32 * (l + 1))
                act.dma_start(YK[:, c0 // P:TT, :], yscr[l, c0:N, :].rearrange("(t p) n -> p t n", p=P)).then_inc(ld_y, 16)
                for f in range(4):
                    banks.wait(act, ("yT", l, f))
                    banks.release(nc.scalar.activation(GF[:, f, c0:N], banks_t[6 + f % 2][:, c0:N], ACT.Gelu_apprx_tanh),
                                  ("yT", l, f))
                for f in range(4):
                    banks.released(act, ("yT", l, f))
                    nc.scalar.activation(GTR[:, 0, f, c0:N], GF[:, f, c0:N], ACT.Copy).then_inc(g_hi, 1)
                round_to(U[("glu", l)] + 2)
                for f in range(4):
                    banks.wait(act, ("glu", l, f))
                    if f >= 2:
                        act.wait_ge(s_f, 4 * l + f - 1)
                    banks.release(nc.scalar.activation(SGT[:, f % 2, c0:N], banks_t[f][:, c0:N], ACT.Sigmoid,
                                                       bias=COLS[:, 96 + f:97 + f]), ("glu", l, f))
                for f in range(4):
                    act.wait_ge(s_f, 4 * l + f + 1)
                    nc.scalar.activation(STR[:, 0, f, c0:N], SF[:, f % 2, c0:N], ACT.Copy).then_inc(s_hi, 1)
                for nb in range(2):
                    round_to(U[("pb", l, nb)] + 2)
                    for f in range(4):
                        k = 8 * l + 4 * nb + f
                        act.wait_ge(m_f, k + 1)
                        nc.scalar.activation(HT[:, 0, 4 * nb + f, c0:N], MT1[:, f, c0:N], ACT.Copy).then_inc(m_hi, 1)
                for nb in range(2):
                    round_to(U[("out", l, nb, 1)] + 2)
                    for t in toks(l):
                        banks.wait(act, ("out", l, nb, t))
                        banks.release(nc.scalar.activation(YA[:, t, nb * 512:(nb + 1) * 512], banks_t[t][:, :], ACT.Copy),
                                      ("out", l, nb, t))
                for nb in range(2):
                    for t in toks(l):
                        banks.released(act, ("out", l, nb, t))
                square_sums(l, "r0", YA, toks(l))
                store_x(l, 0)
                norm(l, 1, toks(l))
                norm_hi(l, 1, c0)

                def ffn(order, i=None):
                    base = U[("g", 0)] if l == 0 else 0
                    h0 = ffn_hc0[l]
                    v = lambda x: x if i is None else x + i * 2 * ECH
                    for n, (kind, c) in enumerate(order):
                        round_to(base + n + 2, i)
                        if kind == "g":
                            for f in range(2):
                                banks.wait(act, ("g", l, c, f), i)
                                if c > 0:
                                    banks.released(act, ("u", l, c - 1, f), i)
                                elif i is not None:
                                    banks.released(act, ("u", l, ECH - 1, f), i, turns_back=1)
                                banks.release(nc.scalar.activation(SIL[:, f, 0:N - c0], banks_t[4 + f][:, 0:N - c0], ACT.Silu),
                                              ("g", l, c, f))
                        elif kind == "u":
                            for f in range(2):
                                banks.released(act, ("u", l, c, f), i)
                                if c >= 2:
                                    banks.wait(act, ("d", l, c - 2, 3, 1), i)
                                elif i is not None:
                                    act.wait_ge(w_used, NU + EU[("d", ECH - 2 + c)] + 1 - EUNITS + i * EUNITS)
                                nc.scalar.activation(HC[:, c % 2, 0, f, 0:N - c0], HF[:, f, 0:N - c0], ACT.Copy)\
                                    .then_inc(hc_hi, 1)

                if l == 0:
                    ffn(ffn_order(DFF // FC))
                    act.wait_ge(w_used, U[("d", DFF // FC - 1)] + 1)
                else:
                    act.wait_ge(top_diff, 1)
                    nc.scalar.activation(RW[:, :, 2:3], RW[:, :, 1:2], ACT.Exp).then_inc(top_exp, 1)
                    round_to(NU - 1)
                    with act.Fori(0, NE) as i:
                        rounded[0] = 0
                        ffn(eorder, i)
                        round_to(EUNITS - 1, i)
                act.wait_ge(ya_done, l + 1)
                square_sums(l, "r1", YA, toks(l))
                store_x(l, 1)

        @block.vector
        def _(dve):
            chain = Chain(dve, dve_step)
            V_ = nc.vector
            split_n = [0]

            def split_to(n, i=None):
                last = NU if i is None else EUNITS
                while split_n[0] <= min(n, last - 1):
                    u = split_n[0]
                    full_u = u if i is None else NU + u
                    slot = full_u % 3
                    dve.wait_ge(w_round, full_u + 1 if i is None else full_u + 1 + i * EUNITS)
                    V_.tensor_tensor(split[:, slot, 1, :], raw[:, slot, :], split[:, slot, 0, :].bitcast(F),
                                     ALU.subtract).then_inc(w_split, 1)
                    split_n[0] += 1

            def lo(out_, src, hi, sem=None):
                ins = V_.tensor_tensor(out_, src, hi.bitcast(F), ALU.subtract)
                return ins.then_inc(sem, 1) if sem is not None else ins

            V_.memset(CW[:, :, :, :].bitcast(F), 0.0).then_inc(cond_zero, 1)
            dve.wait_ge(cond_zero, 1)
            dve.wait_ge(cond_hi, 1)
            lo(CW[:, 1, :, 0:2], CF[:, :].rearrange("p (s k) -> p k s", s=2), CW[:, 0, :, 0:2], cond_ready)
            dve.wait_ge(ld_const, 16)
            dve.wait_ge(ld_bm, 64)
            for l in range(L):
                for nb in range(12):
                    m = 12 * l + nb
                    split_to(U[("mod", l, nb, 1)] + 2)
                    banks.wait(dve, ("mod", l, nb))
                    if m >= 2:
                        dve.wait_ge(mod_stored[m % 2], 16 * (m // 2))
                    st = MS[:, m % 2, :]
                    banks.release(V_.tensor_tensor(st, banks_t[nb % 4][0:2, :], BM[:, l, nb * 512:(nb + 1) * 512], ALU.add),
                                  ("mod", l, nb))
                    if nb // 2 in (2, 5):
                        j = nb // 2 // 3
                        banks.released(dve, ("mod", l, nb))
                        V_.tensor_tensor(st, st, NG[:, l, j, (nb % 2) * 512:(nb % 2 + 1) * 512], ALU.mult)\
                            .then_inc(mod_row, 1)

            def Z(k):
                return ZS[:, k, :]

            def exact_exp(dst, src):
                chain(V_.tensor_scalar(Z(11), src, -87.0, 88.0, ALU.max, ALU.min))
                chain(V_.tensor_scalar(Z(12), Z(11), INV_LN2, ROUND, ALU.mult, ALU.add))
                chain(V_.tensor_scalar(Z(12), Z(12), -ROUND, None, ALU.add))
                for part in LN2:
                    chain(V_.scalar_tensor_tensor(Z(11), Z(12), -part, Z(11), ALU.mult, ALU.add))
                chain(V_.tensor_scalar(Z(13), Z(11), 1.0 / 7, 1.0, ALU.mult, ALU.add))
                for j in range(6, 0, -1):
                    chain(V_.scalar_tensor_tensor(Z(13), Z(13), 1.0 / j, Z(11), ALU.mult, ALU.mult))
                    chain(V_.tensor_scalar(Z(13), Z(13), 1.0, None, ALU.add))
                chain(V_.tensor_scalar(ZI[:, :], Z(12), 127.0, 8388608.0, ALU.add, ALU.mult))
                chain(V_.tensor_tensor(dst, Z(13), ZI[:, :].bitcast(F), ALU.mult))

            def cmul(ore, oim, ar, ai, br, bi, t0, t1):
                chain(V_.tensor_tensor(t0, ai, bi, ALU.mult))
                chain(V_.tensor_tensor(ore, ar, br, ALU.mult))
                chain(V_.tensor_tensor(t1, ai, br, ALU.mult))
                chain(V_.tensor_tensor(oim, ar, bi, ALU.mult))
                chain(V_.tensor_tensor(ore, ore, t0, ALU.subtract))
                chain(V_.tensor_tensor(oim, oim, t1, ALU.add))

            def ssm_prep(l):
                dve.wait_ge(ld_ssm, LD_SSM * (l + 1))
                for r in range(2):
                    banks.wait(dve, ("arow", l, r))
                    banks.release(V_.tensor_copy(Z(r), banks_t[6 + r][:, 0:G]), ("arow", l, r))
                    banks.released(dve, ("arow", l, r))
                for r in range(2):
                    banks.wait(dve, ("crow", l, r))
                    ins = V_.tensor_scalar(CC[:, r, :, :].rearrange("p a b -> p (a b)"), banks_t[4 + r][:, :],
                                           1.0 if r == 0 else -1.0, None, ALU.mult)
                    banks.release(ins, ("crow", l, r))
                    banks.released(dve, ("crow", l, r))
                exact_exp(Z(2), DTR[:, :])
                chain(V_.tensor_tensor(Z(3), Z(0), Z(2), ALU.mult))
                exact_exp(Z(4), Z(3))
                chain(V_.tensor_tensor(Z(5), Z(1), Z(2), ALU.mult))
                chain(V_.tensor_scalar(Z(10), Z(5), 1.0 / TWO_PI, ROUND, ALU.mult, ALU.add))
                chain(V_.tensor_scalar(Z(10), Z(10), -ROUND, None, ALU.add))
                chain(V_.tensor_copy(Z(6), Z(5)))
                for part in PI_PARTS:
                    chain(V_.scalar_tensor_tensor(Z(6), Z(10), -part, Z(6), ALU.mult, ALU.add))
                V_.tensor_scalar(Z(6), Z(6), 3.1415925, -3.1415925, ALU.min, ALU.max).then_inc(ang_ready, 1)
                dve.wait_ge(sin_done, l + 1)
                chain(V_.tensor_tensor(Z(9), Z(8), Z(8), ALU.mult))
                chain(V_.tensor_scalar(Z(9), Z(9), -2.0, 1.0, ALU.mult, ALU.add))
                chain(V_.memset(PW[:, 0, 0, :], 1.0))
                chain(V_.memset(PW[:, 1, 0, :], 0.0))
                chain(V_.tensor_tensor(PW[:, 0, 1, :], Z(4), Z(9), ALU.mult))
                chain(V_.tensor_tensor(PW[:, 1, 1, :], Z(4), Z(7), ALU.mult))
                chain(V_.tensor_tensor(Z(10), Z(0), Z(0), ALU.mult))
                chain(V_.tensor_tensor(Z(11), Z(1), Z(1), ALU.mult))
                chain(V_.tensor_tensor(Z(10), Z(10), Z(11), ALU.add))
                chain(V_.reciprocal(Z(10), Z(10)))
                chain(V_.tensor_scalar(Z(11), PW[:, 0, 1, :], -1.0, None, ALU.add))
                chain(V_.tensor_scalar(Z(12), Z(1), -1.0, None, ALU.mult))
                cmul(Z(13), Z(14), Z(11), PW[:, 1, 1, :], Z(0), Z(12), Z(3), Z(5))
                chain(V_.tensor_tensor(Z(13), Z(13), Z(10), ALU.mult))
                chain(V_.tensor_tensor(Z(14), Z(14), Z(10), ALU.mult))
                wide = lambda z: z.unsqueeze(2).broadcast_to([P, G, H])
                t0, t1 = (BT[:, r, :].rearrange("p (g h) -> p g h", g=G) for r in range(2))
                cmul(BB[:, 0, :, :], BB[:, 1, :, :], wide(Z(13)), wide(Z(14)), BI[:, 0, :, :], BI[:, 1, :, :], t0, t1)
                for k in (1, 2, 4):
                    n = k
                    b = lambda r: PW[:, r, k:k + 1, :].broadcast_to([P, n, G])
                    tmp = [BT[:, r, 0:n * G].rearrange("p (t g) -> p t g", t=n) for r in range(2)]
                    cmul(PW[:, 0, k + 1:k + n + 1, :], PW[:, 1, k + 1:k + n + 1, :], PW[:, 0, 1:n + 1, :],
                         PW[:, 1, 1:n + 1, :], b(0), b(1), *tmp)
                f, w = slice(0, 64), slice(64, P)
                for r in range(2):
                    chain(V_.tensor_copy(PG[f, 0, r, :, :], PW[f, r, 7::-1, :]))
                    chain(V_.tensor_copy(PG[w, 0, r, :, :], PW[w, r, 0:8, :]))
                    chain(V_.tensor_copy(PG[f, 1, r, :, :], PW[f, r, 1:9, :]))
                    chain(V_.tensor_copy(PG[w, 1, r, :, :], PW[w, r, 8:0:-1, :]))
                    chain(V_.tensor_copy(A8[:, 0, r, :], PW[:, 0, 8, :]))
                chain(V_.tensor_scalar(A8[:, 1, 0, :], PW[:, 1, 8, :], -1.0, None, ALU.mult))
                V_.tensor_copy(A8[:, 1, 1, :], PW[:, 1, 8, :]).then_inc(prep_done, 1)

            def columns(l):
                banks.wait(dve, ("cols", l))
                banks.release(V_.tensor_copy(COLS[:, :], banks_t[7][:, 0:100]), ("cols", l))
                banks.released(dve, ("cols", l))
                for s in range(2):
                    for n in range(2):
                        c = s * 32 + (8 if n == 0 else 24)
                        chain(V_.scalar_tensor_tensor(AF[:, s, n, :], COLS[:, c:c + 8], 1.0,
                                                      COLS[:, 64 + 16 * n:72 + 16 * n], ALU.add, ALU.mult))

            def rstd(l, n, tiles):
                k = norm_no[(l, n)]
                a0, a1 = tiles[0], tiles[-1] + 1
                dve.wait_ge(sq_done, k + 1)
                V_.tensor_scalar(RS[:, a0:a1], SS[:, a0:a1], 1.0 / D, EPS, ALU.mult, ALU.add).then_inc(ms_ready, 1)
                dve.wait_ge(rt_done, k + 1)
                chain(V_.reciprocal(RS[:, a0:a1], RS[:, a0:a1]))

            def norm(l, n, tiles):
                rstd(l, n, tiles)
                if (l, n) != (0, 0):
                    dve.wait_ge(x_stored, 16 * x_stores_before[(l, n)])
                for t in tiles:
                    V_.tensor_scalar(X[:, t, :], X[:, t, :], RS[:, t:t + 1], None, ALU.mult).then_inc(xn_ready, 1)
                for k in range(KT):
                    key = ("norm", l, n, k)
                    b = banks_t[6 + k % 2]
                    banks.wait(dve, key)
                    kk = ht_ready_at[(l, n)] - 8 + k
                    if kk >= 2:
                        dve.wait_ge(ht_ready, kk - 1)
                    dst = (lambda s: HTF[:, k, :]) if (l, n) == (1, 1) else (lambda s: TN[:, k % 2, s * CTX:(s + 1) * CTX])
                    for s in sorted({t // 2 for t in tiles}):
                        c = s * 32 + 16 * n + k
                        ins = V_.tensor_scalar(dst(s), b[:, s * CTX:(s + 1) * CTX], AF[:, s, n, k:k + 1],
                                               COLS[:, c:c + 1], ALU.mult, ALU.add)
                    banks.release(ins, key)
                    banks.released(dve, key)
                    dve.wait_ge(ht_hi, kk + 1)
                    a0 = tiles[0] * P
                    src = HTF[:, k, :] if (l, n) == (1, 1) else TN[:, k % 2, a0:N]
                    lo(HT[:, 1, k, a0:N], src, HT[:, 0, k, a0:N], ht_ready)

            def rope(src, dst, nh, t, key, done):
                c = COS[:, t - 2, :]
                s = SIN[:, t - 2, :]
                shape = dst(0).shape
                bc = lambda z: z.unsqueeze(1).unsqueeze(1).broadcast_to(list(shape))
                t0 = TM[:, 0:nh * 32].rearrange("p (a b c) -> p a b c", b=shape[2], c=32)
                t1 = TM[:, 256:256 + nh * 32].rearrange("p (a b c) -> p a b c", b=shape[2], c=32)
                chain(V_.tensor_tensor(dst(0), src(0), bc(c), ALU.mult))
                chain(V_.tensor_tensor(t0, src(1), bc(s), ALU.mult))
                chain(V_.tensor_tensor(dst(1), src(1), bc(c), ALU.mult))
                ins = V_.tensor_tensor(t1, src(0), bc(s), ALU.mult)
                banks.release(ins, key)
                banks.released(dve, key)
                chain(V_.tensor_tensor(dst(0), dst(0), t0, ALU.subtract))
                V_.tensor_tensor(dst(1), dst(1), t1, ALU.add).then_inc(done, 1)
                dve.wait_ge(done, done_n[done.name] + 1)
                done_n[done.name] += 1

            done_n = {q_tok.name: 0, k_tok.name: 0}

            def inproj(l):
                split_to(U[("kv", l)] + 2)
                for t in range(4):
                    key = ("kv", l, t)
                    banks.wait(dve, key)
                    dve.wait_ge(v_ready, 4 * l + t + 1)
                    b = banks_t[t]
                    if t < 2:
                        banks.release(V_.tensor_copy(KS[:, t, :], b[:, 0:P]), key)
                    else:
                        sv = b[:, 0:P].rearrange("p (g a d) -> p g a d", g=2, a=2)
                        dv = KS[:, t, :].rearrange("p (g a d) -> p g a d", g=2, a=2)
                        rope(lambda x: sv[:, :, x:x + 1, :], lambda x: dv[:, :, x:x + 1, :], 2, t, key, k_tok)
                split_to(U[("u", l, 1)] + 2)
                split_to(U[("q", l, 1)] + 0)
                for t in toks(l):
                    key = ("q", l, t)
                    if t == toks(l)[0]:
                        split_to(U[("q", l, 1)] + 2)
                    banks.wait(dve, key)
                    b = banks_t[t]
                    if t < 2:
                        banks.release(V_.tensor_copy(
                            QS[:, t, :].rearrange("p (j g d) -> p g j d", j=4, g=2),
                            b[:, :].rearrange("p (g j d) -> p g j d", g=2, j=4)), key)
                    else:
                        sv = b[:, :].rearrange("p (g j a d) -> p g j a d", g=2, j=4, a=2)
                        dv = QS[:, t, :].rearrange("p (j g a d) -> p g j a d", j=4, g=2, a=2)
                        rope(lambda x: sv[:, :, :, x, :], lambda x: dv[:, :, :, x, :], 8, t, key, q_tok)

            def mats(dst, powers, m, q):
                gs = slice(4 * q, 4 * q + 4)
                pw = [powers[:, r, :, gs].rearrange("p t g -> p g t").unsqueeze(3).broadcast_to([P, 4, T, H]) for r in range(2)]
                mm = [m[:, r, gs, :].unsqueeze(2).broadcast_to([P, 4, T, H]) for r in range(2)]
                tm = TM[:, :].rearrange("p (g t h) -> p g t h", g=4, t=T)
                o = [dst(r).rearrange("p g (t h) -> p g t h", t=T) for r in range(2)]
                return pw, mm, tm, o

            def ssm_in(l):
                banks.wait(dve, ("qT", l, 3))
                for q in range(8):
                    pw, mm, tm, o = mats(lambda r: GP[:, r, :, :], PG[:, 0], BB, q)
                    if q > 0:
                        for r in range(2):
                            banks.wait(dve, ("gt", l, q - 1, r))
                    chain(V_.tensor_tensor(tm, pw[1], mm[1], ALU.mult))
                    chain(V_.tensor_tensor(o[0], pw[0], mm[0], ALU.mult))
                    chain(V_.tensor_tensor(o[0], o[0], tm, ALU.subtract))
                    chain(V_.tensor_tensor(tm, pw[1], mm[0], ALU.mult))
                    chain(V_.tensor_tensor(o[1], pw[0], mm[1], ALU.mult))
                    V_.tensor_tensor(o[1], o[1], tm, ALU.add).then_inc(gp_ready, 1)
                    dve.wait_ge(gp_ready, 8 * l + q + 1)
                    if q > 0:
                        v_back(l, q - 1)
                v_back(l, 7)

            def v_back(l, q):
                key = ("v", l, q)
                banks.wait(dve, key)
                dve.wait_ge(v_fwd, 8 * l + q + 1)
                v = banks_t[q % 2][64:P, :].rearrange("p (r g c) -> p r g c", r=2, g=4)
                s = S[64:P, :, 4 * q:4 * q + 4, :]
                chain(V_.tensor_copy(s[:, :, :, 0:31], v[:, :, :, 1:32]))
                chain(V_.tensor_copy(s[:, :, :, 32:63], v[:, :, :, 33:64]))
                banks.release(V_.tensor_copy(s[:, :, :, 63:64], v[:, :, :, 0:1]), key)

            def attention(l):
                items = att_items(l)
                dve.wait_ge(ld_sink, 16 * (l + 1))

                def maxes(i):
                    t, h = items[i]
                    w = N if t >= 2 else CTX
                    st = ST[:, i % 2, :]
                    banks.wait(dve, ("sc", l, i))
                    chain(V_.reduce_max(st[:, 0:1], banks_t[4 + i % 2][:, 0:w], AX))
                    chain(V_.tensor_scalar(st[:, 0:1], st[:, 0:1], HD ** -0.5, SK[:, h:h + 1], ALU.mult, ALU.max))
                    V_.tensor_scalar(st[:, 1:2], st[:, 0:1], -1.0, None, ALU.mult).then_inc(row_max, 1)

                def norms(i):
                    t, h = items[i]
                    w = N if t >= 2 else CTX
                    st = ST[:, i % 2, :]
                    banks.released(dve, ("sc", l, i))
                    chain(V_.tensor_tensor(st[:, 3:4], st[:, 2:3], LT[:, i % 2, 0:1], ALU.add))
                    chain(V_.reciprocal(st[:, 4:5], st[:, 3:4]))
                    V_.tensor_scalar(PR[:, i % 2, 0:w], PR[:, i % 2, 0:w], st[:, 4:5], None, ALU.mult).then_inc(p_norm, 1)
                    dve.wait_ge(p_norm, att_base[l] + i + 1)
                    if h == 5 and t > toks(l)[0]:
                        o_part(t - 1)

                def o_part(t):
                    dve.wait_ge(o_hi, t + 1 if l == 0 else 2 + t + 1)
                    banks.release(lo(OT[:, 1, :, t * P:(t + 1) * P], banks_t[t % 2][:, :].rearrange("p (k n) -> p k n", k=4),
                                     OT[:, 0, :, t * P:(t + 1) * P]), ("o", l, t))

                for i in range(len(items) + 1):
                    if i < len(items):
                        maxes(i)
                    if i >= 1:
                        norms(i - 1)
                o_part(3)

            def ssm_out(l):
                dve.wait_ge(ld_skip, 16 * (l + 1))
                chain(V_.tensor_tensor(DR[:, :, :], DR[:, :, :], EYE[0:H, 0:H].unsqueeze(1).broadcast_to([H, G, H]), ALU.mult))
                for q in range(9):
                    if q < 8:
                        x = q % 2
                        if q >= 2:
                            banks.wait(dve, ("y", l, q - 2))
                        else:
                            banks.wait(dve, ("gate", l, 7, 1))
                        pw, mm, tm, o = mats(lambda r: Hm[:, x, r, :, :], PG[:, 1], CC, q)
                        chain(V_.tensor_tensor(tm, pw[1], mm[1], ALU.mult))
                        chain(V_.tensor_tensor(o[0], pw[0], mm[0], ALU.mult))
                        chain(V_.tensor_tensor(o[0], o[0], tm, ALU.add))
                        chain(V_.tensor_tensor(tm, pw[1], mm[0], ALU.mult))
                        chain(V_.tensor_tensor(o[1], pw[0], mm[1], ALU.mult))
                        V_.tensor_tensor(o[1], o[1], tm, ALU.subtract).then_inc(h_ready, 1)
                        dve.wait_ge(h_ready, 8 * l + q + 1)
                    if q >= 1:
                        p = q - 1
                        dve.wait_ge(kb_copied, 8 * l + p + 1)
                        banks.release(V_.tensor_tensor(KB[:, p % 2, :, 7, :], DR[:, 4 * p:4 * p + 4, :],
                                                       banks_t[2][0:H, 448:512].rearrange("p (g h) -> p g h", g=4), ALU.add),
                                      ("kb", l, p, 0))

            def glu(l):
                c0 = 0 if l == 0 else CTX
                for f in range(4):
                    dve.wait_ge(g_hi, 4 * l + f + 1)
                    lo(GTR[:, 1, f, c0:N], GF[:, f, c0:N], GTR[:, 0, f, c0:N], g_ready)
                split_to(U[("glu", l)] + 2)
                for f in range(4):
                    banks.released(dve, ("glu", l, f))
                    if f >= 2:
                        dve.wait_ge(s_ready, 4 * l + f - 1)
                    V_.tensor_tensor(SF[:, f % 2, c0:N], GF[:, f, c0:N], SGT[:, f % 2, c0:N], ALU.mult).then_inc(s_f, 1)
                    if f >= 1:
                        s_lo(l, f - 1)
                s_lo(l, 3)

            def s_lo(l, f):
                c0 = 0 if l == 0 else CTX
                dve.wait_ge(s_hi, 4 * l + f + 1)
                lo(STR[:, 1, f, c0:N], SF[:, f % 2, c0:N], STR[:, 0, f, c0:N], s_ready)

            def merge(l):
                c0 = 0 if l == 0 else CTX
                for nb in range(2):
                    split_to(U[("pa", l, nb)] + 2)
                    for f in range(4):
                        ft = 8 * l + 4 * nb + f
                        banks.wait(dve, ("pa", l, nb, f))
                        dve.wait_ge(ld_g[f % 2], 32 * (ft // 2 + 1))
                        if nb > 0:
                            dve.wait_ge(m_ready, 8 * l + f + 1)
                        banks.release(V_.tensor_tensor(MT1[:, f, c0:N], banks_t[f][:, c0:N], SGA[:, f % 2, c0:N], ALU.mult),
                                      ("pa", l, nb, f))
                        banks.released(dve, ("pa", l, nb, f))
                        if f == 3:
                            split_to(U[("pb", l, nb)] + 2)
                        if f < 3:
                            split_to(U[("pa", l, nb)] + 2)
                        merge_b(l, nb, f, c0)

            def merge_b(l, nb, f, c0):
                k = 8 * l + 4 * nb + f
                banks.wait(dve, ("pb", l, nb, f))
                banks.release(V_.tensor_tensor(TM[:, c0:N], banks_t[4 + f][:, c0:N], SGB[:, f % 2, c0:N], ALU.mult),
                              ("pb", l, nb, f))
                banks.released(dve, ("pb", l, nb, f))
                V_.tensor_tensor(MT1[:, f, c0:N], MT1[:, f, c0:N], TM[:, c0:N], ALU.add).then_inc(m_f, 1)
                dve.wait_ge(m_hi, k + 1)
                lo(HT[:, 1, 4 * nb + f, c0:N], MT1[:, f, c0:N], HT[:, 0, 4 * nb + f, c0:N], m_ready)

            def residual(l, n):
                rstd(l, f"r{n}", toks(l))
                dve.wait_ge(ld_gb, 32 * (2 * l + n + 1))
                dve.wait_ge(ld_x, ld_x_at[(l, n + 1)])
                for t in toks(l):
                    chain(V_.scalar_tensor_tensor(YA[:, t, :], YA[:, t, :], RS[:, t:t + 1], GB[:, t // 2, :], ALU.mult, ALU.mult))
                    V_.tensor_tensor(X[:, t, :], X[:, t, :], YA[:, t, :], ALU.add).then_inc(x_new, 1)
                dve.wait_ge(x_new, x_new_at[(l, n)])

            def ffn(l, order, i=None):
                c0 = 0 if l == 0 else CTX
                base = U[("g", 0)] if l == 0 else 0
                h0 = ffn_hc0[l]
                v = lambda x: x if i is None else x + i * 2 * ECH
                for n, (kind, c) in enumerate(order):
                    split_to(base + n + 2, i)
                    if kind == "u":
                        for f in range(2):
                            banks.released(dve, ("g", l, c, f), i)
                            banks.wait(dve, ("u", l, c, f), i)
                            if h0 + 2 * c + f >= 2:
                                dve.wait_ge(hc_ready, v(h0 + 2 * c + f - 1))
                            banks.release(V_.tensor_tensor(HF[:, f, 0:N - c0], banks_t[6 + f][:, 0:N - c0],
                                                           SIL[:, f, 0:N - c0], ALU.mult), ("u", l, c, f))
                        for f in range(2):
                            dve.wait_ge(hc_hi, v(h0 + 2 * c + f + 1))
                            lo(HC[:, c % 2, 1, f, 0:N - c0], HF[:, f, 0:N - c0], HC[:, c % 2, 0, f, 0:N - c0], hc_ready)
                    elif kind == "d":
                        for t in toks(l):
                            for nb in range(2):
                                key = ("d", l, c, t, nb)
                                banks.wait(dve, key, i)
                                y = YA[:, t, nb * 512:(nb + 1) * 512]
                                b = banks_t[(2 * t + nb) % 4][:, :]
                                if l == 1:
                                    ins = V_.scalar_tensor_tensor(y, b, GC[:, t - 2:t - 1], y, ALU.mult, ALU.add)
                                elif c == 0:
                                    ins = V_.tensor_copy(y, b)
                                else:
                                    ins = V_.tensor_tensor(y, y, b, ALU.add)
                                banks.release(ins, key)

            def router():
                banks.wait(dve, "router")
                dve.wait_ge(ld_wr, 32)
                banks.release(V_.tensor_tensor(LG[:, :, :], banks_t[0][:, 0:2 * NE].rearrange("p (t e) -> p t e", t=2),
                                               BR[:, :].unsqueeze(1).broadcast_to([P, 2, NE]), ALU.add), "router")
                banks.released(dve, "router")
                for t in range(2):
                    for j in range(2):
                        chain(V_.reduce_max(TV[:, t, j:j + 1], LG[:, t, :], AX))
                        chain(V_.scalar_tensor_tensor(TF[:, t, :], LG[:, t, :], TV[:, t, j:j + 1], IOTA8,
                                                      ALU.is_equal, ALU.mult))
                        chain(V_.tensor_reduce(RW[:, t, 3 + j:4 + j], TF[:, t, :], AX, ALU.min))
                        if j == 0:
                            chain(V_.tensor_scalar(TF[:, t, :], IOTA8, RW[:, t, 3:4], None, ALU.is_equal))
                            chain(V_.scalar_tensor_tensor(LG[:, t, :], TF[:, t, :], -1e30, LG[:, t, :], ALU.mult, ALU.add))
                    ins = V_.tensor_tensor(RW[:, t, 1:2], TV[:, t, 1:2], TV[:, t, 0:1], ALU.subtract)
                    if t == 0:
                        chain(ins)
                ins.then_inc(top_diff, 1)
                dve.wait_ge(top_exp, 1)
                for t in range(2):
                    e = RW[:, t, 2:3]
                    chain(V_.tensor_scalar(RW[:, t, 5:6], e, 1.0, None, ALU.add))
                    chain(V_.reciprocal(RW[:, t, 6:7], RW[:, t, 5:6]))
                    chain(V_.tensor_tensor(RW[:, t, 7:8], e, RW[:, t, 6:7], ALU.mult))
                    chain(V_.tensor_scalar(GA[:, t, :], IOTA8, RW[:, t, 3:4], RW[:, t, 6:7], ALU.is_equal, ALU.mult))
                    chain(V_.tensor_scalar(TF[:, t, :], IOTA8, RW[:, t, 4:5], RW[:, t, 7:8], ALU.is_equal, ALU.mult))
                    chain(V_.tensor_tensor(GA[:, t, :], GA[:, t, :], TF[:, t, :], ALU.add))

            for l in range(L):
                ssm_prep(l)
                columns(l)
                norm(l, 0, list(range(4)))
                inproj(l)
                ssm_in(l)
                split_to(U[("gate", l, 7)] + 2)
                attention(l)
                ssm_out(l)
                glu(l)
                merge(l)
                split_to(U[("out", l, 1, 1)] + 2)
                residual(l, 0)
                norm(l, 1, toks(l))
                if l == 0:
                    ffn(0, ffn_order(DFF // FC))
                    for t in range(2):
                        for nb in range(2):
                            banks.released(dve, ("d", 0, DFF // FC - 1, 2 + t, nb))
                else:
                    router()
                    chain(V_.memset(YA[:, 2:4, :], 0.0))
                    n0 = chain.n
                    with dve.Fori(0, NE) as i:
                        split_n[0] = 0
                        dve.wait_ge(free[3], banks.emptied[("d", 1, 0, 3, 1)][1] - 1 + i * ECH)
                        V_.tensor_copy(GC[:, :], GA[:, :, bass.ds(i, 1)].rearrange("p a b -> p (a b)")).then_inc(dve_step, 1)
                        dve.wait_ge(dve_step, n0 + 1 + i)
                        ffn(1, eorder, i)
                        split_to(EUNITS - 1, i)
                    chain.n = n0 + NE
                    for t in range(2):
                        for nb in range(2):
                            banks.released(dve, ("d", 1, ECH - 1, 2 + t, nb), NE - 1)
                dve.nop().then_inc(ya_done, 1)
                residual(l, 1)

        @block.gpsimd
        def _(pool):
            pool.dma_start(CT[:, :], consts).then_inc(ld_const, 16)
            pool.dma_start(CV[8:16, :], a["c"].rearrange("b (k p) -> (b k) p", p=P)).then_inc(ld_cond, 16)
            pool.dma_start(CV[0:8, :], a["c_ctx"].rearrange("(k p) -> k p", p=P)).then_inc(ld_cond, 16)
            for s in range(2):
                pool.dma_start(BM[s:s + 1, :, :], a["b_mod"].unsqueeze(0)).then_inc(ld_bm, 16)
                pool.dma_start(NG[s:s + 1, :, :, :], a["norm_g"][:, 1::2, :].unsqueeze(0)).then_inc(ld_bm, 16)

            def ssm_loads(l):
                if l > 0:
                    pool.wait_ge(x_new, x_new_at[(0, 1)])
                for d in range(2):
                    h = slice(64 * d, 64 * d + 64)
                    for r, name in enumerate(("ssm_a_re", "ssm_a_im")):
                        pool.dma_start(ARI[:, r, h], a[name][l, d]).then_inc(ld_ssm, 16)
                    for r, name in enumerate(("ssm_b_re", "ssm_b_im")):
                        pool.dma_start(BI[h, r, :, :], a[name][l, d].rearrange("g p h -> p g h")).then_inc(ld_ssm, 16)
                    for r, name in enumerate(("ssm_c_re", "ssm_c_im")):
                        pool.dma_start(CI[:, r, :, d, :], a[name][l, d].rearrange("(b g) h p -> (g h) b p", g=8))\
                            .then_inc(ld_ssm, 16)

            for l in range(L):
                for d in range(2):
                    if l > 0 and d == 0:
                        pool.wait_ge(x_new, x_new_at[(0, 1)])
                    pool.dma_start(DTR[64 * d:64 * d + 64, :], a["ssm_log_dt"][l, d].partition_broadcast(64))\
                        .then_inc(ld_ssm, 16)
                ssm_loads(l)
                if l == 0:
                    pool.dma_start(X[:, 0:2, :], a["ctx"][0].rearrange("(t p) d -> p t d", p=P)).then_inc(ld_x, 16)
                    pool.dma_start(X[:, 2:4, :], a["x"][0].rearrange("(t p) d -> p t d", p=P)).then_inc(ld_x, 16)
                    gates_seen = 0
                    for m in range(12 * L):
                        ll, nb = m // 12, m % 12
                        if nb // 2 in (2, 5):
                            gates_seen += 1
                            pool.wait_ge(mod_row, gates_seen)
                        else:
                            banks.released(pool, ("mod", ll, nb))
                        pool.dma_start(modrow[ll, :, nb * 512:(nb + 1) * 512], MS[:, m % 2, :]).then_inc(mod_stored[m % 2], 16)
                    for x in range(2):
                        pool.wait_ge(mod_stored[x], 16 * 6 * L)
                for s in range(2):
                    for j, c in enumerate((0, 3072)):
                        pool.dma_start(CR[s * 32 + 16 * j:s * 32 + 16 * j + 16, :],
                                       modrow[l, s, c:c + 2048].rearrange("(k p) -> k p", p=P)).then_inc(ld_cols, 16)
                pool.dma_start(CR[64:96, :], a["norm_g"][l].rearrange("n (k p) -> (n k) p", p=P)).then_inc(ld_cols, 16)
                pool.dma_start(CR[96:100, :], a["b_glu"][l].rearrange("(k p) -> k p", p=P)).then_inc(ld_cols, 16)
                pool.dma_start(SK[:, :], a["attn_sink"][l].partition_broadcast(P)).then_inc(ld_sink, 16)
                for x in range(2):
                    pool.wait_ge(u_stored[x], 32 * (l + 1))
                pool.wait_ge(prep_done, l + 1)
                for s in range(2):
                    pool.dma_start(UU[s * 64:(s + 1) * 64, :, :],
                                   uscr[l, :, s * 256:(s + 1) * 256].rearrange("(c t) h -> c t h", t=T)).then_inc(ld_u, 16)
                pool.wait_ge(ld_u, 32 * (l + 1))
                for s in range(2):
                    h = slice(64 * s, 64 * s + 64)
                    nc.gpsimd.tensor_copy(UP[h, :, :, :].rearrange("p g t h -> p t g h"),
                                          UU[h, :, :].rearrange("p t (g h) -> p t g h", g=H)).then_inc(u_grouped, 1)
                banks.released(pool, ("kT", l))
                pool.dma_start(DR[:, :, :].rearrange("p g h -> p (g h)"), a["ssm_d"][l].partition_broadcast(H))\
                    .then_inc(ld_skip, 16)
                for q in range(8):
                    banks.released(pool, ("v", l, q))
                base = pool_n[0]
                nc.gpsimd.memset(S[0:64, :, :, 0:1], 0.0).then_inc(pool_step, 1)
                nc.gpsimd.memset(S[64:P, :, :, 31:32], 0.0).then_inc(pool_step, 1)
                pool.wait_ge(pool_step, base + 2)
                n = base + 2
                fwd = [(i, i + 1) for i in range(1, 63)]
                bwd = [(c, c - 1) for c in range(30, 0, -1)] + [(0, 63)] + [(c, c - 1) for c in range(63, 32, -1)]
                for pair in zip(fwd, bwd):
                    sides = [(slice(0, 64), pair[0]), (slice(64, P), pair[1])]
                    for stage in range(4):
                        for h, (p0, p1) in sides:
                            s = S[h, :, :, p0]
                            d = S[h, :, :, p1]
                            m0, m1 = RT[h, 0, :, :], RT[h, 1, :, :]
                            if n > base + 2:
                                pool.wait_ge(pool_step, n - 1)
                            if stage == 0:
                                ins = nc.gpsimd.tensor_tensor(m0, A8[h, 0, :, :], s, ALU.mult)
                            elif stage == 1:
                                ins = nc.gpsimd.tensor_tensor(m1, A8[h, 1, :, :], s[:, ::-1, :], ALU.mult)
                            elif stage == 2:
                                ins = nc.gpsimd.tensor_tensor(m0, m0, m1, ALU.add)
                            else:
                                ins = nc.gpsimd.tensor_tensor(d, d, m0, ALU.add)
                            ins.then_inc(pool_step, 1)
                            n += 1
                pool.wait_ge(pool_step, n)
                pool_n[0] = n
                pool.nop().then_inc(rec_done, 1)
                for x in range(2):
                    pool.wait_ge(g_stored[x], 128 * (l + 1))
                c0 = 0 if l == 0 else CTX
                for ft in range(8):
                    if ft >= 2:
                        pool.wait_ge(m_f, 8 * l + ft - 1)
                    elif ft == 0:
                        banks.released(pool, ("o", l, 3))
                    pool.dma_start(SGA[:, ft % 2, c0:N], gscr[l, ft, :, c0:N]).then_inc(ld_g[ft % 2], 16)
                    pool.dma_start(SGB[:, ft % 2, c0:N], gscr[l, 8 + ft, :, c0:N]).then_inc(ld_g[ft % 2], 16)
                for n_ in range(2):
                    if n_ == 0:
                        pool.wait_ge(m_ready, 8 * (l + 1))
                    else:
                        pool.wait_ge(ht_ready, ht_ready_at[(l, 1)])
                        pool.wait_ge(x_stored, 16 * (2 * l + 1))
                    for s in range(2):
                        pool.dma_start(GB[:, s, :], modrow[l, s, (3 * n_ + 2) * D:(3 * n_ + 3) * D].partition_broadcast(P))\
                            .then_inc(ld_gb, 16)
                    if (l, n_) == (0, 0):
                        pool.dma_start(X[:, 0:2, :], a["ctx"][0].rearrange("(t p) d -> p t d", p=P)).then_inc(ld_x, 16)
                        pool.dma_start(X[:, 2:4, :], a["x"][0].rearrange("(t p) d -> p t d", p=P)).then_inc(ld_x, 16)
                    else:
                        t0 = toks(l)[0]
                        pool.dma_start(X[:, t0:TT, :], xscr[2 * l + n_ - 1, t0 * P:N, :].rearrange("(t p) d -> p t d", p=P)).then_inc(ld_x, 16)

        @block.sync
        def _(sp):
            loaded = [0]

            def load_to(n):
                while loaded[0] <= min(n, NU - 1):
                    u = loaded[0]
                    if u >= 3:
                        sp.wait_ge(w_split, u - 2)
                    _, src, nk, ncol = units[u]
                    sp.dma_start(raw[:, u % 3, :].rearrange("p (a n) -> p a n", a=nk), src).then_inc(w_landed[u % 3], 16)
                    loaded[0] += 1

            for l in range(L):
                load_to(U[("glu", l)] + 2)
                for q in range(8):
                    x = q % 2
                    for side in range(2):
                        banks.released(sp, ("kb", l, q, side))
                    if q >= 2:
                        banks.wait(sp, ("y", l, q - 2))
                    for t in range(T):
                        sp.dma_start(MI[t * H:(t + 1) * H, x, :, :],
                                     KB[:, x, :, 7 - t:15 - t, :].rearrange("p g t h -> p g (t h)")).then_inc(mi_loaded[x], 16)
            sp.dma_start(WR[:, :, :], a["w_router"][0].rearrange("(k p) e -> p k e", p=P)).then_inc(ld_wr, 16)
            sp.dma_start(BR[:, :], a["b_router"][0].partition_broadcast(P)).then_inc(ld_wr, 16)
            load_to(NU - 1)
            with sp.Fori(0, NE) as i:
                for n, (kind, c) in enumerate(eorder):
                    slot = (NU + n) % 3
                    sp.wait_ge(w_split, NU + n - 2 + i * EUNITS)
                    w = a[{"g": "w_exp_gate", "u": "w_exp_up", "d": "w_exp_down"}[kind]][0][bass.ds(i, 1)]
                    w = w.rearrange("e k n -> (e k) n")
                    if kind == "d":
                        src = w[c * FC:(c + 1) * FC, :]
                    else:
                        src = w[:, c * FC:(c + 1) * FC]
                    nk = 2 if kind == "d" else 8
                    sp.dma_start(raw[:, slot, :].rearrange("p (a n) -> p a n", a=nk),
                                 src.rearrange("(a p) n -> p a n", p=P)).then_inc(w_landed[slot], 16)


def constants():
    f = np.float32
    q, k = np.arange(P)[:, None], np.arange(CTX)[None, :]
    masks = [np.where(np.abs(q + P * t - k) <= 128, f(0), f(NEG)) for t in range(2)]
    rows, width = 256 // 64, 64
    row = np.repeat(np.arange(rows, dtype=f), width)
    col = np.tile(np.arange(width, dtype=f), rows)
    inv = (f(10000.0) ** (-np.arange(16, dtype=f) / f(16))).astype(f)
    ang = np.concatenate([row[:, None] * inv, col[:, None] * inv], axis=-1)
    cos, sin = (z.astype(f).reshape(2, P, 32).transpose(1, 0, 2).reshape(P, 64) for z in (np.cos(ang), np.sin(ang)))
    iota = np.broadcast_to(np.arange(NE, dtype=f) - NE, (P, NE))
    out = np.concatenate([np.eye(P, dtype=f), *masks, cos, sin, iota, np.zeros((P, 120), f)], axis=1)
    return np.ascontiguousarray(out.astype(f))


_INS = ['x', 'c', 'ctx', 'c_ctx', 'w_mod', 'b_mod', 'norm_g', 'w_in', 'attn_sink', 'ssm_a_re', 'ssm_a_im',
        'ssm_log_dt', 'ssm_b_re', 'ssm_b_im', 'ssm_c_re', 'ssm_c_im', 'ssm_d', 'w_glu', 'b_glu',
        'w_branch_attn', 'w_branch_ssm', 'w_out', 'w_ffn_gate', 'w_ffn_up', 'w_ffn_down',
        'w_router', 'b_router', 'w_exp_gate', 'w_exp_up', 'w_exp_down']


def kernel(**inputs):
    import concourse.bacc as bacc
    from concourse.bass_utils import run_bass_kernel_spmd

    nc = bacc.Bacc("TRN2", target_bir_lowering=False, num_devices=1)
    arrays, a = {}, {}
    for name in _INS:
        v = np.ascontiguousarray(inputs[name])
        arrays[f"in_{name}"] = v
        a[name] = nc.dram_tensor(f"in_{name}", v.shape, mybir.dt.from_np(v.dtype), kind="ExternalInput").ap()
    table = constants()
    arrays["in_consts"] = table
    consts = nc.dram_tensor("in_consts", table.shape, F, kind="ExternalInput").ap()
    out = nc.dram_tensor("out_x", (1, 256, D), F, kind="ExternalOutput").ap()
    build_program(nc, a, consts, out)
    r = run_bass_kernel_spmd(nc, [arrays], core_ids=[0])
    return r.results[0]["out_x"]
```

```python
from contextlib import ExitStack

import numpy as np

import concourse.bass as bass
from concourse import mybir

F = mybir.dt.float32
R = mybir.dt.float32r
I32 = mybir.dt.int32
ACT = mybir.ActivationFunctionType
ALU = mybir.AluOpType
AX = mybir.AxisListType.X

P = 128
L = 2
D = 1024
KT = D // P
N = 512
TT = N // P
CTX = 256
HD = 64
NH = 8
NKV = 2
QPK = NH // NKV
DS = 512
G = 32
H = 16
T = 8
C = N // T
DFF = 2816
DFE = 3584
NE = 8
FC = 256
EPS = 1e-6
NEG = -(2.0 ** 103)
MM3 = ((0, 0), (0, 1), (1, 0))
TWO_PI = 6.283185307179586
PREP_PARTS = 13
PREP_SIN = 5
PREP0, PREP1 = 8, 6
PREP_STEP = 2
PREP_EARLY = 8
PI_PARTS = (6.28125, 0.0019353071693331003, 1.0253131677018246e-11)
ROUND = 12582912.0
LN2 = (0.693359375, -2.1219444005469057e-4)
INV_LN2 = 1.4426950408889634


def toks(l):
    return [0, 1, 2, 3] if l == 0 else [2, 3]


class Banks:

    def __init__(self, full, free, w_used):
        self.full, self.free, self.w_used = full, free, w_used
        self.uses, self.fulls = [0] * 8, [0] * 8
        self.filled, self.emptied = {}, {}

    def begin(self, pe, key, bank, i=None, per=0):
        if self.uses[bank] > 0:
            pe.wait_ge(self.free[bank], self.uses[bank] if i is None else self.uses[bank] + i * per)
        self.uses[bank] += 1
        assert key not in self.emptied, key
        self.emptied[key] = (self.free[bank], self.uses[bank], per, bank)

    def end(self, ins, key, per=0):
        bank = self.emptied[key][3]
        self.fulls[bank] += 1
        ins.then_inc(self.full[bank], 1)
        self.filled[key] = (self.full[bank], self.fulls[bank], per)

    def end_unit(self, ins, key, unit, per=0):
        ins.then_inc(self.w_used, 1)
        self.filled[key] = (self.w_used, unit + 1, per)

    def wait(self, eng, key, i=None, turns_back=0):
        sem, count, per = self.filled[key]
        count -= turns_back * per
        eng.wait_ge(sem, count if i is None else count + i * per)

    def release(self, ins, key):
        ins.then_inc(self.emptied[key][0], 1)

    def released(self, eng, key, i=None, turns_back=0):
        sem, count, per, _ = self.emptied[key]
        count -= turns_back * per
        eng.wait_ge(sem, count if i is None else count + i * per)


class Chain:

    def __init__(self, eng, sem):
        self.eng, self.sem, self.n = eng, sem, 0

    def __call__(self, ins):
        ins.then_inc(self.sem, 1)
        self.n += 1
        self.eng.wait_ge(self.sem, self.n)


def weight_units(a):
    units = []

    def rows(key, w, k0, nk, c0, nc):
        units.append((key, w[k0 * P:(k0 + nk) * P, c0:c0 + nc].rearrange("(a p) n -> p a n", p=P), nk, nc))

    for l in range(L):
        for nb in range(12):
            for hf in range(2):
                rows(("mod", l, nb, hf), a["w_mod"][l], 4 * hf, 4, nb * 512, 512)
    for l in range(L):
        w = a["w_in"][l]
        rows(("kv", l), w, 0, 8, 512, 256)
        for hf in range(2):
            rows(("u", l, hf), w, 4 * hf, 4, 768, 512)
        for hf in range(2):
            rows(("q", l, hf), w, 4 * hf, 4, 0, 512)
        for i in range(8):
            rows(("gate", l, i), w, 0, 8, 1280 + 256 * i, 256)
        rows(("glu", l), a["w_glu"][l], 0, 4, 0, 512)
        for nb in range(2):
            rows(("pa", l, nb), a["w_branch_attn"][l], 0, 4, nb * 512, 512)
            rows(("pb", l, nb), a["w_branch_ssm"][l], 0, 4, nb * 512, 512)
        for nb in range(2):
            for hf in range(2):
                rows(("out", l, nb, hf), a["w_out"][l], 4 * hf, 4, nb * 512, 512)
        if l == 0:
            for kind, c in ffn_order(DFF // FC):
                w = a[{"g": "w_ffn_gate", "u": "w_ffn_up", "d": "w_ffn_down"}[kind]][0]
                if kind == "d":
                    rows(("d", c), w, 2 * c, 2, 0, D)
                else:
                    rows((kind, c), w, 0, 8, c * FC, FC)
    return units


def ffn_order(chunks):
    out = []
    for c in range(chunks + 1):
        if c < chunks:
            out += [("g", c), ("u", c)]
        if c > 0:
            out.append(("d", c - 1))
    return out


EC = 512
NEC = DFE // EC
MAXB = 11
MOE_USES = (1, 1, 7, 5, 4, 4, 4, 4)
MOE_FULLS = (1, 0, 7, 5, 0, 1, 0, 1)


def moe_order():
    out = []
    for c in range(NEC + 1):
        if c < NEC:
            out += [(kind, c, h) for kind in "gu" for h in range(2)]
        if c > 0:
            out += [("d", c - 1, h) for h in range(2)]
    return out


def build_program(nc, a, consts, out):
    units = weight_units(a)
    U = {u[0]: n for n, u in enumerate(units)}
    NU = len(units)
    eorder = moe_order()
    EUNITS = len(eorder)
    EU = {kc: n for n, kc in enumerate(eorder)}

    ctx = ExitStack()
    with ctx:
        cursor = [16512]

        def region(size):
            at = cursor[0]
            cursor[0] += size
            return at

        def sb(name, shape, dt, at):
            return nc.alloc_sbuf_tensor_at(name, shape, dt, offset=at)

        r_raw, r_split = region(3 * 8192), region(3 * 16384)
        r_x, r_ht, r_ot = region(16384), region(32768), region(16384)
        r_gb, r_qk, r_qs = region(8192), region(12288), region(10240)
        r_uy, r_small, r_ring = region(8192), region(15104), region(10240)
        r_const = region(0)

        raw = sb("raw", [P, 3, 2048], F, r_raw)
        split = sb("split", [P, 3, 2, 2048], R, r_split)
        X = sb("X", [P, TT, D], F, r_x)
        S = sb("ssm_state", [P, 2, G, C], F, r_x)
        STR = sb("ssm_out", [P, 2, 4, N], R, r_x)
        HT = sb("HT", [P, 2, KT, N], R, r_ht)
        XC = sb("block_in", [P, 2, KT, P], R, r_ht)
        XM = sb("block_in_f", [P, KT, P], F, r_ht + 8192)
        HB = sb("block_hidden", [P, 2, 2, 4, P], R, r_ht + 12288)
        YE = sb("block_out", [P, D], F, r_ht + 20480)
        SB = sb("block_silu", [P, 2, EC], F, r_ht + 24576)
        HE = sb("block_hidden_f", [P, 2, EC], F, r_ht + 28672)
        BM = sb("b_mod_rows", [2, L, 6 * D], F, r_ht)
        Hm = sb("read_mats", [P, 3, 2, 4, P], F, r_ht)
        KB = sb("lag_blocks", [H, 3, 4, 15, H], F, r_ht + 12288)
        MI = sb("chunk_mats", [P, 3, 4, P], F, r_ht + 12288 + 11520)
        REV = sb("reversal", [P, 2, G, 16], F, r_ht + 12288)
        GTR = sb("glu_in", [P, 2, 4, N], R, r_ht)
        OT = sb("attn_out", [P, 2, 4, N], R, r_ot)
        YA = sb("YA", [P, TT, D], F, r_ot)
        GB = sb("gate_rows", [P, 2, D], F, r_gb)
        UC = sb("chunked_u", [P, G, C], F, r_gb)
        qT = sb("qT", [P, TT, 4, P], F, r_qk)
        kT = sb("kT", [P, N], F, r_qk + 8192)
        V = sb("V", [P, TT, P], F, r_qk + 10240)
        QS = sb("q_tok", [P, TT, 512], F, r_qs)
        KS = sb("k_tok", [P, TT, P], F, r_qs + 8192)
        PR = sb("probs", [P, 2, 512], F, r_qs)
        PT = sb("probsT", [P, 2, 4, P], F, r_qs + 4096)
        YK = sb("y_tok", [P, TT, 512], F, r_qs)
        NG = sb("norm_rows", [2, L, 2, D], F, r_qk)
        SGA = sb("sig_a", [P, 2, 512], F, r_qk)
        SGB = sb("sig_b", [P, 2, 512], F, r_qk + 4096)
        HC = sb("hidden", [P, 2, 2, 2, 512], R, r_qk)
        UU = sb("u_chunks", [P, T, 256], F, r_uy)
        YY = sb("y_chunks", [P, T, 256], F, r_uy)
        GF = sb("gelu", [P, 4, 512], F, r_uy)
        MT1 = sb("merge_a", [P, 4, 512], F, r_uy)
        TAB = sb("moe_consts", [P, 2, P], F, r_qk)
        ONES = sb("ones", [P, P], F, r_qk + 1024)
        PICK = sb("pick", [P, 2, P], F, r_qk + 1536)
        PICKG = sb("pick_gated", [P, 2, P], F, r_qk + 2560)
        PUT = sb("put", [P, 2, P], F, r_qk + 3584)
        SLOT = sb("slot_of", [P, 2, MAXB + 1], F, r_qk + 4608)
        GATE = sb("gate_of", [P, 2, MAXB + 1], F, r_qk + 4704)
        SEL = sb("selected", [P, 2, NE], F, r_qk + 4800)
        OV = sb("overflow", [P, 4, NE], F, r_qk + 4864)
        PLAN = sb("plan_f", [P, 16], F, r_qk + 4992)
        PLANI = sb("plan", [P, 16], I32, r_qk + 5056)
        MS = sb("mod_stage", [2, 2, 512], F, r_qk + 16384)
        UP = sb("u_grouped", [P, H, T, H], F, r_ot)
        HTF = sb("HT_f32", [P, KT, CTX], F, r_uy)
        SIL = sb("silu", [P, 2, 512], F, r_uy)
        HF = sb("hidden_f", [P, 2, 512], F, r_uy + 4096)
        PW = sb("powers", [P, 2, T + 1, G], F, r_small)
        BB = sb("b_bar", [P, 2, G, H], F, r_small + 2304)
        CC = sb("c_mat", [P, 2, G, H], F, r_small + 2304 + 4096)
        A8 = sb("a_chunk", [P, 2, 2, G], F, r_small + 2304 + 8192)
        PG = sb("powers_in_out", [P, 2, 2, T, G], F, r_small + 11008)
        BT = sb("b_bar_tmp", [P, 2, 512], F, r_small + 11008)
        GP = [sb(f"in_mats_pre{i}", [P, 2, 4, P], F, (r_qs + 4096, r_uy)[i]) for i in range(2)]
        GT = [sb(f"in_mats_t{i}", [P, 2, 4, P], F, (r_qs, r_uy + 4096)[i]) for i in range(2)]
        DR = sb("ssm_skip", [H, G, H], F, r_qs + 8192)
        ZS = sb("zoh", [P, 16, G], F, r_ring + 8192)
        TM = sb("tmp", [P, 512], F, r_ring + 8192)
        CW = sb("cond_cols", [P, 2, KT, P], R, r_ring)
        STG = sb("stage", [P, 2, 512], F, r_ring)
        JUNK = sb("junk", [P, 2, D], F, r_ring)
        JUNK0 = sb("junk_first", [P, 2, D], F, r_gb)
        TN = sb("norm_tmp", [P, 2, 512], F, r_ring + 4096)
        SGT = sb("glu_sig", [P, 2, 512], F, r_ring)
        SF = sb("ssm_out_f", [P, 2, 512], F, r_ring + 4096)
        CI_ = [sb(f"c_rows{l}", [P, 2, 4, 2, 64], F, (r_uy, r_ring)[l]) for l in range(L)]
        BI_ = [sb(f"b_rows{l}", [P, 2, G, H], F, (r_uy, r_ring)[l] + 4096) for l in range(L)]

        cur = [r_const]

        def small(name, shape, dt=F):
            size = 4 * int(np.prod(shape[1:]))
            t = sb(name, shape, dt, cur[0])
            cur[0] += (size + 31) // 32 * 32
            return t

        CT = small("consts", [P, 768 + 128])
        EYE = CT[:, 0:128]
        MASK = [CT[:, 128:384], CT[:, 384:640]]
        COS = CT[:, 640:704].rearrange("p (t d) -> p t d", t=2)
        SIN = CT[:, 704:768].rearrange("p (t d) -> p t d", t=2)
        IOTA8 = CT[:, 768:776]
        CR = small("col_rows", [100, P])
        CV = small("cond_rows", [16, P])
        CF = small("cond_f", [P, 16])
        COLS = small("cols", [P, 100])
        AF = small("norm_gain", [P, 2, 2, KT])
        SS = small("sumsq", [P, TT])
        RS = small("rstd", [P, TT])
        SK = small("sink", [P, NH])
        ST = small("softmax_stats", [P, 2, 8])
        DTR = small("ssm_dt", [P, G])
        ARI = small("ssm_a_rows", [G, 2, P])
        ZI = small("zoh_int", [P, G], I32)
        RT = small("recur_tmp", [P, 2, 2, G])
        WR = small("router", [P, KT, NE])
        LG = small("logits", [P, 2, NE])
        TV = small("top_v", [P, 2, 8])
        TI = small("top_i", [P, 2, 8], mybir.dt.uint32)
        TF = small("top_f", [P, 2, 8])
        GA = small("gates", [P, 2, NE])
        RW = small("gate_tmp", [P, 2, 8])
        BR = small("router_bias", [P, NE])
        LT = small("sink_exp", [P, 2, 8])
        assert cur[0] <= 229344, cur[0]

        banks_t = [ctx.enter_context(nc.psum_tensor(f"bank{i}", [P, 512], F)) for i in range(8)]

        modrow = nc.dram_tensor("mod_rows", [L, 2, 6 * D], F).ap()
        uscr = nc.dram_tensor("u_scratch", [L, N, DS], F).ap()
        yscr = nc.dram_tensor("y_scratch", [L, N, DS], F).ap()
        gscr = nc.dram_tensor("gate_scratch", [L, 16, P, N], F).ap()
        xscr = nc.dram_tensor("x_scratch", [N, D], F).ap()

        def sem(name):
            return ctx.enter_context(nc.semaphore(name))

        full = [sem(f"bank_full{i}") for i in range(8)]
        free = [sem(f"bank_free{i}") for i in range(8)]
        
        w_landed = [sem(f"w_landed{i}") for i in range(3)]
        w_round, w_split, w_used = sem("w_rounded"), sem("w_split"), sem("w_used")
        banks = Banks(full, free, w_used)
        dve_step, act_step, pool_step = sem("dve_step"), sem("act_step"), sem("pool_step")
        ld_const, ld_cond, ld_bm = sem("ld_const"), sem("ld_cond"), sem("ld_bm")
        cond_zero, cond_hi, cond_ready = sem("cond_zero"), sem("cond_hi"), sem("cond_ready")
        mod_row, mod_stored = sem("mod_row"), [sem(f"mod_stored{i}") for i in range(2)]
        ld_cols, ld_x, ld_gb = sem("ld_cols"), sem("ld_x"), sem("ld_gb")
        sq_done, ms_ready, rt_done = sem("sq_done"), sem("ms_ready"), sem("rt_done")
        xn_ready, ht_hi, ht_ready = sem("xn_ready"), sem("ht_hi"), sem("ht_ready")
        q_tok, k_tok, v_ready = sem("q_tok"), sem("k_tok"), sem("v_ready")
        u_stored, ld_u, u_grouped = [sem(f"u_stored{i}") for i in range(2)], sem("ld_u"), sem("u_grouped")
        g_stored = [sem(f"gate_stored{i}") for i in range(2)]
        ld_g = [sem(f"ld_gates{i}") for i in range(2)]
        row_max, sink_done, p_norm = sem("row_max"), sem("sink_done"), sem("probs_norm")
        o_hi = sem("o_hi")
        ld_ssm, ld_skip, ang_ready, sin_done = sem("ld_ssm"), sem("ld_skip"), sem("ang_ready"), sem("sin_done")
        prep_done, gp_ready, v_fwd = sem("prep_done"), sem("in_pre"), sem("v_fwd")
        rec_done = sem("recurrence")
        h_ready, kb_copied, mi_loaded = sem("read_mats"), sem("kb_copied"), [sem(f"mi_loaded{i}") for i in range(3)]
        y_stored, ld_y, g_hi, g_ready = sem("y_stored"), sem("ld_y"), sem("g_hi"), sem("g_ready")
        s_f, s_hi, s_ready = sem("s_f"), sem("s_hi"), sem("s_ready")
        m_f, m_hi, m_ready = sem("m_f"), sem("m_hi"), sem("m_ready")
        x_new, x_stored = sem("x_new"), sem("x_stored")
        hc_hi, hc_ready = sem("hidden_hi"), sem("hidden_ready")
        ld_wr, top_diff, top_exp, out_stored = sem("ld_router"), sem("top_diff"), sem("top_exp"), sem("out_stored")
        ld_tab, sel_ready, plan_ready = sem("ld_moe_consts"), sem("selected"), sem("plan_ready")
        pick_ready, gated_ready = sem("pick_ready"), sem("gated_ready")
        xc_hi, xc_ready = sem("xc_hi"), sem("xc_ready")
        he_hi = sem("he_hi")
        LD_SSM = 14 * 16

        def mi_count(l, q):
            return 16 * T * (l * len(range(q % 3, 8, 3)) + q // 3 + 1)

        xn_ready_at = {(0, 0): 4, (0, 1): 8, (1, 0): 12, (1, 1): 14}
        ht_ready_at = {(0, 0): 8, (0, 1): 16, (1, 0): 24, (1, 1): 32}
        att_items = lambda l: [(t, h) for t in toks(l) for h in range(NH)]
        att_base = [0, 4 * NH]
        norm_at = {(0, 0): 0, (0, "r0"): 4, (0, 1): 8, (0, "r1"): 12, (1, 0): 16, (1, "r0"): 20, (1, 1): 22, (1, "r1"): 24}
        x_new_at = {(0, 0): 4, (0, 1): 8, (1, 0): 10, (1, 1): 12}
        ld_x_at = {(0, 0): 32, (0, 1): 64, (0, 2): 64, (1, 0): 64, (1, 1): 80, (1, 2): 80}
        ld_sink = sem("ld_sink")
        pool_n = [0]
        

        block = ctx.enter_context(nc.Block())

        def unit_view(slot, part, nk, ncol):
            return split[:, slot, part, :].rearrange("p (a n) -> p a n", a=nk)

        @block.tensor
        def _(pe):
            def unit(key):
                n = U[key]
                pe.wait_ge(w_split, n + 1)
                nk = units[n][2]
                return [unit_view(n % 3, q, nk, units[n][3]) for q in range(2)]

            def mm3(outp, lhs, rhs, start, stop):
                for j, (x, w) in enumerate(MM3):
                    ins = nc.tensor.matmul(outp, lhs(x, w), rhs(x, w), start=start and j == 0, stop=stop and j == 2)
                return ins

            def bank(i):
                return banks_t[i]

            def ssm_prep(l):
                pe.wait_ge(ld_ssm, LD_SSM * (l + 1))
                for r in range(2):
                    banks.begin(pe, ("arow", l, r), 6 + r)
                    banks.end(nc.tensor.transpose(bank(6 + r)[:, 0:G], ARI[:, r, :], EYE[0:G, 0:G]), ("arow", l, r))
                for r in range(2):
                    banks.begin(pe, ("crow", l, r), 4 + r)
                    for b in range(4):
                        ins = nc.tensor.transpose(bank(4 + r)[:, b * P:(b + 1) * P],
                                                  CI_[l][:, r, b, :, :].rearrange("p a b -> p (a b)"), EYE)
                    banks.end(ins, ("crow", l, r))

            pe.wait_ge(ld_const, 16)
            pe.wait_ge(ld_cond, 32)
            banks.begin(pe, "cond", 6)
            banks.end(nc.tensor.transpose(bank(6)[:, 0:16], CV[:, :], EYE[0:16, 0:16]), "cond")
            pe.wait_ge(cond_ready, 1)
            for l in range(L):
                for nb in range(12):
                    if (l, nb) == (0, PREP0 - 1):
                        ssm_prep(0)
                    key = ("mod", l, nb)
                    for hf in range(2):
                        w = unit(("mod", l, nb, hf))
                        if hf == 0:
                            banks.begin(pe, key, nb % 4)
                        for k in range(4):
                            ins = mm3(bank(nb % 4)[:, :], lambda x, q: CW[:, x, 4 * hf + k, :],
                                      lambda x, q: w[q][:, k, :], hf == 0 and k == 0, hf == 1 and k == 3)
                        if hf == 1:
                            banks.end_unit(ins, key, U[("mod", l, nb, hf)])
                        else:
                            ins.then_inc(w_used, 1)

            def columns(l):
                pe.wait_ge(ld_cols, 96 * (l + 1))
                banks.begin(pe, ("cols", l), 7)
                banks.end(nc.tensor.transpose(bank(7)[:, 0:100], CR[:, :], EYE[0:100, 0:100]), ("cols", l))

            def norm(l, n, tiles):
                pe.wait_ge(xn_ready, xn_ready_at[(l, n)])
                for k in range(KT):
                    key = ("norm", l, n, k)
                    b = 6 + k % 2
                    banks.begin(pe, key, b)
                    for t in tiles:
                        ins = nc.tensor.transpose(bank(b)[:, t * P:(t + 1) * P], YA[:, t, k * P:(k + 1) * P], EYE)
                    banks.end(ins, key)

            def tok_major(name, l, tiles, keys, width, src):
                n = len(keys)
                for i, ukey in enumerate(keys):
                    w = unit(ukey)
                    nk = units[U[ukey]][2]
                    for t in tiles:
                        key = (name, l, t)
                        if i == 0:
                            banks.begin(pe, key, t)
                        for k in range(nk):
                            kk = i * nk + k
                            ins = mm3(bank(t)[:, 0:width], lambda x, q: src[:, x, kk, t * P:(t + 1) * P],
                                      lambda x, q: w[q][:, k, :], kk == 0, i == n - 1 and k == nk - 1)
                        if i == n - 1 and t == tiles[-1]:
                            banks.end_unit(ins, key, U[ukey])
                        elif i == n - 1:
                            banks.end(ins, key)
                        elif t == tiles[-1]:
                            ins.then_inc(w_used, 1)

            def inproj(l):
                pe.wait_ge(ht_ready, ht_ready_at[(l, 0)])
                tok_major("kv", l, range(4), [("kv", l)], 256, HT)
                tok_major("u", l, range(4), [("u", l, 0), ("u", l, 1)], 512, HT)
                tok_major("q", l, toks(l), [("q", l, 0), ("q", l, 1)], 512, HT)
                for t in range(2):
                    banks.released(pe, ("kv", l, t))
                pe.wait_ge(k_tok, 2 * (l + 1))
                banks.begin(pe, ("kT", l), 7)
                for t in range(4):
                    ins = nc.tensor.transpose(bank(7)[:, t * P:(t + 1) * P], KS[:, t, :], EYE)
                banks.end(ins, ("kT", l))
                for t in toks(l):
                    if t < 2:
                        banks.released(pe, ("q", l, t))
                    else:
                        pe.wait_ge(q_tok, 2 * l + t - 1)
                    b = 6 + t % 2
                    banks.begin(pe, ("qT", l, t), b)
                    for j in range(4):
                        ins = nc.tensor.transpose(bank(b)[:, j * P:(j + 1) * P], QS[:, t, j * P:(j + 1) * P], EYE)
                    banks.end(ins, ("qT", l, t))

            def gates(l):
                c0 = 0 if l == 0 else CTX
                for i in range(8):
                    w = unit(("gate", l, i))
                    for f in range(2):
                        key = ("gate", l, i, f)
                        banks.begin(pe, key, 4 + f)
                        for k in range(KT):
                            ins = mm3(bank(4 + f)[:, 0:N - c0], lambda x, q: w[q][:, k, f * P:(f + 1) * P],
                                      lambda x, q: HT[:, x, k, c0:N], k == 0, k == KT - 1)
                        if f == 0:
                            banks.end(ins, key)
                        else:
                            banks.end_unit(ins, key, U[("gate", l, i)])

            def attention(l):
                banks.released(pe, ("kT", l))
                items = att_items(l)

                def scores(i):
                    t, h = items[i]
                    g, j = h // QPK, h % QPK
                    key, b = ("sc", l, i), 4 + i % 2
                    if h == 0:
                        banks.released(pe, ("qT", l, t))
                    banks.begin(pe, key, b)
                    lat = t >= 2
                    w = N if lat else CTX
                    if lat:
                        nc.tensor.matmul(bank(b)[:, CTX:N], EYE, MASK[t - 2], start=True, stop=False,
                                         skip_group_check=True)
                        nc.tensor.matmul(bank(b)[:, CTX:N], qT[g * HD:(g + 1) * HD, t, j, :],
                                         kT[g * HD:(g + 1) * HD, CTX:N], start=False, stop=True, skip_group_check=True)
                        ins = nc.tensor.matmul(bank(b)[:, 0:CTX], qT[g * HD:(g + 1) * HD, t, j, :],
                                               kT[g * HD:(g + 1) * HD, 0:CTX], start=False, stop=True,
                                               skip_group_check=True)
                    else:
                        ins = nc.tensor.matmul(bank(b)[:, 0:w], qT[g * HD:(g + 1) * HD, t, j, :],
                                               kT[g * HD:(g + 1) * HD, 0:w], start=True, stop=True)
                    banks.end(ins, key)

                def turn(i):
                    t, h = items[i]
                    key, b = ("pt", l, i), 6 + i % 2
                    pe.wait_ge(p_norm, att_base[l] + i + 1)
                    banks.begin(pe, key, b)
                    for kb in range(4 if t >= 2 else 2):
                        ins = nc.tensor.transpose(bank(b)[:, kb * P:(kb + 1) * P], PR[:, i % 2, kb * P:(kb + 1) * P], EYE)
                    banks.end(ins, key)

                def pv(i):
                    t, h = items[i]
                    g = h // QPK
                    key, b = ("o", l, t), t % 2
                    banks.released(pe, ("pt", l, i))
                    if h == 0:
                        banks.begin(pe, key, b)
                    nkb = 4 if t >= 2 else 2
                    r = (h % 2) * HD
                    for kb in range(nkb):
                        ins = nc.tensor.matmul(bank(b)[r:r + HD, (h // 2) * P:(h // 2 + 1) * P],
                                               V[:, kb, g * HD:(g + 1) * HD], PT[:, i % 2, kb, :],
                                               start=kb == 0, stop=kb == nkb - 1)
                    if h == NH - 1:
                        banks.end(ins, key)

                n = len(items)
                for i in range(n + 3):
                    if i < n:
                        scores(i)
                    if 2 <= i < n + 2:
                        turn(i - 2)
                    if i >= 3:
                        pv(i - 3)

            def ssm_in(l):
                pe.wait_ge(u_grouped, 2 * (l + 1))
                for q in range(4):
                    b = 6 + q % 2
                    s = q // 2
                    banks.begin(pe, ("uc", l, q), b)
                    for g in range(8):
                        gl = (8 * q + g) % 16
                        ins = nc.tensor.transpose(bank(b)[:, g * C:(g + 1) * C],
                                                  UP[s * C:(s + 1) * C, gl, :, :].rearrange("p t h -> p (t h)"),
                                                  EYE[s * C:(s + 1) * C, s * C:(s + 1) * C])
                    banks.end(ins, ("uc", l, q))
                for q in range(4):
                    banks.released(pe, ("uc", l, q))
                for q in range(9):
                    if q < 8:
                        pe.wait_ge(gp_ready, 8 * l + q + 1)
                        for r in range(2):
                            banks.begin(pe, ("gt", l, q, r), 4 + r)
                            for g in range(4):
                                ins = nc.tensor.transpose(bank(4 + r)[:, g * P:(g + 1) * P], GP[q % 2][:, r, g, :], EYE)
                            banks.end(ins, ("gt", l, q, r))
                    if q >= 1:
                        p = q - 1
                        for r in range(2):
                            banks.released(pe, ("gt", l, p, r))
                        b = p % 2
                        banks.begin(pe, ("v", l, p), b)
                        for r in range(2):
                            for g in range(4):
                                ins = nc.tensor.matmul(bank(b)[:, (r * 4 + g) * C:(r * 4 + g + 1) * C],
                                                       GT[p % 2][:, r, g, :], UC[:, 4 * p + g, :], start=True, stop=True)
                        banks.end(ins, ("v", l, p))

            def ssm_out(l):
                c0 = 0 if l == 0 else C // 2
                for q in range(10):
                    if q < 8:
                        pe.wait_ge(h_ready, 8 * l + q + 1)
                        x = q % 3
                        for side in range(2):
                            banks.begin(pe, ("kb", l, q, side), 2 + side)
                            h = slice(64 * side, 64 * side + 64)
                            lags = slice(0, 112) if side == 0 else slice(16, 128)
                            for g in range(4):
                                gi = 4 * q + g
                                for r in range(2):
                                    ins = nc.tensor.matmul(bank(2 + side)[0:H, g * 112:(g + 1) * 112], BB[h, r, gi, :],
                                                           Hm[h, x, r, g, lags], start=r == 0, stop=r == 1,
                                                           skip_group_check=True)
                            if side == 1:
                                banks.end(ins, ("kb", l, q, 1))
                        for g in range(4):
                            gi = 4 * q + g
                            for r in range(2):
                                ins = nc.tensor.matmul(bank(2)[0:H, 448 + g * H:448 + (g + 1) * H], BB[:, r, gi, :],
                                                       CC[:, r, gi, :], start=r == 0, stop=r == 1, skip_group_check=True)
                        banks.end(ins, ("kb", l, q, 0))
                    if q == 1:
                        pe.wait_ge(rec_done, l + 1)
                    if q >= 2:
                        p = q - 2
                        x = p % 3
                        s = p // 4
                        pe.wait_ge(mi_loaded[x], mi_count(l, p))
                        b = p % 2
                        banks.begin(pe, ("y", l, p), b)
                        rows = slice(s * 64, s * 64 + C - c0)
                        for g in range(4):
                            gi = 4 * p + g
                            o = bank(b)[rows, g * P:(g + 1) * P]
                            nc.tensor.matmul(o, UC[:, gi, c0:C], MI[:, x, g, :], start=True, stop=False)
                            nc.tensor.matmul(o, S[:, 0, gi, c0:C], Hm[:, x, 0, g, :], start=False, stop=False)
                            ins = nc.tensor.matmul(o, S[:, 1, gi, c0:C], Hm[:, x, 1, g, :], start=False, stop=True)
                        banks.end(ins, ("y", l, p))

            def glu(l):
                c0 = 0 if l == 0 else CTX
                pe.wait_ge(ld_y, 16 * (l + 1))
                for f in range(4):
                    b = 6 + f % 2
                    banks.begin(pe, ("yT", l, f), b)
                    for t in toks(l):
                        ins = nc.tensor.transpose(bank(b)[:, t * P:(t + 1) * P], YK[:, t, f * P:(f + 1) * P], EYE)
                    banks.end(ins, ("yT", l, f))
                pe.wait_ge(g_ready, 4 * (l + 1))
                w = unit(("glu", l))
                for f in range(4):
                    key = ("glu", l, f)
                    banks.begin(pe, key, f)
                    for k in range(4):
                        ins = mm3(bank(f)[:, c0:N], lambda x, q: w[q][:, k, f * P:(f + 1) * P],
                                  lambda x, q: GTR[:, x, k, c0:N], k == 0, k == 3)
                    if f < 3:
                        banks.end(ins, key)
                    else:
                        banks.end_unit(ins, key, U[("glu", l)])

            def merge(l):
                c0 = 0 if l == 0 else CTX
                for t in toks(l):
                    banks.released(pe, ("o", l, t))
                for nb in range(2):
                    for name, src in (("pa", OT), ("pb", STR)):
                        w = unit((name, l, nb))
                        if name == "pb" and nb == 0:
                            pe.wait_ge(s_ready, 4 * (l + 1))
                        for f in range(4):
                            key = (name, l, nb, f)
                            b = f if name == "pa" else 4 + f
                            banks.begin(pe, key, b)
                            for k in range(4):
                                ins = mm3(bank(b)[:, c0:N], lambda x, q: w[q][:, k, f * P:(f + 1) * P],
                                          lambda x, q: src[:, x, k, c0:N], k == 0, k == 3)
                            if f < 3:
                                banks.end(ins, key)
                            else:
                                banks.end_unit(ins, key, U[(name, l, nb)])
                pe.wait_ge(m_ready, 8 * (l + 1))
                for nb in range(2):
                    for hf in range(2):
                        w = unit(("out", l, nb, hf))
                        for t in toks(l):
                            key = ("out", l, nb, t)
                            if hf == 0:
                                banks.begin(pe, key, t)
                            for k in range(4):
                                ins = mm3(bank(t)[:, :], lambda x, q: HT[:, x, 4 * hf + k, t * P:(t + 1) * P],
                                          lambda x, q: w[q][:, k, :], hf == 0 and k == 0, hf == 1 and k == 3)
                            if hf == 1 and t == 3:
                                banks.end_unit(ins, key, U[("out", l, nb, hf)])
                            elif hf == 1:
                                banks.end(ins, key)
                            elif t == 3:
                                ins.then_inc(w_used, 1)

            def ffn():
                base = U[("g", 0)]
                for n, (kind, c) in enumerate(ffn_order(DFF // FC)):
                    if n == PREP1:
                        ssm_prep(1)
                    w = unit((kind, c))
                    if kind in "gu":
                        for f in range(2):
                            b = (4 if kind == "g" else 6) + f
                            key = ("f" + kind, c, f)
                            banks.begin(pe, key, b)
                            for k in range(KT):
                                ins = mm3(bank(b)[:, :], lambda x, q: w[q][:, k, f * P:(f + 1) * P],
                                          lambda x, q: HT[:, x, k, :], k == 0, k == KT - 1)
                            if f == 0:
                                banks.end(ins, key)
                            else:
                                banks.end_unit(ins, key, base + n)
                    else:
                        pe.wait_ge(hc_ready, 2 * (c + 1))
                        for t in range(TT):
                            for nb in range(2):
                                key = ("fd", c, t, nb)
                                b = (2 * t + nb) % 4
                                banks.begin(pe, key, b)
                                for f in range(2):
                                    ins = mm3(bank(b)[:, :], lambda x, q: HC[:, c % 2, x, f, t * P:(t + 1) * P],
                                              lambda x, q: w[q][:, f, nb * 512:(nb + 1) * 512], f == 0, f == 1)
                                if (t, nb) == (3, 1):
                                    banks.end_unit(ins, key, base + n)
                                else:
                                    banks.end(ins, key)

            def gather(name, i=None):
                pe.wait_ge(pick_ready, 1 if i is None else i + 2)
                for half in range(2):
                    b = 3 - half
                    banks.begin(pe, (name, half), b, i, MOE_USES[b])
                    for k in range(4):
                        for t in range(2):
                            kk = 4 * half + k
                            ins = nc.tensor.matmul(bank(b)[:, k * P:(k + 1) * P], YA[:, 2 + t, kk * P:(kk + 1) * P],
                                                   PICK[:, t, :], start=t == 0, stop=t == 1)
                    banks.end(ins, (name, half), 0 if i is None else MOE_FULLS[b])

            def scatter(name, i, done):
                for nb in range(2):
                    banks.released(pe, ("ye0", nb), done)
                for t in range(2):
                    for nb in range(2):
                        b = (5, 7, 2, 3)[2 * t + nb]
                        banks.begin(pe, (name, t, nb), b, i, MOE_USES[b])
                        ins = nc.tensor.matmul(bank(b)[:, :], PUT[:, t, :], YE[:, nb * 512:(nb + 1) * 512],
                                               start=True, stop=True)
                        banks.end(ins, (name, t, nb), MOE_FULLS[b])

            def block_turn(i):
                def eunit(kch):
                    n = NU + EU[kch]
                    pe.wait_ge(w_split, n + 1 + i * EUNITS)
                    nk = 2 if kch[0] == "d" else 4
                    return [unit_view(n % 3, q, nk, 2048 // nk) for q in range(2)]

                def product(kind, c):
                    b = (4 if kind == "g" else 6) + c % 2
                    banks.begin(pe, (kind + "e", c), b, i, MOE_USES[b])
                    for h in range(2):
                        w = eunit((kind, c, h))
                        for k in range(4):
                            ins = mm3(bank(b)[:, :], lambda x, q: XC[:, x, 4 * h + k, :],
                                      lambda x, q: w[q][:, k, :], h == 0 and k == 0, h == 1 and k == 3)
                        if h == 0:
                            ins.then_inc(w_used, 1)
                    banks.end_unit(ins, (kind + "e", c), NU + EU[(kind, c, 1)], EUNITS)

                def turn_hidden(c):
                    b = 2 + c % 2
                    banks.released(pe, ("ue", c), i)
                    banks.begin(pe, ("he", c), b, i, MOE_USES[b])
                    for k in range(4):
                        ins = nc.tensor.transpose(bank(b)[:, k * P:(k + 1) * P], HE[:, c % 2, k * P:(k + 1) * P], EYE)
                    banks.end(ins, ("he", c), MOE_FULLS[b])

                def down(c):
                    banks.released(pe, ("he", c), i)
                    for h in range(2):
                        w = eunit(("d", c, h))
                        if c == 0 and h == 0:
                            for nb in range(2):
                                banks.begin(pe, ("ye", nb), nb, i, MOE_USES[nb])
                        last = (c, h) == (NEC - 1, 1)
                        for nb in range(2):
                            for k in range(2):
                                ins = mm3(bank(nb)[:, :], lambda x, q: HB[:, c % 2, x, 2 * h + k, :],
                                          lambda x, q: w[q][:, k, nb * 512:(nb + 1) * 512],
                                          c == 0 and h == 0 and k == 0, last and k == 1)
                            if last and nb == 0:
                                banks.end(ins, ("ye", 0), MOE_FULLS[0])
                        if last:
                            banks.end_unit(ins, ("ye", 1), NU + EU[("d", c, h)], EUNITS)
                        else:
                            ins.then_inc(w_used, 1)

                pe.wait_ge(xc_ready, i + 1)
                for c in range(NEC):
                    product("g", c)
                    if c == 0:
                        scatter("back", i, i)
                    if c == 2:
                        pe.wait_ge(gated_ready, i + 1)
                        banks.begin(pe, "put", 2, i, MOE_USES[2])
                        for t in range(2):
                            ins = nc.tensor.transpose(bank(2)[:, t * P:(t + 1) * P], PICKG[:, t, :], EYE)
                        banks.end(ins, "put", MOE_FULLS[2])
                    if c > 0:
                        turn_hidden(c - 1)
                    product("u", c)
                    if c > 0:
                        down(c - 1)
                turn_hidden(NEC - 1)
                gather("ga", i)
                down(NEC - 1)

            def router():
                for k in range(KT):
                    banks.released(pe, ("norm", 1, 1, k))
                pe.wait_ge(ld_wr, 32)
                banks.begin(pe, "router", 0)
                for t in range(2):
                    for k in range(KT):
                        ins = nc.tensor.matmul(bank(0)[:, t * NE:(t + 1) * NE], HTF[:, k, t * P:(t + 1) * P],
                                               WR[:, k, :], start=k == 0, stop=k == KT - 1)
                banks.end(ins, "router")
                pe.wait_ge(sel_ready, 1)
                pe.wait_ge(ld_tab, 16)
                banks.begin(pe, "rank", 1)
                o = bank(1)[:, 0:3 * NE].rearrange("p (t e) -> p t e", t=3)
                nc.tensor.matmul(o[:, 0, :], TAB[:, 0, :], SEL[:, 0, :], start=True, stop=True)
                nc.tensor.matmul(o[:, 1, :], ONES[:, :], SEL[:, 0, :], start=True, stop=False)
                nc.tensor.matmul(o[:, 1, :], TAB[:, 0, :], SEL[:, 1, :], start=False, stop=True)
                nc.tensor.matmul(o[:, 2, :], ONES[:, :], SEL[:, 0, :], start=True, stop=False)
                ins = nc.tensor.matmul(o[:, 2, :], ONES[:, :], SEL[:, 1, :], start=False, stop=True)
                banks.end(ins, "rank")
                for nb in (1, 0):
                    banks.begin(pe, ("ye0", nb), nb, None, MOE_USES[nb])
                    ins = nc.tensor.matmul(bank(nb)[:, :], PUT[:, 0, :], YA[:, 2, nb * 512:(nb + 1) * 512],
                                           start=True, stop=True)
                banks.end(ins, ("ye0", 0), MOE_FULLS[0])
                gather("ga0")

            for l in range(L):
                columns(l)
                norm(l, 0, range(4))
                inproj(l)
                ssm_in(l)
                gates(l)
                attention(l)
                ssm_out(l)
                glu(l)
                merge(l)
                norm(l, 1, toks(l))
                if l == 0:
                    pe.wait_ge(ht_ready, ht_ready_at[(l, 1)])
                    ffn()
                else:
                    router()
                    pe.wait_ge(plan_ready, 1)
                    blocks = pe.value_load(PLANI[0:1, 0:1], min_val=NE, max_val=MAXB)
                    with pe.Fori(0, blocks) as i:
                        block_turn(i)
                    scatter("back_last", blocks - 1, blocks)

        @block.scalar
        def _(act):
            chain = Chain(act, act_step)
            rounded = [0]

            def round_to(n, i=None, past=0):
                last = NU + past if i is None else EUNITS + 3
                while rounded[0] <= min(n, last - 1):
                    u = rounded[0]
                    full_u = u if i is None else NU + u
                    slot = full_u % 3
                    if i is None:
                        act.wait_ge(w_landed[slot], 16 * (u // 3 + 1))
                        if u >= 3:
                            act.wait_ge(w_used, u - 2)
                    else:
                        act.wait_ge(w_landed[slot], 16 * (full_u // 3 + 1) + i * (16 * EUNITS // 3))
                        act.wait_ge(w_used, full_u - 2 + i * EUNITS)
                    nc.scalar.activation(split[:, slot, 0, :], raw[:, slot, :], ACT.Copy).then_inc(w_round, 1)
                    rounded[0] += 1

            banks.wait(act, "cond")
            banks.release(nc.scalar.activation(CF[:, :], banks_t[6][:, 0:16], ACT.Silu), "cond")
            banks.released(act, "cond")
            act.wait_ge(cond_zero, 1)
            nc.scalar.activation(CW[:, 0, :, 0:2], CF[:, :].rearrange("p (s k) -> p k s", s=2), ACT.Copy)\
                .then_inc(cond_hi, 1)

            def sines(l):
                act.wait_ge(ang_ready, l + 1)
                nc.scalar.activation(ZS[:, 7, :], ZS[:, 6, :], ACT.Sin)
                nc.scalar.activation(ZS[:, 8, :], ZS[:, 6, :], ACT.Sin, scale=0.5).then_inc(sin_done, 1)

            def square(l, n, tiles, t, y, junk):
                k = norm_at[(l, n)] + tiles.index(t)
                if k >= 2:
                    act.wait_ge(sq_done, max(k - 1, norm_at[(l, n)]))
                nc.scalar.activation(junk[:, t % 2, :], y, ACT.Square, accum_out=SS[:, t:t + 1]).then_inc(sq_done, 1)

            def root(l, n, tiles, t):
                act.wait_ge(ms_ready, norm_at[(l, n)] + tiles.index(t) + 1)
                nc.scalar.activation(RS[:, t:t + 1], RS[:, t:t + 1], ACT.Sqrt).then_inc(rt_done, 1)

            def norm(l, n, tiles, x_at):
                for t in tiles:
                    act.wait_ge(x_new, x_at - tiles[-1] + t)
                    square(l, n, tiles, t, X[:, t, :], JUNK)
                    if t > tiles[0]:
                        root(l, n, tiles, t - 1)
                root(l, n, tiles, tiles[-1])

            for m in range(12 * L):
                round_to(U[("mod", m // 12, m % 12, 1)] + 2)
                if m == PREP0 + PREP_SIN * PREP_STEP:
                    sines(0)
                elif m == PREP0:
                    act.wait_ge(ld_x, ld_x_at[(0, 0)])
                    for t in toks(0):
                        square(0, 0, toks(0), t, X[:, t, :], JUNK0)

            def norm_hi(l, n, c0):
                for k in range(KT):
                    banks.released(act, ("norm", l, n, k))
                    nc.scalar.activation(HT[:, 0, k, c0:N], TN[:, k % 2, c0:N], ACT.Copy).then_inc(ht_hi, 1)

            for l in range(L):
                c0 = 0 if l == 0 else CTX
                if l == 0:
                    for t in toks(0):
                        root(0, 0, toks(0), t)
                else:
                    norm(l, 0, toks(0), x_new_at[(0, 1)])
                    act.dma_start(xscr.rearrange("(t p) d -> p t d", p=P), X[:, :, :]).then_inc(x_stored, 16)
                norm_hi(l, 0, 0)
                round_to(U[("kv", l)] + 2)
                for t in range(4):
                    banks.wait(act, ("kv", l, t))
                    nc.scalar.activation(V[:, t, :], banks_t[t][:, P:2 * P], ACT.Copy).then_inc(v_ready, 1)
                round_to(U[("u", l, 1)] + 2)
                for t in range(4):
                    banks.wait(act, ("u", l, t))
                    if t >= 2:
                        act.wait_ge(u_stored[t % 2], 16 * (2 * l + 1))
                    elif l > 0:
                        act.wait_ge(g_stored[t], 128 * l)
                    banks.release(nc.scalar.activation(STG[:, t % 2, :], banks_t[t][:, :], ACT.Copy), ("u", l, t))
                    banks.released(act, ("u", l, t))
                    act.dma_start(uscr[l, t * P:(t + 1) * P, :], STG[:, t % 2, :]).then_inc(u_stored[t % 2], 16)
                round_to(U[("q", l, 1)] + 2)
                banks.wait(act, ("kT", l))
                banks.release(nc.scalar.activation(kT[:, :], banks_t[7][:, :], ACT.Copy), ("kT", l))
                for t in toks(l):
                    banks.wait(act, ("qT", l, t))
                    banks.release(nc.scalar.activation(qT[:, t, :, :].rearrange("p a b -> p (a b)"),
                                                       banks_t[6 + t % 2][:, :], ACT.Copy), ("qT", l, t))
                for q in range(4):
                    banks.wait(act, ("uc", l, q))
                    banks.release(nc.scalar.activation(UC[:, 8 * q:8 * q + 8, :].rearrange("p a b -> p (a b)"),
                                                       banks_t[6 + q % 2][:, :], ACT.Copy), ("uc", l, q))
                for q in range(9):
                    if q < 8:
                        if q >= 2:
                            banks.wait(act, ("v", l, q - 2))
                        for r in range(2):
                            banks.wait(act, ("gt", l, q, r))
                            banks.release(nc.scalar.activation(GT[q % 2][:, r, :, :].rearrange("p a b -> p (a b)"),
                                                               banks_t[4 + r][:, :], ACT.Copy), ("gt", l, q, r))
                    if q >= 1:
                        p = q - 1
                        banks.wait(act, ("v", l, p))
                        if l > 0 and p == 0:
                            act.wait_ge(x_stored, 16)
                        nc.scalar.activation(
                            S[0:64, :, 4 * p:4 * p + 4, 1:C],
                            banks_t[p % 2][0:64, :].rearrange("p (r g c) -> p r g c", r=2, g=4)[:, :, :, 0:C - 1],
                            ACT.Copy).then_inc(v_fwd, 1)
                for i in range(8):
                    round_to(U[("gate", l, i)] + 2)
                    for f in range(2):
                        banks.wait(act, ("gate", l, i, f))
                        if i == 0:
                            act.wait_ge(u_stored[f], 32 * (l + 1))
                        else:
                            act.wait_ge(g_stored[f], 16 * (8 * l + i))
                        banks.release(nc.scalar.activation(STG[:, f, c0:N], banks_t[4 + f][:, 0:N - c0], ACT.Sigmoid),
                                      ("gate", l, i, f))
                        banks.released(act, ("gate", l, i, f))
                        act.dma_start(gscr[l, 2 * i + f, :, c0:N], STG[:, f, c0:N]).then_inc(g_stored[f], 16)
                act.wait_ge(ld_sink, 16 * (l + 1))
                items = att_items(l)

                def exps(i):
                    t, h = items[i]
                    k = att_base[l] + i
                    w = N if t >= 2 else CTX
                    banks.wait(act, ("sc", l, i))
                    act.wait_ge(row_max, k + 1)
                    st = ST[:, i % 2, :]
                    if k >= 2:
                        act.wait_ge(p_norm, k - 1)
                    if i >= 2:
                        banks.wait(act, ("pt", l, i - 2))
                    nc.scalar.activation(LT[:, i % 2, 0:1], SK[:, h:h + 1], ACT.Exp, bias=st[:, 1:2]).then_inc(sink_done, 1)
                    banks.release(nc.scalar.activation(PR[:, i % 2, 0:w], banks_t[4 + i % 2][:, 0:w], ACT.Exp,
                                                       bias=st[:, 1:2], scale=HD ** -0.5, accum_out=st[:, 2:3]),
                                  ("sc", l, i))

                def turned(i):
                    t, h = items[i]
                    w = N if t >= 2 else CTX
                    banks.wait(act, ("pt", l, i))
                    banks.release(nc.scalar.activation(PT[:, i % 2, 0:w // P, :].rearrange("p a b -> p (a b)"),
                                                       banks_t[6 + i % 2][:, 0:w], ACT.Copy), ("pt", l, i))
                    if h == 1 and t > toks(l)[0]:
                        o_part(t - 1)

                def o_part(t):
                    banks.wait(act, ("o", l, t))
                    nc.scalar.activation(OT[:, 0, :, t * P:(t + 1) * P],
                                         banks_t[t % 2][:, :].rearrange("p (k n) -> p k n", k=4), ACT.Copy).then_inc(o_hi, 1)

                n = len(items)
                for i in range(n + 2):
                    if i < n:
                        exps(i)
                    if i >= 2:
                        turned(i - 2)
                o_part(3)
                for q in range(10):
                    if q < 8:
                        x = q % 3
                        if q >= 3:
                            act.wait_ge(mi_loaded[x], mi_count(l, q - 3))
                        for side in (1, 0):
                            banks.wait(act, ("kb", l, q, side))
                            ins = nc.scalar.activation(
                                KB[:, x, :, 8 - 8 * side:15 - 8 * side, :],
                                banks_t[2 + side][0:H, 0:448].rearrange("p (g a h) -> p g a h", g=4, a=7), ACT.Copy)
                            if side == 1:
                                banks.release(ins, ("kb", l, q, 1))
                            else:
                                ins.then_inc(kb_copied, 1)
                    if q >= 2:
                        p = q - 2
                        s = p // 4
                        rows = slice(s * 64, s * 64 + (64 if l == 0 else 32))
                        gl = (4 * p) % 16
                        banks.wait(act, ("y", l, p))
                        banks.release(nc.scalar.activation(
                            YY[rows, :, gl * H:(gl + 4) * H].rearrange("p t (g h) -> p g t h", g=4),
                            banks_t[p % 2][rows, :].rearrange("p (g t h) -> p g t h", g=4, t=T), ACT.Copy), ("y", l, p))
                banks.released(act, ("y", l, 6))
                banks.released(act, ("y", l, 7))
                nch = 64 if l == 0 else 32
                for s in range(2):
                    act.dma_start(yscr[l, c0:N, s * 256:(s + 1) * 256].rearrange("(c t) h -> c t h", t=T),
                                  YY[s * 64:s * 64 + nch, :, :]).then_inc(y_stored, 16)
                act.wait_ge(y_stored, 32 * (l + 1))
                act.dma_start(YK[:, c0 // P:TT, :], yscr[l, c0:N, :].rearrange("(t p) n -> p t n", p=P)).then_inc(ld_y, 16)
                for f in range(4):
                    banks.wait(act, ("yT", l, f))
                    banks.release(nc.scalar.activation(GF[:, f, c0:N], banks_t[6 + f % 2][:, c0:N], ACT.Gelu_apprx_tanh),
                                  ("yT", l, f))
                for f in range(4):
                    banks.released(act, ("yT", l, f))
                    nc.scalar.activation(GTR[:, 0, f, c0:N], GF[:, f, c0:N], ACT.Copy).then_inc(g_hi, 1)
                round_to(U[("glu", l)] + 2)
                for f in range(4):
                    banks.wait(act, ("glu", l, f))
                    if f >= 2:
                        act.wait_ge(s_f, 4 * l + f - 1)
                    banks.release(nc.scalar.activation(SGT[:, f % 2, c0:N], banks_t[f][:, c0:N], ACT.Sigmoid,
                                                       bias=COLS[:, 96 + f:97 + f]), ("glu", l, f))
                for f in range(4):
                    act.wait_ge(s_f, 4 * l + f + 1)
                    nc.scalar.activation(STR[:, 0, f, c0:N], SF[:, f % 2, c0:N], ACT.Copy).then_inc(s_hi, 1)
                for nb in range(2):
                    round_to(U[("pb", l, nb)] + 2)
                    for f in range(4):
                        k = 8 * l + 4 * nb + f
                        act.wait_ge(m_f, k + 1)
                        nc.scalar.activation(HT[:, 0, 4 * nb + f, c0:N], MT1[:, f, c0:N], ACT.Copy).then_inc(m_hi, 1)
                for nb in range(2):
                    round_to(U[("out", l, nb, 1)] + 2)
                    for t in toks(l):
                        banks.wait(act, ("out", l, nb, t))
                        banks.release(nc.scalar.activation(YA[:, t, nb * 512:(nb + 1) * 512], banks_t[t][:, :], ACT.Copy),
                                      ("out", l, nb, t))
                        if nb == 1:
                            banks.released(act, ("out", l, nb, t))
                            square(l, "r0", toks(l), t, YA[:, t, :], JUNK)
                            if t > toks(l)[0]:
                                root(l, "r0", toks(l), t - 1)
                root(l, "r0", toks(l), 3)
                norm(l, 1, toks(l), x_new_at[(l, 0)])
                if l == 0:
                    norm_hi(l, 1, c0)

                def ffn():
                    base = U[("g", 0)]
                    for n, (kind, c) in enumerate(ffn_order(DFF // FC)):
                        round_to(base + n + 2)
                        if n == PREP1 + PREP_SIN:
                            sines(1)
                        if kind == "g":
                            for f in range(2):
                                banks.wait(act, ("fg", c, f))
                                if c > 0:
                                    banks.released(act, ("fu", c - 1, f))
                                banks.release(nc.scalar.activation(SIL[:, f, :], banks_t[4 + f][:, :], ACT.Silu), ("fg", c, f))
                        elif kind == "u":
                            for f in range(2):
                                banks.released(act, ("fu", c, f))
                                if c >= 2:
                                    banks.wait(act, ("fd", c - 2, 3, 1))
                                nc.scalar.activation(HC[:, c % 2, 0, f, :], HF[:, f, :], ACT.Copy).then_inc(hc_hi, 1)
                    act.wait_ge(w_used, U[("d", DFF // FC - 1)] + 1)

                def block_in(name, i=None):
                    banks.released(act, (name, 1), i)
                    nc.scalar.activation(XC[:, 0, :, :], XM[:, :, :], ACT.Copy).then_inc(xc_hi, 1)

                def block_out(done):
                    banks.wait(act, ("ye0", 0), done)
                    banks.wait(act, ("ye", 1), done, 1)
                    for nb in range(2):
                        banks.release(nc.scalar.activation(YE[:, nb * 512:(nb + 1) * 512], banks_t[nb][:, :], ACT.Copy),
                                      ("ye0", nb))

                def hidden_hi(c, i):
                    banks.wait(act, ("he", c), i)
                    if c >= 2:
                        banks_used = NU + EU[("d", c - 2, 1)] + 1
                        act.wait_ge(w_used, banks_used + i * EUNITS)
                    elif c == 1:
                        act.wait_ge(w_used, NU + EU[("d", NEC - 2, 1)] + 1 - EUNITS + i * EUNITS)
                    else:
                        act.wait_ge(w_used, NU + i * EUNITS)
                    nc.scalar.activation(HB[:, c % 2, 0, :, :].rearrange("p a b -> p (a b)"), banks_t[2 + c % 2][:, :],
                                         ACT.Copy).then_inc(he_hi, 1)

                def block_turn(i):
                    block_out(i)
                    for c in range(NEC):
                        round_to(EU[("g", c, 1)] + 2, i)
                        banks.wait(act, ("ge", c), i)
                        if c >= 2:
                            banks.released(act, ("ue", c - 2), i)
                        banks.release(nc.scalar.activation(SB[:, c % 2, :], banks_t[4 + c % 2][:, :], ACT.Silu), ("ge", c))
                        if c == 2:
                            banks.wait(act, "put", i)
                            banks.release(nc.scalar.activation(PUT[:, :, :].rearrange("p a b -> p (a b)"),
                                                               banks_t[2][:, 0:2 * P], ACT.Copy), "put")
                        if c > 0:
                            hidden_hi(c - 1, i)
                        round_to(EU[("u", c, 1)] + 2, i)
                        if c > 0:
                            round_to(EU[("d", c - 1, 1)] + 2, i)
                    hidden_hi(NEC - 1, i)
                    round_to(EUNITS, i)
                    block_in("ga", i)
                    round_to(EUNITS + 2, i)

                if l == 0:
                    ffn()
                else:
                    act.wait_ge(top_diff, 1)
                    nc.scalar.activation(RW[:, :, 2:3], RW[:, :, 1:2], ACT.Exp).then_inc(top_exp, 1)
                    block_in("ga0")
                    round_to(NU + 2, past=3)
                    act.wait_ge(plan_ready, 1)
                    blocks = act.value_load(PLANI[0:1, 0:1], min_val=NE, max_val=MAXB)
                    with act.Fori(0, blocks) as i:
                        rounded[0] = 3
                        block_turn(i)
                    block_out(blocks)
                for t in toks(l):
                    for nb in range(2):
                        if l == 0:
                            banks.released(act, ("fd", DFF // FC - 1, t, nb))
                        else:
                            banks.released(act, ("back_last", t - 2, nb), blocks - 1)
                    square(l, "r1", toks(l), t, YA[:, t - 2 * l, :], JUNK)
                    if t > toks(l)[0]:
                        root(l, "r1", toks(l), t - 1)
                root(l, "r1", toks(l), 3)
            for t in toks(1):
                act.wait_ge(x_new, x_new_at[(1, 1)] - 3 + t)
                act.dma_start(out[0, (t - 2) * P:(t - 1) * P, :], X[:, t, :]).then_inc(out_stored, 16)
            act.wait_ge(out_stored, 32)

        @block.vector
        def _(dve):
            chain = Chain(dve, dve_step)
            V_ = nc.vector
            split_n = [0]

            def split_to(n, i=None, past=0):
                last = NU + past if i is None else EUNITS + 3
                while split_n[0] <= min(n, last - 1):
                    u = split_n[0]
                    full_u = u if i is None else NU + u
                    slot = full_u % 3
                    dve.wait_ge(w_round, full_u + 1 if i is None else full_u + 1 + i * EUNITS)
                    V_.tensor_tensor(split[:, slot, 1, :], raw[:, slot, :], split[:, slot, 0, :].bitcast(F),
                                     ALU.subtract).then_inc(w_split, 1)
                    split_n[0] += 1

            def lo(out_, src, hi, sem=None):
                ins = V_.tensor_tensor(out_, src, hi.bitcast(F), ALU.subtract)
                return ins.then_inc(sem, 1) if sem is not None else ins

            V_.memset(CW[:, :, :, :].bitcast(F), 0.0).then_inc(cond_zero, 1)
            dve.wait_ge(cond_zero, 1)
            dve.wait_ge(cond_hi, 1)
            lo(CW[:, 1, :, 0:2], CF[:, :].rearrange("p (s k) -> p k s", s=2), CW[:, 0, :, 0:2], cond_ready)
            def Z(k):
                return ZS[:, k, :]

            def cmul(ore, oim, ar, ai, br, bi, t0, t1):
                chain(V_.tensor_tensor(t0, ai, bi, ALU.mult))
                chain(V_.tensor_tensor(ore, ar, br, ALU.mult))
                chain(V_.tensor_tensor(t1, ai, br, ALU.mult))
                chain(V_.tensor_tensor(oim, ar, bi, ALU.mult))
                chain(V_.tensor_tensor(ore, ore, t0, ALU.subtract))
                chain(V_.tensor_tensor(oim, oim, t1, ALU.add))

            def exact_exp(dst, src, stage):
                if stage == 0:
                    chain(V_.tensor_scalar(Z(11), src, -87.0, 88.0, ALU.max, ALU.min))
                    chain(V_.tensor_scalar(Z(12), Z(11), INV_LN2, ROUND, ALU.mult, ALU.add))
                    chain(V_.tensor_scalar(Z(12), Z(12), -ROUND, None, ALU.add))
                    for part in LN2:
                        chain(V_.scalar_tensor_tensor(Z(11), Z(12), -part, Z(11), ALU.mult, ALU.add))
                    chain(V_.tensor_scalar(Z(13), Z(11), 1.0 / 7, 1.0, ALU.mult, ALU.add))
                else:
                    for j in range(6, 0, -1):
                        chain(V_.scalar_tensor_tensor(Z(13), Z(13), 1.0 / j, Z(11), ALU.mult, ALU.mult))
                        chain(V_.tensor_scalar(Z(13), Z(13), 1.0, None, ALU.add))
                    chain(V_.tensor_scalar(ZI[:, :], Z(12), 127.0, 8388608.0, ALU.add, ALU.mult))
                    chain(V_.tensor_tensor(dst, Z(13), ZI[:, :].bitcast(F), ALU.mult))

            def ssm_prep(l, part):
                BI = BI_[l]
                if part == 0:
                    dve.wait_ge(ld_ssm, LD_SSM * (l + 1))
                    for r in range(2):
                        banks.wait(dve, ("arow", l, r))
                        banks.release(V_.tensor_copy(Z(r), banks_t[6 + r][:, 0:G]), ("arow", l, r))
                        banks.released(dve, ("arow", l, r))
                    for r in range(2):
                        banks.wait(dve, ("crow", l, r))
                        ins = V_.tensor_scalar(CC[:, r, :, :].rearrange("p a b -> p (a b)"), banks_t[4 + r][:, :],
                                               1.0 if r == 0 else -1.0, None, ALU.mult)
                        banks.release(ins, ("crow", l, r))
                        banks.released(dve, ("crow", l, r))
                elif part == 1:
                    exact_exp(Z(2), DTR[:, :], 0)
                elif part == 2:
                    exact_exp(Z(2), DTR[:, :], 1)
                elif part == 3:
                    chain(V_.tensor_tensor(Z(3), Z(0), Z(2), ALU.mult))
                    exact_exp(Z(4), Z(3), 0)
                elif part == 4:
                    exact_exp(Z(4), Z(3), 1)
                elif part == 5:
                    chain(V_.tensor_tensor(Z(5), Z(1), Z(2), ALU.mult))
                    chain(V_.tensor_scalar(Z(10), Z(5), 1.0 / TWO_PI, ROUND, ALU.mult, ALU.add))
                    chain(V_.tensor_scalar(Z(10), Z(10), -ROUND, None, ALU.add))
                    chain(V_.tensor_copy(Z(6), Z(5)))
                    for piece in PI_PARTS:
                        chain(V_.scalar_tensor_tensor(Z(6), Z(10), -piece, Z(6), ALU.mult, ALU.add))
                    V_.tensor_scalar(Z(6), Z(6), 3.1415925, -3.1415925, ALU.min, ALU.max).then_inc(ang_ready, 1)
                elif part == 6:
                    dve.wait_ge(sin_done, l + 1)
                    chain(V_.tensor_tensor(Z(9), Z(8), Z(8), ALU.mult))
                    chain(V_.tensor_scalar(Z(9), Z(9), -2.0, 1.0, ALU.mult, ALU.add))
                    chain(V_.memset(PW[:, 0, 0, :], 1.0))
                    chain(V_.memset(PW[:, 1, 0, :], 0.0))
                    chain(V_.tensor_tensor(PW[:, 0, 1, :], Z(4), Z(9), ALU.mult))
                    chain(V_.tensor_tensor(PW[:, 1, 1, :], Z(4), Z(7), ALU.mult))
                    chain(V_.tensor_tensor(Z(10), Z(0), Z(0), ALU.mult))
                    chain(V_.tensor_tensor(Z(11), Z(1), Z(1), ALU.mult))
                    chain(V_.tensor_tensor(Z(10), Z(10), Z(11), ALU.add))
                    chain(V_.reciprocal(Z(10), Z(10)))
                elif part == 7:
                    chain(V_.tensor_scalar(Z(11), PW[:, 0, 1, :], -1.0, None, ALU.add))
                    chain(V_.tensor_scalar(Z(12), Z(1), -1.0, None, ALU.mult))
                    cmul(Z(13), Z(14), Z(11), PW[:, 1, 1, :], Z(0), Z(12), Z(3), Z(5))
                    chain(V_.tensor_tensor(Z(13), Z(13), Z(10), ALU.mult))
                    chain(V_.tensor_tensor(Z(14), Z(14), Z(10), ALU.mult))
                elif part == 8:
                    wide = lambda z: z.unsqueeze(2).broadcast_to([P, G, H])
                    t0, t1 = (BT[:, r, :].rearrange("p (g h) -> p g h", g=G) for r in range(2))
                    cmul(BB[:, 0, :, :], BB[:, 1, :, :], wide(Z(13)), wide(Z(14)), BI[:, 0, :, :], BI[:, 1, :, :], t0, t1)
                elif part < 12:
                    n = k = 2 ** (part - 9)
                    b = lambda r: PW[:, r, k:k + 1, :].broadcast_to([P, n, G])
                    tmp = [BT[:, r, 0:n * G].rearrange("p (t g) -> p t g", t=n) for r in range(2)]
                    cmul(PW[:, 0, k + 1:k + n + 1, :], PW[:, 1, k + 1:k + n + 1, :], PW[:, 0, 1:n + 1, :],
                         PW[:, 1, 1:n + 1, :], b(0), b(1), *tmp)
                else:
                    f, w = slice(0, 64), slice(64, P)
                    for r in range(2):
                        chain(V_.tensor_copy(PG[f, 0, r, :, :], PW[f, r, 7::-1, :]))
                        chain(V_.tensor_copy(PG[w, 0, r, :, :], PW[w, r, 0:8, :]))
                        chain(V_.tensor_copy(PG[f, 1, r, :, :], PW[f, r, 1:9, :]))
                        chain(V_.tensor_copy(PG[w, 1, r, :, :], PW[w, r, 8:0:-1, :]))
                        chain(V_.tensor_copy(A8[:, 0, r, :], PW[:, 0, 8, :]))
                    chain(V_.tensor_scalar(A8[:, 1, 0, :], PW[:, 1, 8, :], -1.0, None, ALU.mult))
                    V_.tensor_copy(A8[:, 1, 1, :], PW[:, 1, 8, :]).then_inc(prep_done, 1)

            dve.wait_ge(ld_const, 16)
            dve.wait_ge(ld_bm, 64)
            for l in range(L):
                for nb in range(12):
                    m = 12 * l + nb
                    split_to(U[("mod", l, nb, 1)] + 2)
                    banks.wait(dve, ("mod", l, nb))
                    if m >= 2:
                        dve.wait_ge(mod_stored[m % 2], 16 * (m // 2))
                    st = MS[:, m % 2, :]
                    banks.release(V_.tensor_tensor(st, banks_t[nb % 4][0:2, :], BM[:, l, nb * 512:(nb + 1) * 512], ALU.add),
                                  ("mod", l, nb))
                    if nb // 2 in (2, 5):
                        j = nb // 2 // 3
                        banks.released(dve, ("mod", l, nb))
                        V_.tensor_tensor(st, st, NG[:, l, j, (nb % 2) * 512:(nb % 2 + 1) * 512], ALU.mult)\
                            .then_inc(mod_row, 1)
                    part, rest = divmod(m - PREP0, PREP_STEP)
                    if 0 <= part < PREP_EARLY and rest == 0:
                        ssm_prep(0, part)
            for part in range(PREP_EARLY, PREP_PARTS):
                ssm_prep(0, part)

            def columns(l):
                banks.wait(dve, ("cols", l))
                banks.release(V_.tensor_copy(COLS[:, :], banks_t[7][:, 0:100]), ("cols", l))
                banks.released(dve, ("cols", l))
                for s in range(2):
                    for n in range(2):
                        c = s * 32 + (8 if n == 0 else 24)
                        chain(V_.scalar_tensor_tensor(AF[:, s, n, :], COLS[:, c:c + 8], 1.0,
                                                      COLS[:, 64 + 16 * n:72 + 16 * n], ALU.add, ALU.mult))

            def rstd(l, n, tiles, t):
                k = norm_at[(l, n)] + tiles.index(t) + 1
                dve.wait_ge(sq_done, k)
                V_.tensor_scalar(RS[:, t:t + 1], SS[:, t:t + 1], 1.0 / D, EPS, ALU.mult, ALU.add).then_inc(ms_ready, 1)
                dve.wait_ge(rt_done, k)
                chain(V_.reciprocal(RS[:, t:t + 1], RS[:, t:t + 1]))

            def norm(l, n, tiles):
                for t in tiles:
                    rstd(l, n, tiles, t)
                    V_.tensor_scalar(YA[:, t, :], X[:, t, :], RS[:, t:t + 1], None, ALU.mult).then_inc(xn_ready, 1)
                for k in range(KT):
                    key = ("norm", l, n, k)
                    b = banks_t[6 + k % 2]
                    banks.wait(dve, key)
                    kk = ht_ready_at[(l, n)] - 8 + k
                    if kk >= 2 and (l, n) != (1, 1):
                        dve.wait_ge(ht_ready, kk - 1)
                    dst = (lambda s: HTF[:, k, :]) if (l, n) == (1, 1) else (lambda s: TN[:, k % 2, s * CTX:(s + 1) * CTX])
                    for s in sorted({t // 2 for t in tiles}):
                        c = s * 32 + 16 * n + k
                        ins = V_.tensor_scalar(dst(s), b[:, s * CTX:(s + 1) * CTX], AF[:, s, n, k:k + 1],
                                               COLS[:, c:c + 1], ALU.mult, ALU.add)
                    banks.release(ins, key)
                    if (l, n) != (1, 1) and k > 0:
                        norm_lo(l, n, k - 1, tiles[0] * P)
                if (l, n) != (1, 1):
                    norm_lo(l, n, KT - 1, tiles[0] * P)

            def norm_lo(l, n, k, a0):
                banks.released(dve, ("norm", l, n, k))
                dve.wait_ge(ht_hi, ht_ready_at[(l, n)] - 8 + k + 1)
                lo(HT[:, 1, k, a0:N], TN[:, k % 2, a0:N], HT[:, 0, k, a0:N], ht_ready)

            def rope(src, dst, nh, t, key, done):
                c = COS[:, t - 2, :]
                s = SIN[:, t - 2, :]
                shape = dst(0).shape
                bc = lambda z: z.unsqueeze(1).unsqueeze(1).broadcast_to(list(shape))
                t0 = TM[:, 0:nh * 32].rearrange("p (a b c) -> p a b c", b=shape[2], c=32)
                t1 = TM[:, 256:256 + nh * 32].rearrange("p (a b c) -> p a b c", b=shape[2], c=32)
                chain(V_.tensor_tensor(dst(0), src(0), bc(c), ALU.mult))
                chain(V_.tensor_tensor(t0, src(1), bc(s), ALU.mult))
                chain(V_.tensor_tensor(dst(1), src(1), bc(c), ALU.mult))
                ins = V_.tensor_tensor(t1, src(0), bc(s), ALU.mult)
                banks.release(ins, key)
                banks.released(dve, key)
                chain(V_.tensor_tensor(dst(0), dst(0), t0, ALU.subtract))
                V_.tensor_tensor(dst(1), dst(1), t1, ALU.add).then_inc(done, 1)
                dve.wait_ge(done, done_n[done.name] + 1)
                done_n[done.name] += 1

            done_n = {q_tok.name: 0, k_tok.name: 0}

            def inproj(l):
                split_to(U[("kv", l)] + 2)
                for t in range(4):
                    key = ("kv", l, t)
                    banks.wait(dve, key)
                    dve.wait_ge(v_ready, 4 * l + t + 1)
                    b = banks_t[t]
                    if t < 2:
                        banks.release(V_.tensor_copy(KS[:, t, :], b[:, 0:P]), key)
                    else:
                        sv = b[:, 0:P].rearrange("p (g a d) -> p g a d", g=2, a=2)
                        dv = KS[:, t, :].rearrange("p (g a d) -> p g a d", g=2, a=2)
                        rope(lambda x: sv[:, :, x:x + 1, :], lambda x: dv[:, :, x:x + 1, :], 2, t, key, k_tok)
                split_to(U[("u", l, 1)] + 2)
                split_to(U[("q", l, 1)] + 0)
                for t in toks(l):
                    key = ("q", l, t)
                    if t == toks(l)[0]:
                        split_to(U[("q", l, 1)] + 2)
                    banks.wait(dve, key)
                    b = banks_t[t]
                    if t < 2:
                        banks.release(V_.tensor_copy(
                            QS[:, t, :].rearrange("p (j g d) -> p g j d", j=4, g=2),
                            b[:, :].rearrange("p (g j d) -> p g j d", g=2, j=4)), key)
                    else:
                        sv = b[:, :].rearrange("p (g j a d) -> p g j a d", g=2, j=4, a=2)
                        dv = QS[:, t, :].rearrange("p (j g a d) -> p g j a d", j=4, g=2, a=2)
                        rope(lambda x: sv[:, :, :, x, :], lambda x: dv[:, :, :, x, :], 8, t, key, q_tok)

            def mats(dst, powers, m, q):
                gs = slice(4 * q, 4 * q + 4)
                pw = [powers[:, r, :, gs].rearrange("p t g -> p g t").unsqueeze(3).broadcast_to([P, 4, T, H]) for r in range(2)]
                mm = [m[:, r, gs, :].unsqueeze(2).broadcast_to([P, 4, T, H]) for r in range(2)]
                tm = TM[:, :].rearrange("p (g t h) -> p g t h", g=4, t=T)
                o = [dst(r).rearrange("p g (t h) -> p g t h", t=T) for r in range(2)]
                return pw, mm, tm, o

            def ssm_in(l):
                banks.wait(dve, ("qT", l, 3))
                for q in range(8):
                    pw, mm, tm, o = mats(lambda r: GP[q % 2][:, r, :, :], PG[:, 0], BB, q)
                    if q == 1:
                        dve.wait_ge(u_grouped, 2 * (l + 1))
                    elif q > 1:
                        for r in range(2):
                            banks.wait(dve, ("gt", l, q - 2, r))
                    chain(V_.tensor_tensor(tm, pw[1], mm[1], ALU.mult))
                    chain(V_.tensor_tensor(o[0], pw[0], mm[0], ALU.mult))
                    chain(V_.tensor_tensor(o[0], o[0], tm, ALU.subtract))
                    chain(V_.tensor_tensor(tm, pw[1], mm[0], ALU.mult))
                    chain(V_.tensor_tensor(o[1], pw[0], mm[1], ALU.mult))
                    V_.tensor_tensor(o[1], o[1], tm, ALU.add).then_inc(gp_ready, 1)
                    dve.wait_ge(gp_ready, 8 * l + q + 1)
                    if q > 1:
                        v_back(l, q - 2)
                v_back(l, 6)
                v_back(l, 7)

            def v_back(l, q):
                key = ("v", l, q)
                banks.wait(dve, key)
                dve.wait_ge(v_fwd, 8 * l + q + 1)
                if l > 0 and q == 0:
                    dve.wait_ge(x_stored, 16)
                v = banks_t[q % 2][64:P, :].rearrange("p (r g c) -> p r g c", r=2, g=4)
                s = S[64:P, :, 4 * q:4 * q + 4, :]
                chain(V_.tensor_copy(s[:, :, :, 1:33], v[:, :, :, 31::-1]))
                banks.release(V_.tensor_copy(s[:, :, :, 33:64], v[:, :, :, 63:32:-1]), key)

            def attention(l):
                items = att_items(l)
                dve.wait_ge(ld_sink, 16 * (l + 1))

                def maxes(i):
                    t, h = items[i]
                    w = N if t >= 2 else CTX
                    st = ST[:, i % 2, :]
                    banks.wait(dve, ("sc", l, i))
                    chain(V_.reduce_max(st[:, 0:1], banks_t[4 + i % 2][:, 0:w], AX))
                    chain(V_.tensor_scalar(st[:, 0:1], st[:, 0:1], HD ** -0.5, SK[:, h:h + 1], ALU.mult, ALU.max))
                    V_.tensor_scalar(st[:, 1:2], st[:, 0:1], -1.0, None, ALU.mult).then_inc(row_max, 1)

                def norms(i):
                    t, h = items[i]
                    w = N if t >= 2 else CTX
                    st = ST[:, i % 2, :]
                    banks.released(dve, ("sc", l, i))
                    chain(V_.tensor_tensor(st[:, 3:4], st[:, 2:3], LT[:, i % 2, 0:1], ALU.add))
                    chain(V_.reciprocal(st[:, 4:5], st[:, 3:4]))
                    V_.tensor_scalar(PR[:, i % 2, 0:w], PR[:, i % 2, 0:w], st[:, 4:5], None, ALU.mult).then_inc(p_norm, 1)
                    dve.wait_ge(p_norm, att_base[l] + i + 1)
                    if h == 5 and t > toks(l)[0]:
                        o_part(t - 1)

                def o_part(t):
                    dve.wait_ge(o_hi, t + 1 if l == 0 else 2 + t + 1)
                    banks.release(lo(OT[:, 1, :, t * P:(t + 1) * P], banks_t[t % 2][:, :].rearrange("p (k n) -> p k n", k=4),
                                     OT[:, 0, :, t * P:(t + 1) * P]), ("o", l, t))

                for i in range(len(items) + 1):
                    if i < len(items):
                        maxes(i)
                    if i >= 1:
                        norms(i - 1)
                o_part(3)

            def ssm_out(l):
                dve.wait_ge(ld_skip, 16 * (l + 1))
                chain(V_.tensor_tensor(DR[:, :, :], DR[:, :, :], EYE[0:H, 0:H].unsqueeze(1).broadcast_to([H, G, H]), ALU.mult))
                for q in range(9):
                    if q < 8:
                        x = q % 3
                        if q >= 3:
                            banks.wait(dve, ("y", l, q - 3))
                        else:
                            banks.wait(dve, ("gate", l, 7, 1))
                        pw, mm, tm, o = mats(lambda r: Hm[:, x, r, :, :], PG[:, 1], CC, q)
                        chain(V_.tensor_tensor(tm, pw[1], mm[1], ALU.mult))
                        chain(V_.tensor_tensor(o[0], pw[0], mm[0], ALU.mult))
                        chain(V_.tensor_tensor(o[0], o[0], tm, ALU.add))
                        chain(V_.tensor_tensor(tm, pw[1], mm[0], ALU.mult))
                        chain(V_.tensor_tensor(o[1], pw[0], mm[1], ALU.mult))
                        V_.tensor_tensor(o[1], o[1], tm, ALU.subtract).then_inc(h_ready, 1)
                        dve.wait_ge(h_ready, 8 * l + q + 1)
                    if q >= 1:
                        p = q - 1
                        dve.wait_ge(kb_copied, 8 * l + p + 1)
                        banks.release(V_.tensor_tensor(KB[:, p % 3, :, 7, :], DR[:, 4 * p:4 * p + 4, :],
                                                       banks_t[2][0:H, 448:512].rearrange("p (g h) -> p g h", g=4), ALU.add),
                                      ("kb", l, p, 0))

            def glu(l):
                c0 = 0 if l == 0 else CTX
                for f in range(4):
                    dve.wait_ge(g_hi, 4 * l + f + 1)
                    lo(GTR[:, 1, f, c0:N], GF[:, f, c0:N], GTR[:, 0, f, c0:N], g_ready)
                split_to(U[("glu", l)] + 2)
                for f in range(4):
                    banks.released(dve, ("glu", l, f))
                    if f >= 2:
                        dve.wait_ge(s_ready, 4 * l + f - 1)
                    V_.tensor_tensor(SF[:, f % 2, c0:N], GF[:, f, c0:N], SGT[:, f % 2, c0:N], ALU.mult).then_inc(s_f, 1)
                    if f >= 1:
                        s_lo(l, f - 1)
                s_lo(l, 3)

            def s_lo(l, f):
                c0 = 0 if l == 0 else CTX
                dve.wait_ge(s_hi, 4 * l + f + 1)
                lo(STR[:, 1, f, c0:N], SF[:, f % 2, c0:N], STR[:, 0, f, c0:N], s_ready)

            def merge(l):
                c0 = 0 if l == 0 else CTX
                for nb in range(2):
                    split_to(U[("pa", l, nb)] + 2)
                    for f in range(4):
                        ft = 8 * l + 4 * nb + f
                        banks.wait(dve, ("pa", l, nb, f))
                        dve.wait_ge(ld_g[f % 2], 32 * (ft // 2 + 1))
                        if nb > 0:
                            dve.wait_ge(m_ready, 8 * l + f + 1)
                        banks.release(V_.tensor_tensor(MT1[:, f, c0:N], banks_t[f][:, c0:N], SGA[:, f % 2, c0:N], ALU.mult),
                                      ("pa", l, nb, f))
                        banks.released(dve, ("pa", l, nb, f))
                        if f == 3:
                            split_to(U[("pb", l, nb)] + 2)
                        merge_b(l, nb, f, c0)

            def merge_b(l, nb, f, c0):
                k = 8 * l + 4 * nb + f
                banks.wait(dve, ("pb", l, nb, f))
                banks.release(V_.tensor_tensor(TM[:, c0:N], banks_t[4 + f][:, c0:N], SGB[:, f % 2, c0:N], ALU.mult),
                              ("pb", l, nb, f))
                banks.released(dve, ("pb", l, nb, f))
                V_.tensor_tensor(MT1[:, f, c0:N], MT1[:, f, c0:N], TM[:, c0:N], ALU.add).then_inc(m_f, 1)
                dve.wait_ge(m_hi, k + 1)
                lo(HT[:, 1, 4 * nb + f, c0:N], MT1[:, f, c0:N], HT[:, 0, 4 * nb + f, c0:N], m_ready)

            def residual(l, n):
                dve.wait_ge(ld_gb, 32 * (2 * l + n + 1))
                dve.wait_ge(ld_x, ld_x_at[(l, n + 1)])
                for t in toks(l):
                    rstd(l, f"r{n}", toks(l), t)
                    y = YA[:, t - 2 if (l, n) == (1, 1) else t, :]
                    chain(V_.scalar_tensor_tensor(y, y, RS[:, t:t + 1], GB[:, t // 2, :], ALU.mult, ALU.mult))
                    V_.tensor_tensor(X[:, t, :], X[:, t, :], y, ALU.add).then_inc(x_new, 1)
                dve.wait_ge(x_new, x_new_at[(l, n)])

            def ffn():
                base = U[("g", 0)]
                for n, (kind, c) in enumerate(ffn_order(DFF // FC)):
                    split_to(base + n + 2)
                    if 0 <= n - PREP1 < PREP_PARTS:
                        ssm_prep(1, n - PREP1)
                    if kind == "u":
                        for f in range(2):
                            banks.released(dve, ("fg", c, f))
                            banks.wait(dve, ("fu", c, f))
                            if 2 * c + f >= 2:
                                dve.wait_ge(hc_ready, 2 * c + f - 1)
                            banks.release(V_.tensor_tensor(HF[:, f, :], banks_t[6 + f][:, :], SIL[:, f, :], ALU.mult),
                                          ("fu", c, f))
                        for f in range(2):
                            dve.wait_ge(hc_hi, 2 * c + f + 1)
                            lo(HC[:, c % 2, 1, f, :], HF[:, f, :], HC[:, c % 2, 0, f, :], hc_ready)
                    elif kind == "d":
                        for t in range(TT):
                            for nb in range(2):
                                key = ("fd", c, t, nb)
                                banks.wait(dve, key)
                                y = YA[:, t, nb * 512:(nb + 1) * 512]
                                b = banks_t[(2 * t + nb) % 4][:, :]
                                if c > 0:
                                    banks.released(dve, ("fd", c - 1, t, nb))
                                    ins = V_.tensor_tensor(y, y, b, ALU.add)
                                else:
                                    ins = V_.tensor_copy(y, b)
                                banks.release(ins, key)

            def picks(dst, j, sem, gates=None):
                iota = TAB[:, 1, :]
                for t in range(2):
                    slot = SLOT[:, t, bass.ds(j, 1)]
                    if gates is None:
                        ins = V_.tensor_scalar(dst[:, t, :], iota, slot, None, ALU.is_equal)
                    else:
                        ins = V_.tensor_scalar(dst[:, t, :], iota, slot, GATE[:, t, bass.ds(j, 1)], ALU.is_equal, ALU.mult)
                ins.then_inc(sem, 1)

            def block_in(name, i=None):
                for half in range(2):
                    banks.wait(dve, (name, half), i)
                    for k in range(4):
                        kk = 4 * half + k
                        c = 32 + 16 + kk
                        ins = V_.tensor_scalar(XM[:, kk, :], banks_t[3 - half][:, k * P:(k + 1) * P],
                                               AF[:, 1, 1, kk:kk + 1], COLS[:, c:c + 1], ALU.mult, ALU.add)
                    banks.release(ins, (name, half))
                banks.released(dve, (name, 1), i)
                dve.wait_ge(xc_hi, 1 if i is None else i + 2)
                lo(XC[:, 1, :, :], XM[:, :, :], XC[:, 0, :, :], xc_ready)

            def add_block(name, i):
                for t in range(2):
                    for nb in range(2):
                        banks.wait(dve, (name, t, nb), i)
                        y = YA[:, t, nb * 512:(nb + 1) * 512]
                        b = banks_t[(5, 7, 2, 3)[2 * t + nb]][:, :]
                        banks.release(V_.tensor_tensor(y, y, b, ALU.add), (name, t, nb))

            def hidden_lo(c, i):
                banks.wait(dve, ("he", c), i)
                dve.wait_ge(he_hi, c + 1 + i * NEC)
                banks.release(lo(HB[:, c % 2, 1, :, :].rearrange("p a b -> p (a b)"), banks_t[2 + c % 2][:, :],
                                 HB[:, c % 2, 0, :, :].rearrange("p a b -> p (a b)")), ("he", c))

            def block_turn(i):
                for c in range(NEC):
                    split_to(EU[("g", c, 1)] + 2, i)
                    if c == 0:
                        add_block("back", i)
                    if c == 1:
                        picks(PICKG, i, gated_ready, gates=True)
                        picks(PICK, i + 1, pick_ready)
                    if c > 0:
                        hidden_lo(c - 1, i)
                    split_to(EU[("u", c, 1)] + 2, i)
                    banks.released(dve, ("ge", c), i)
                    banks.wait(dve, ("ue", c), i)
                    if c >= 2:
                        banks.wait(dve, ("he", c - 2), i)
                    banks.release(V_.tensor_tensor(HE[:, c % 2, :], banks_t[6 + c % 2][:, :], SB[:, c % 2, :], ALU.mult),
                                  ("ue", c))
                    if c > 0:
                        split_to(EU[("d", c - 1, 1)] + 2, i)
                hidden_lo(NEC - 1, i)
                split_to(EUNITS, i)
                block_in("ga", i)
                split_to(EUNITS + 2, i)

            def router():
                banks.wait(dve, "router")
                dve.wait_ge(ld_wr, 32)
                banks.release(V_.tensor_tensor(LG[:, :, :], banks_t[0][:, 0:2 * NE].rearrange("p (t e) -> p t e", t=2),
                                               BR[:, :].unsqueeze(1).broadcast_to([P, 2, NE]), ALU.add), "router")
                banks.released(dve, "router")
                for t in range(2):
                    for j in range(2):
                        chain(V_.reduce_max(TV[:, t, j:j + 1], LG[:, t, :], AX))
                        chain(V_.scalar_tensor_tensor(TF[:, t, :], LG[:, t, :], TV[:, t, j:j + 1], IOTA8,
                                                      ALU.is_equal, ALU.mult))
                        chain(V_.tensor_reduce(RW[:, t, 3 + j:4 + j], TF[:, t, :], AX, ALU.min))
                        if j == 0:
                            chain(V_.tensor_scalar(TF[:, t, :], IOTA8, RW[:, t, 3:4], None, ALU.is_equal))
                            chain(V_.scalar_tensor_tensor(LG[:, t, :], TF[:, t, :], -1e30, LG[:, t, :], ALU.mult, ALU.add))
                    ins = V_.tensor_tensor(RW[:, t, 1:2], TV[:, t, 1:2], TV[:, t, 0:1], ALU.subtract)
                    if t == 0:
                        chain(ins)
                ins.then_inc(top_diff, 1)
                selection()
                dve.wait_ge(top_exp, 1)
                for t in range(2):
                    e = RW[:, t, 2:3]
                    chain(V_.tensor_scalar(RW[:, t, 5:6], e, 1.0, None, ALU.add))
                    chain(V_.reciprocal(RW[:, t, 6:7], RW[:, t, 5:6]))
                    chain(V_.tensor_tensor(RW[:, t, 7:8], e, RW[:, t, 6:7], ALU.mult))
                    chain(V_.tensor_scalar(GA[:, t, :], IOTA8, RW[:, t, 3:4], RW[:, t, 6:7], ALU.is_equal, ALU.mult))
                    chain(V_.tensor_scalar(TF[:, t, :], IOTA8, RW[:, t, 4:5], RW[:, t, 7:8], ALU.is_equal, ALU.mult))
                    chain(V_.tensor_tensor(GA[:, t, :], GA[:, t, :], TF[:, t, :], ALU.add))
                    chain(V_.tensor_copy(GATE[:, t, 0:NE], GA[:, t, :]))
                plan()

            def selection():
                for t in range(2):
                    chain(V_.tensor_scalar(SEL[:, t, :], IOTA8, RW[:, t, 3:4], None, ALU.is_equal))
                    chain(V_.tensor_scalar(TF[:, t, :], IOTA8, RW[:, t, 4:5], None, ALU.is_equal))
                    ins = V_.tensor_tensor(SEL[:, t, :], SEL[:, t, :], TF[:, t, :], ALU.add)
                    if t == 0:
                        chain(ins)
                ins.then_inc(sel_ready, 1)

            def plan():
                dve.wait_ge(sel_ready, 1)
                banks.wait(dve, "rank")
                rank = banks_t[1][:, 0:3 * NE].rearrange("p (t e) -> p t e", t=3)
                s8 = SLOT[:, :, 0:NE]
                chain(V_.tensor_scalar(s8, rank[:, 0:2, :], 1.0, None, ALU.add))
                chain(V_.tensor_tensor(s8, s8, SEL[:, :, :], ALU.mult))
                chain(V_.tensor_scalar(s8, s8, -1.0, None, ALU.add))
                banks.release(V_.tensor_scalar(OV[:, 0, :], rank[:, 2, :], float(P) + 0.5, None, ALU.is_gt), "rank")
                banks.released(dve, "rank")
                chain(V_.memset(OV[:, 1, 0:1], 0.0))
                for e in range(1, NE):
                    chain(V_.tensor_tensor(OV[:, 1, e:e + 1], OV[:, 1, e - 1:e], OV[:, 0, e - 1:e], ALU.add))
                chain(V_.tensor_tensor(PLAN[:, 0:1], OV[:, 1, NE - 1:NE], OV[:, 0, NE - 1:NE], ALU.add))
                chain(V_.tensor_scalar(PLAN[:, 0:1], PLAN[:, 0:1], float(NE), None, ALU.add))
                chain(V_.tensor_scalar(PLAN[:, 1:1 + NE], IOTA8, float(NE), None, ALU.add))
                for k in range(MAXB - NE):
                    b = NE + k
                    chain(V_.scalar_tensor_tensor(OV[:, 2, :], OV[:, 1, :], float(k), OV[:, 0, :], ALU.is_equal, ALU.mult))
                    rows = [(PLAN[:, 1:1 + NE], PLAN[:, 1 + b:2 + b])]
                    rows += [(SLOT[:, t, 0:NE], SLOT[:, t, b:b + 1]) for t in range(2)]
                    rows += [(GATE[:, t, 0:NE], GATE[:, t, b:b + 1]) for t in range(2)]
                    for src, dst in rows:
                        chain(V_.tensor_tensor(OV[:, 3, :], OV[:, 2, :], src, ALU.mult))
                        chain(V_.tensor_reduce(dst, OV[:, 3, :], AX, ALU.add))
                    chain(V_.tensor_scalar(SLOT[:, :, b:b + 1], SLOT[:, :, b:b + 1], -float(P), None, ALU.add))
                chain(V_.memset(SLOT[:, :, MAXB:MAXB + 1], -1.0))
                chain(V_.memset(GATE[:, :, MAXB:MAXB + 1], 0.0))
                chain(V_.tensor_scalar(PLAN[:, 1 + MAXB:16], PLAN[:, 1:5], 0.0, None, ALU.mult))
                V_.tensor_copy(PLANI[:, :], PLAN[:, :]).then_inc(plan_ready, 1)

            for l in range(L):
                columns(l)
                norm(l, 0, toks(0))
                inproj(l)
                ssm_in(l)
                split_to(U[("gate", l, 7)] + 2)
                attention(l)
                ssm_out(l)
                glu(l)
                merge(l)
                split_to(U[("out", l, 1, 1)] + 2)
                residual(l, 0)
                norm(l, 1, toks(l))
                if l == 0:
                    ffn()
                    for t in range(TT):
                        for nb in range(2):
                            banks.released(dve, ("fd", DFF // FC - 1, t, nb))
                else:
                    chain(V_.memset(PUT[:, :, :], 0.0))
                    chain(V_.memset(ONES[:, :], 1.0))
                    chain(V_.memset(YA[:, 0:2, :], 0.0))
                    router()
                    dve.wait_ge(ld_tab, 16)
                    picks(PICK, 0, pick_ready)
                    block_in("ga0")
                    split_to(NU + 2, past=3)
                    dve.wait_ge(plan_ready, 1)
                    blocks = dve.value_load(PLANI[0:1, 0:1], min_val=NE, max_val=MAXB)
                    with dve.Fori(0, blocks) as i:
                        split_n[0] = 3
                        block_turn(i)
                    add_block("back_last", blocks - 1)
                    for t in range(2):
                        for nb in range(2):
                            banks.released(dve, ("back_last", t, nb), blocks - 1)
                residual(l, 1)

        @block.gpsimd
        def _(pool):
            pool.dma_start(CT[:, :], consts[:, 0:896]).then_inc(ld_const, 16)
            pool.dma_start(CV[8:16, :], a["c"].rearrange("b (k p) -> (b k) p", p=P)).then_inc(ld_cond, 16)
            pool.dma_start(CV[0:8, :], a["c_ctx"].rearrange("(k p) -> k p", p=P)).then_inc(ld_cond, 16)
            for s in range(2):
                pool.dma_start(BM[s:s + 1, :, :], a["b_mod"].unsqueeze(0)).then_inc(ld_bm, 16)
                pool.dma_start(NG[s:s + 1, :, :, :], a["norm_g"][:, 1::2, :].unsqueeze(0)).then_inc(ld_bm, 16)

            def ssm_loads(l):
                CI, BI = CI_[l], BI_[l]
                for d in range(2):
                    h = slice(64 * d, 64 * d + 64)
                    pool.dma_start(DTR[h, :], a["ssm_log_dt"][l, d].partition_broadcast(64)).then_inc(ld_ssm, 16)
                    for r, name in enumerate(("ssm_a_re", "ssm_a_im")):
                        pool.dma_start(ARI[:, r, h], a[name][l, d]).then_inc(ld_ssm, 16)
                    for r, name in enumerate(("ssm_b_re", "ssm_b_im")):
                        pool.dma_start(BI[h, r, :, :], a[name][l, d].rearrange("g p h -> p g h")).then_inc(ld_ssm, 16)
                    for r, name in enumerate(("ssm_c_re", "ssm_c_im")):
                        pool.dma_start(CI[:, r, :, d, :], a[name][l, d].rearrange("(b g) h p -> (g h) b p", g=8))\
                            .then_inc(ld_ssm, 16)

            ssm_loads(0)
            for l in range(L):
                if l > 0:
                    pool.wait_ge(x_new, x_new_at[(0, 1)])
                if l == 0:
                    pool.dma_start(X[:, 0:2, :], a["ctx"][0].rearrange("(t p) d -> p t d", p=P)).then_inc(ld_x, 16)
                    pool.dma_start(X[:, 2:4, :], a["x"][0].rearrange("(t p) d -> p t d", p=P)).then_inc(ld_x, 16)
                    gates_seen = 0
                    for m in range(12 * L):
                        ll, nb = m // 12, m % 12
                        if nb // 2 in (2, 5):
                            gates_seen += 1
                            pool.wait_ge(mod_row, gates_seen)
                        else:
                            banks.released(pool, ("mod", ll, nb))
                        pool.dma_start(modrow[ll, :, nb * 512:(nb + 1) * 512], MS[:, m % 2, :]).then_inc(mod_stored[m % 2], 16)
                    for x in range(2):
                        pool.wait_ge(mod_stored[x], 16 * 6 * L)
                for s in range(2):
                    for j, c in enumerate((0, 3072)):
                        pool.dma_start(CR[s * 32 + 16 * j:s * 32 + 16 * j + 16, :],
                                       modrow[l, s, c:c + 2048].rearrange("(k p) -> k p", p=P)).then_inc(ld_cols, 16)
                pool.dma_start(CR[64:96, :], a["norm_g"][l].rearrange("n (k p) -> (n k) p", p=P)).then_inc(ld_cols, 16)
                pool.dma_start(CR[96:100, :], a["b_glu"][l].rearrange("(k p) -> k p", p=P)).then_inc(ld_cols, 16)
                pool.dma_start(SK[:, :], a["attn_sink"][l].partition_broadcast(P)).then_inc(ld_sink, 16)
                for x in range(2):
                    pool.wait_ge(u_stored[x], 32 * (l + 1))
                pool.wait_ge(prep_done, l + 1)
                for s in range(2):
                    pool.dma_start(UU[s * 64:(s + 1) * 64, :, :],
                                   uscr[l, :, s * 256:(s + 1) * 256].rearrange("(c t) h -> c t h", t=T)).then_inc(ld_u, 16)
                pool.wait_ge(ld_u, 32 * (l + 1))
                for s in range(2):
                    h = slice(64 * s, 64 * s + 64)
                    nc.gpsimd.tensor_copy(UP[h, :, :, :].rearrange("p g t h -> p t g h"),
                                          UU[h, :, :].rearrange("p t (g h) -> p t g h", g=H)).then_inc(u_grouped, 1)
                banks.released(pool, ("kT", l))
                pool.dma_start(DR[:, :, :].rearrange("p g h -> p (g h)"), a["ssm_d"][l].partition_broadcast(H))\
                    .then_inc(ld_skip, 16)
                if l > 0:
                    pool.wait_ge(x_stored, 16)
                for q in range(8):
                    banks.released(pool, ("v", l, q))
                base = pool_n[0]
                nc.gpsimd.memset(S[:, :, :, 0:1], 0.0).then_inc(pool_step, 1)
                n = base + 1
                for c in range(1, C - 1):
                    state, nxt = S[:, :, :, c], S[:, :, :, c + 1]
                    m0, m1 = RT[:, 0, :, :], RT[:, 1, :, :]
                    pool.wait_ge(pool_step, n)
                    nc.gpsimd.tensor_tensor(m0, A8[:, 0, :, :], state, ALU.mult).then_inc(pool_step, 1)
                    nc.gpsimd.tensor_tensor(m1, A8[:, 1, :, :], state[:, ::-1, :], ALU.mult).then_inc(pool_step, 1)
                    pool.wait_ge(pool_step, n + 2)
                    nc.gpsimd.tensor_tensor(m0, m0, m1, ALU.add).then_inc(pool_step, 1)
                    pool.wait_ge(pool_step, n + 3)
                    nc.gpsimd.tensor_tensor(nxt, nxt, m0, ALU.add).then_inc(pool_step, 1)
                    n += 4
                pool.wait_ge(pool_step, n)
                banks.wait(pool, ("gate", l, 7, 1))
                for half in range(l, 2):
                    low = S[64:P, :, :, 32 * half:32 * half + 16]
                    high = S[64:P, :, :, 32 * half + 16:32 * half + 32]
                    for dst, src in ((REV[64:P], low), (low, high[:, :, :, ::-1]), (high, REV[64:P][:, :, :, ::-1])):
                        nc.gpsimd.tensor_copy(dst, src).then_inc(pool_step, 1)
                        n += 1
                        pool.wait_ge(pool_step, n)
                pool_n[0] = n
                pool.nop().then_inc(rec_done, 1)
                for x in range(2):
                    pool.wait_ge(g_stored[x], 128 * (l + 1))
                c0 = 0 if l == 0 else CTX
                for ft in range(8):
                    if ft >= 2:
                        pool.wait_ge(m_f, 8 * l + ft - 1)
                    elif ft == 0:
                        banks.released(pool, ("o", l, 3))
                    pool.dma_start(SGA[:, ft % 2, c0:N], gscr[l, ft, :, c0:N]).then_inc(ld_g[ft % 2], 16)
                    pool.dma_start(SGB[:, ft % 2, c0:N], gscr[l, 8 + ft, :, c0:N]).then_inc(ld_g[ft % 2], 16)
                for n_ in range(2):
                    if n_ == 0:
                        pool.wait_ge(m_ready, 8 * (l + 1))
                    else:
                        pool.wait_ge(x_new, x_new_at[(l, 0)])
                        if l == 0:
                            pool.wait_ge(ht_ready, ht_ready_at[(0, 1)])
                            ssm_loads(1)
                    for s in range(2):
                        pool.dma_start(GB[:, s, :], modrow[l, s, (3 * n_ + 2) * D:(3 * n_ + 3) * D].partition_broadcast(P))\
                            .then_inc(ld_gb, 16)
                    if (l, n_) == (0, 0):
                        pool.dma_start(X[:, 0:2, :], a["ctx"][0].rearrange("(t p) d -> p t d", p=P)).then_inc(ld_x, 16)
                        pool.dma_start(X[:, 2:4, :], a["x"][0].rearrange("(t p) d -> p t d", p=P)).then_inc(ld_x, 16)
                    elif (l, n_) == (1, 0):
                        pool.dma_start(X[:, 2:4, :], xscr[CTX:N, :].rearrange("(t p) d -> p t d", p=P)).then_inc(ld_x, 16)
                    elif (l, n_) == (1, 1):
                        pool.dma_start(TAB[:, :, :], consts[:, 896:1152].rearrange("p (a b) -> p a b", a=2)).then_inc(ld_tab, 16)

        @block.sync
        def _(sp):
            loaded = [0]

            def load_to(n):
                while loaded[0] <= min(n, NU - 1):
                    u = loaded[0]
                    if u >= 3:
                        sp.wait_ge(w_split, u - 2)
                    _, src, nk, ncol = units[u]
                    sp.dma_start(raw[:, u % 3, :].rearrange("p (a n) -> p a n", a=nk), src).then_inc(w_landed[u % 3], 16)
                    loaded[0] += 1

            for l in range(L):
                load_to(U[("glu", l)] + 2)
                for q in range(8):
                    x = q % 3
                    for side in range(2):
                        banks.released(sp, ("kb", l, q, side))
                    if q >= 3:
                        banks.wait(sp, ("y", l, q - 3))
                    for t in range(T):
                        sp.dma_start(MI[t * H:(t + 1) * H, x, :, :],
                                     KB[:, x, :, 7 - t:15 - t, :].rearrange("p g t h -> p g (t h)")).then_inc(mi_loaded[x], 16)
            sp.dma_start(WR[:, :, :], a["w_router"][0].rearrange("(k p) e -> p k e", p=P)).then_inc(ld_wr, 16)
            sp.dma_start(BR[:, :], a["b_router"][0].partition_broadcast(P)).then_inc(ld_wr, 16)
            load_to(NU - 1)
            sp.wait_ge(plan_ready, 1)
            blocks = sp.value_load(PLANI[0:1, 0:1], min_val=NE, max_val=MAXB)

            def load_unit(n, expert, i):
                kind, c, h = eorder[n]
                slot = (NU + n) % 3
                sp.wait_ge(w_split, NU + n - 2 + i * EUNITS)
                w = a[{"g": "w_exp_gate", "u": "w_exp_up", "d": "w_exp_down"}[kind]][0][bass.ds(expert, 1)]
                w = w.rearrange("e k n -> (e k) n")
                if kind == "d":
                    src = w[c * EC + h * 256:c * EC + (h + 1) * 256, :]
                else:
                    src = w[h * 512:(h + 1) * 512, c * EC:(c + 1) * EC]
                nk = 2 if kind == "d" else 4
                sp.dma_start(raw[:, slot, :].rearrange("p (a n) -> p a n", a=nk),
                             src.rearrange("(a p) n -> p a n", p=P)).then_inc(w_landed[slot], 16)

            with sp.Fori(0, blocks) as i:
                expert = sp.value_load(PLANI[0:1, bass.ds(i + 1, 1)], min_val=0, max_val=NE - 1)
                for n in range(EUNITS):
                    load_unit(n, expert, i)
            expert = sp.value_load(PLANI[0:1, 1:2], min_val=0, max_val=NE - 1)
            for n in range(3):
                load_unit(n, expert, blocks)


def constants():
    f = np.float32
    q, k = np.arange(P)[:, None], np.arange(CTX)[None, :]
    masks = [np.where(np.abs(q + P * t - k) <= 128, f(0), f(NEG)) for t in range(2)]
    rows, width = 256 // 64, 64
    row = np.repeat(np.arange(rows, dtype=f), width)
    col = np.tile(np.arange(width, dtype=f), rows)
    inv = (f(10000.0) ** (-np.arange(16, dtype=f) / f(16))).astype(f)
    ang = np.concatenate([row[:, None] * inv, col[:, None] * inv], axis=-1)
    cos, sin = (z.astype(f).reshape(2, P, 32).transpose(1, 0, 2).reshape(P, 64) for z in (np.cos(ang), np.sin(ang)))
    before = (np.arange(P)[:, None] < np.arange(P)[None, :]).astype(f)
    slots = np.broadcast_to(np.arange(P, dtype=f), (P, P))
    iota = np.broadcast_to(np.arange(NE, dtype=f) - NE, (P, NE))
    out = np.concatenate([np.eye(P, dtype=f), *masks, cos, sin, iota, np.zeros((P, 120), f), before, slots], axis=1)
    return np.ascontiguousarray(out.astype(f))


_INS = ['x', 'c', 'ctx', 'c_ctx', 'w_mod', 'b_mod', 'norm_g', 'w_in', 'attn_sink', 'ssm_a_re', 'ssm_a_im',
        'ssm_log_dt', 'ssm_b_re', 'ssm_b_im', 'ssm_c_re', 'ssm_c_im', 'ssm_d', 'w_glu', 'b_glu',
        'w_branch_attn', 'w_branch_ssm', 'w_out', 'w_ffn_gate', 'w_ffn_up', 'w_ffn_down',
        'w_router', 'b_router', 'w_exp_gate', 'w_exp_up', 'w_exp_down']


def kernel(**inputs):
    import concourse.bacc as bacc
    from concourse.bass_utils import run_bass_kernel_spmd

    nc = bacc.Bacc("TRN2", target_bir_lowering=False, num_devices=1)
    arrays, a = {}, {}
    for name in _INS:
        v = np.ascontiguousarray(inputs[name])
        arrays[f"in_{name}"] = v
        a[name] = nc.dram_tensor(f"in_{name}", v.shape, mybir.dt.from_np(v.dtype), kind="ExternalInput").ap()
    table = constants()
    arrays["in_consts"] = table
    consts = nc.dram_tensor("in_consts", table.shape, F, kind="ExternalInput").ap()
    out = nc.dram_tensor("out_x", (1, 256, D), F, kind="ExternalOutput").ap()
    build_program(nc, a, consts, out)
    r = run_bass_kernel_spmd(nc, [arrays], core_ids=[0])
    return r.results[0]["out_x"]
```
